# Optimizing a Trainium2 kernel written in Bass

```python
import math
import jax
import jax.numpy as jnp
from jax import lax
import numpy as np

D_MODEL = 1024
BATCH = 1
SEQ = 512
DEPTH = 2

GRID_W = 64
CTX_LEN = 256
N_MIXERS = 2
N_SSD_LAYERS = (DEPTH + 1) // 2
N_POOL_LAYERS = DEPTH // 2
EPS = 1e-6

SSD_D_INNER = 2 * D_MODEL
SSD_HEAD_DIM = 64
SSD_HEADS = SSD_D_INNER // SSD_HEAD_DIM
SSD_GROUPS = 8
SSD_HPG = SSD_HEADS // SSD_GROUPS
SSD_STATE = 128
SSD_CONV = 5
SSD_CHUNK = 128
SSD_BC_DIM = SSD_GROUPS * SSD_STATE
SSD_CONV_DIM = SSD_D_INNER + 2 * SSD_BC_DIM
SSD_IN_DIM = SSD_D_INNER + SSD_CONV_DIM + 2 * SSD_HEADS

POOL_WINDOWS = (2, 4, 8, 16)
POOL_GROUPS = len(POOL_WINDOWS)
POOL_GROUP_DIM = D_MODEL // POOL_GROUPS

PEER_HEADS = 8
PEER_NKEYS = 128
PEER_EXPERTS = PEER_NKEYS * PEER_NKEYS
PEER_DKEY = 256
PEER_HALF = PEER_DKEY // 2
PEER_TOPK = 16
PEER_BLOCK = 128

kernel_name = 'hybrid_ssd_pool_peer_dit'

def rmsnorm(x, w):
    xf = x.astype(jnp.float32)
    y = xf * lax.rsqrt(jnp.mean(xf * xf, axis=-1, keepdims=True) + EPS)
    return (y * w.astype(jnp.float32)).astype(x.dtype)

def modulate(x, w, shift, scale):
    return rmsnorm(x, w) * (1 + scale) + shift

def rev(t):
    return jnp.flip(t, axis=1)

def dwconv(x, w, b):
    y = lax.conv_general_dilated(x, w[:, None, :].astype(x.dtype), window_strides=(1,),
                                 padding=[(SSD_CONV // 2, SSD_CONV // 2)],
                                 dimension_numbers=('NWC', 'WIO', 'NWC'),
                                 feature_group_count=x.shape[-1])
    return y + b.astype(x.dtype)

def segsum(a):
    t = a.shape[-1]
    a_rep = jnp.broadcast_to(a[..., None], a.shape + (t,))
    a_rep = jnp.where(jnp.tril(jnp.ones((t, t), bool), -1), a_rep, 0.0)
    s = jnp.cumsum(a_rep, axis=-2)
    return jnp.where(jnp.tril(jnp.ones((t, t), bool)), s, -jnp.inf)

def ssd_prep(x, dt, a_coef, bm):
    b, l = x.shape[:2]
    nc = l // SSD_CHUNK
    xd = (x * dt[..., None]).reshape(b, nc, SSD_CHUNK, SSD_GROUPS, SSD_HPG, SSD_HEAD_DIM)
    a = (dt * a_coef).reshape(b, nc, SSD_CHUNK, SSD_GROUPS, SSD_HPG).transpose(0, 3, 4, 1, 2)
    bmc = bm.reshape(b, nc, SSD_CHUNK, SSD_GROUPS, SSD_STATE)
    return xd, a, jnp.cumsum(a, axis=-1), bmc

def ssd_states(xd, a_cs, bmc, init):
    decay = jnp.exp(a_cs[..., -1:] - a_cs)
    st = jnp.einsum('bcqgn,bgrcq,bcqgrp->bcgrpn', bmc, decay, xd)
    st = jnp.concatenate([init[:, None], st], axis=1)
    a_chunk = jnp.pad(a_cs[..., -1], ((0, 0), (0, 0), (0, 0), (1, 0)))
    decay_chunk = jnp.exp(segsum(a_chunk))
    st = jnp.einsum('bgrzc,bcgrpn->bzgrpn', decay_chunk, st)
    return st[:, :-1], st[:, -1]

def ssd_scan(x, dt, a_coef, bm, cm, init):
    xd, a, a_cs, bmc = ssd_prep(x, dt, a_coef, bm)
    cmc = cm.reshape(bmc.shape)
    st_in, st_fin = ssd_states(xd, a_cs, bmc, init)
    lmat = jnp.exp(segsum(a))
    cb = jnp.einsum('bclgn,bcsgn->bcgls', cmc, bmc)
    y_diag = jnp.einsum('bcgls,bgrcls,bcsgrp->bclgrp', cb, lmat, xd)
    y_off = jnp.einsum('bclgn,bcgrpn,bgrcl->bclgrp', cmc, st_in, jnp.exp(a_cs))
    return (y_diag + y_off).reshape(x.shape), st_fin

def ssd_final_state(x, dt, a_coef, bm, init):
    xd, _, a_cs, bmc = ssd_prep(x, dt, a_coef, bm)
    return ssd_states(xd, a_cs, bmc, init)[1]

def ssd_inputs(h, in_w, conv_w, conv_b, dt_bias):
    b, l, _ = h.shape
    proj = h @ in_w
    z = proj[..., :SSD_D_INNER]
    xbc = jax.nn.silu(dwconv(proj[..., SSD_D_INNER:SSD_D_INNER + SSD_CONV_DIM], conv_w, conv_b)).astype(jnp.float32)
    xs = xbc[..., :SSD_D_INNER].reshape(b, l, SSD_GROUPS, SSD_HPG, SSD_HEAD_DIM)
    bm = xbc[..., SSD_D_INNER:SSD_D_INNER + SSD_BC_DIM].reshape(b, l, SSD_GROUPS, SSD_STATE)
    cm = xbc[..., SSD_D_INNER + SSD_BC_DIM:].reshape(b, l, SSD_GROUPS, SSD_STATE)
    dt_raw = proj[..., SSD_D_INNER + SSD_CONV_DIM:].astype(jnp.float32).reshape(b, l, 2, SSD_GROUPS, SSD_HPG)
    dt = jax.nn.softplus(dt_raw + dt_bias.astype(jnp.float32).reshape(2, SSD_GROUPS, SSD_HPG))
    return z, xs, bm, cm, dt

def ssd_bidir(xs, bm, cm, dt, a_coef, init_f, init_b):
    y_f, s_f = ssd_scan(xs, dt[:, :, 0], a_coef[0], bm, cm, init_f)
    y_b, s_b = ssd_scan(rev(xs), rev(dt[:, :, 1]), a_coef[1], rev(bm), rev(cm), init_b)
    return y_f + rev(y_b), s_f, s_b

def ssd_output(y, xs, z, d, norm_w, out_w):
    b, l = z.shape[:2]
    y = (y + d.astype(jnp.float32).reshape(SSD_GROUPS, SSD_HPG)[..., None] * xs).reshape(b, l, SSD_D_INNER)
    y = rmsnorm(y * jax.nn.silu(z.astype(jnp.float32)), norm_w)
    return y.astype(z.dtype) @ out_w

def ssd_mixer(h, hc, in_w, conv_w, conv_b, dt_bias, a_log, d, norm_w, out_w, ctx_out):
    a_coef = -jnp.exp(a_log.astype(jnp.float32)).reshape(2, SSD_GROUPS, SSD_HPG)
    zc, xc, bc, cc, dtc = ssd_inputs(hc, in_w, conv_w, conv_b, dt_bias)
    zero = jnp.zeros((hc.shape[0], SSD_GROUPS, SSD_HPG, SSD_HEAD_DIM, SSD_STATE), jnp.float32)
    y_ctx = None
    if ctx_out:
        yc, s_f, s_b = ssd_bidir(xc, bc, cc, dtc, a_coef, zero, zero)
        y_ctx = ssd_output(yc, xc, zc, d, norm_w, out_w)
    else:
        s_f = ssd_final_state(xc, dtc[:, :, 0], a_coef[0], bc, zero)
        s_b = ssd_final_state(rev(xc), rev(dtc[:, :, 1]), a_coef[1], rev(bc), zero)
    z, xs, bm, cm, dt = ssd_inputs(h, in_w, conv_w, conv_b, dt_bias)
    y, _, _ = ssd_bidir(xs, bm, cm, dt, a_coef, s_f, s_b)
    return ssd_output(y, xs, z, d, norm_w, out_w), y_ctx

def window_sum(x, k, axis):
    n = x.shape[axis]
    lo = k // 2
    hi = k - 1 - lo
    pad = [(0, 0)] * x.ndim
    pad[axis] = (1, 0)
    cs = jnp.pad(jnp.cumsum(x, axis=axis), pad)
    t = np.arange(n)
    end = np.minimum(t + hi + 1, n)
    start = np.maximum(t - lo, 0)
    s = jnp.take(cs, end, axis=axis) - jnp.take(cs, start, axis=axis)
    return s, (end - start).astype(np.float32)

def pool_mixer(h, w, scale, on_grid):
    b, l, _ = h.shape
    if on_grid:
        rows = l // GRID_W
        hg = h.astype(jnp.float32).reshape(b, rows, GRID_W, POOL_GROUPS, POOL_GROUP_DIM)
    else:
        hg = h.astype(jnp.float32).reshape(b, l, POOL_GROUPS, POOL_GROUP_DIM)
    axes = tuple(range(1, hg.ndim - 2))
    outs = []
    for g, k in enumerate(POOL_WINDOWS):
        xg = hg[..., g, :]
        s = xg
        cnt = np.ones((1,) * len(axes), np.float32)
        for ax in axes:
            s, cn = window_sum(s, k, ax)
            cnt = cnt * cn.reshape([-1 if a == ax else 1 for a in axes])
        outs.append(s / cnt[..., None] - xg)
    p = jnp.stack(outs, axis=-2).astype(h.dtype)
    y = jnp.einsum('b...gc,gcd->b...gd', p, w).reshape(b, l, D_MODEL)
    return y * scale

def peer(x, q_w, keys, u, v):
    shp = x.shape
    t = x.reshape(-1, D_MODEL)
    nb = t.shape[0] // PEER_BLOCK

    def block(xb):
        q = (xb @ q_w).astype(jnp.float32).reshape(-1, PEER_HEADS, 2, PEER_HALF)
        s = jnp.einsum('thkc,hknc->thkn', q, keys.astype(jnp.float32))
        s1, i1 = lax.top_k(s[:, :, 0], PEER_TOPK)
        s2, i2 = lax.top_k(s[:, :, 1], PEER_TOPK)
        nt = xb.shape[0]
        cand = (s1[..., :, None] + s2[..., None, :]).reshape(nt, PEER_HEADS, PEER_TOPK * PEER_TOPK)
        cidx = (i1[..., :, None] * PEER_NKEYS + i2[..., None, :]).reshape(nt, PEER_HEADS, PEER_TOPK * PEER_TOPK)
        top, pos = lax.top_k(cand, PEER_TOPK)
        idx = jnp.take_along_axis(cidx, pos, axis=-1)
        g = jax.nn.softmax(top, axis=-1).astype(xb.dtype)
        a = jax.nn.gelu(jnp.einsum('td,thkd->thk', xb, u[idx]))
        return jnp.einsum('thk,thkd->td', g * a, v[idx])

    y = lax.map(block, t.reshape(nb, PEER_BLOCK, D_MODEL))
    return y.reshape(shp)

def setup_inputs(seed: int = 0) -> dict:
    key = jax.random.key(seed)
    ks = jax.random.split(key, 22)
    nrm = jax.random.normal
    dt0 = jnp.exp(jax.random.uniform(ks[8], (N_SSD_LAYERS, 2, SSD_HEADS),
                                     minval=math.log(1e-3), maxval=math.log(1e-1)))
    return {
        'x': nrm(ks[0], (BATCH, SEQ, D_MODEL), jnp.float32),
        'c': nrm(ks[1], (BATCH, D_MODEL), jnp.float32),
        'ctx': nrm(ks[2], (BATCH, CTX_LEN, D_MODEL), jnp.float32),
        'c_ctx': nrm(ks[3], (D_MODEL,), jnp.float32),
        'mod_w': nrm(ks[4], (DEPTH, D_MODEL, 6 * D_MODEL), jnp.float32) * (0.5 * D_MODEL ** -0.5),
        'mod_b': 0.02 * nrm(ks[5], (DEPTH, 6 * D_MODEL), jnp.float32),
        'norm_w': 1.0 + 0.05 * nrm(ks[6], (DEPTH, 2, D_MODEL), jnp.float32),
        'ssd_in_w': nrm(ks[7], (N_SSD_LAYERS, D_MODEL, SSD_IN_DIM), jnp.float32) * D_MODEL ** -0.5,
        'ssd_conv_w': nrm(ks[9], (N_SSD_LAYERS, SSD_CONV, SSD_CONV_DIM), jnp.float32) * SSD_CONV ** -0.5,
        'ssd_conv_b': 0.02 * nrm(ks[10], (N_SSD_LAYERS, SSD_CONV_DIM), jnp.float32),
        'ssd_dt_bias': dt0 + jnp.log(-jnp.expm1(-dt0)),
        'ssd_a_log': jnp.log(jax.random.uniform(ks[11], (N_SSD_LAYERS, 2, SSD_HEADS), minval=1.0, maxval=16.0)),
        'ssd_d': 1.0 + 0.05 * nrm(ks[12], (N_SSD_LAYERS, SSD_HEADS), jnp.float32),
        'ssd_norm_w': 1.0 + 0.05 * nrm(ks[13], (N_SSD_LAYERS, SSD_D_INNER), jnp.float32),
        'ssd_out_w': nrm(ks[14], (N_SSD_LAYERS, SSD_D_INNER, D_MODEL), jnp.float32) * SSD_D_INNER ** -0.5,
        'pool_w': nrm(ks[15], (N_POOL_LAYERS, POOL_GROUPS, POOL_GROUP_DIM, POOL_GROUP_DIM), jnp.float32) * POOL_GROUP_DIM ** -0.5,
        'pool_scale': 1.0 + 0.05 * nrm(ks[16], (N_POOL_LAYERS, D_MODEL), jnp.float32),
        'peer_q_w': nrm(ks[17], (DEPTH, D_MODEL, PEER_HEADS * PEER_DKEY), jnp.float32) * D_MODEL ** -0.5,
        'peer_keys': nrm(ks[18], (DEPTH, PEER_HEADS, 2, PEER_NKEYS, PEER_HALF), jnp.float32) * PEER_HALF ** -0.5,
        'peer_u': nrm(ks[19], (DEPTH, PEER_EXPERTS, D_MODEL), jnp.float32) * D_MODEL ** -0.5,
        'peer_v': nrm(ks[20], (DEPTH, PEER_EXPERTS, D_MODEL), jnp.float32) * PEER_HEADS ** -0.5,
        'final_norm_w': 1.0 + 0.05 * nrm(ks[21], (D_MODEL,), jnp.float32),
    }

def reference(x, c, ctx, c_ctx, mod_w, mod_b, norm_w, ssd_in_w, ssd_conv_w, ssd_conv_b, ssd_dt_bias,
              ssd_a_log, ssd_d, ssd_norm_w, ssd_out_w, pool_w, pool_scale, peer_q_w, peer_keys,
              peer_u, peer_v, final_norm_w):
    sc = jax.nn.silu(c)
    scc = jax.nn.silu(c_ctx)
    xc = ctx
    for i in range(DEPTH):
        kind = i % N_MIXERS
        j = i // N_MIXERS
        ctx_later = any(k % N_MIXERS == 0 for k in range(i + 1, DEPTH))
        m = jnp.split((sc @ mod_w[i] + mod_b[i])[:, None, :], 6, axis=-1)
        if kind == 0 or ctx_later:
            mc = jnp.split(scc @ mod_w[i] + mod_b[i], 6, axis=-1)
            hc = modulate(xc, norm_w[i, 0], mc[0], mc[1])
        h = modulate(x, norm_w[i, 0], m[0], m[1])
        if kind == 0:
            y, yc = ssd_mixer(h, hc, ssd_in_w[j], ssd_conv_w[j], ssd_conv_b[j], ssd_dt_bias[j], ssd_a_log[j],
                              ssd_d[j], ssd_norm_w[j], ssd_out_w[j], ctx_later)
        else:
            y = pool_mixer(h, pool_w[j], pool_scale[j], True)
            if ctx_later:
                yc = pool_mixer(hc, pool_w[j], pool_scale[j], False)
        x = x + m[2] * y
        x = x + m[5] * peer(modulate(x, norm_w[i, 1], m[3], m[4]), peer_q_w[i], peer_keys[i], peer_u[i], peer_v[i])
        if ctx_later:
            xc = xc + mc[2] * yc
            xc = xc + mc[5] * peer(modulate(xc, norm_w[i, 1], mc[3], mc[4]), peer_q_w[i], peer_keys[i],
                                   peer_u[i], peer_v[i])
    return rmsnorm(x, final_norm_w)


_drawn_inputs = setup_inputs


def setup_inputs(seed=0):
    import zlib

    import numpy as np

    out = dict(_drawn_inputs(seed))
    spreads = {}
    factors = {'ctx': 3.606,
     'c_ctx': 3.067,
     'ssd_conv_b': 4.781,
     'ssd_d': 6.808,
     'ssd_norm_w': 3.024,
     'pool_scale': 3.794}
    for name, (base, spread) in spreads.items():
        noise = np.random.default_rng([zlib.crc32(name.encode()), seed]).standard_normal(out[name].shape)
        drawn = base * np.exp(spread * noise) if base else spread * noise
        out[name] = jnp.asarray(drawn.astype(out[name].dtype))
    for name, factor in factors.items():
        out[name] = (out[name] * factor).astype(out[name].dtype)
    return out
```

```python
from contextlib import ExitStack, contextmanager

import concourse.bass as bass
from concourse import mybir

F32 = mybir.dt.float32
U32 = mybir.dt.uint32
ALU = mybir.AluOpType
ACT = mybir.ActivationFunctionType
AX = mybir.AxisListType

P = 128
D = 1024
KD = D // P
LAT = 4
CTX = 2
TT = LAT + CTX
SEQ = LAT * P
CTX_LEN = CTX * P
GROUPS = 8
HPG = 4
HEADS = GROUPS * HPG
HD = 64
INNER = HEADS * HD
CI = INNER // P
TAPS = 5
HALO = TAPS // 2
PH = 8
HH = 2 * PH
NKEY = 128
TOPK = 16
SEL = PH * TOPK
NEXP = NKEY * NKEY
RING = 8
BATCHES = SEL // RING
PGROUPS = 4
EPS = 1e-6
LOWEST = -3.0e38
ENGINES = 5
UNITS = [("lat", 0), ("lat", 1), ("lat", 2), ("ctx", 0), ("ctx", 1), ("ctx", 2), ("lat", 3),
         ("z", 0), ("z", 1), ("z", 2), ("z", 3)]
UNIT_BANKS = (0, 1, 2, 0, 1, 2, 0, 1, 2, 2, 0)
CONVS = 7
NU = len(UNITS)
ST_BANKS = (0, 1, 5, 6, 7)
F_TILES, B_TILES = (0, 1, 2, 3, 4), (1, 0, 5, 4, 3)
SERIES = 9


class Counts:

    def __init__(self):
        self.posted, self.taken, self.phases = {}, {}, 0

    @staticmethod
    def add(table, sem, unit):
        entry = table.setdefault(sem.name, [0, 0])
        entry[1] += unit
        return entry[0] + entry[1]

    def post(self, sem, unit=1):
        self.add(self.posted, sem, unit)
        return unit

    def own(self, sem):
        return self.add(self.posted, sem, 0)

    def take(self, sem, unit=1, ahead=0):
        return self.add(self.taken, sem, unit) + ahead

    @contextmanager
    def loop(self, eng, rounds, posts, takes):
        starts = []
        with eng.Fori(0, rounds) as i:
            for table, per in ((self.posted, posts), (self.taken, takes)):
                start = {name: sum(entry) for name, entry in table.items()}
                per = {s.name: k for s, k in per.items()}
                starts.append((table, start, per))
                for name in set(start) | set(per):
                    base, k = start.get(name, 0), per.get(name, 0)
                    table[name] = [i * k + base if k else base, 0]
            yield i
        for table, start, per in starts:
            wrong = {name: entry[1] for name, entry in table.items() if entry[1] != per.get(name, 0)}
            assert not wrong, f"the round adds {wrong}"
            for name in table:
                table[name] = [start.get(name, 0) + rounds * per.get(name, 0), 0]


def hybrid(nc, a, out, layers=2):
    with ExitStack() as ctx:
        def sb(name, shape, dt=F32):
            return ctx.enter_context(nc.sbuf_tensor(name, shape, dt))

        def sem(name):
            return ctx.enter_context(nc.semaphore(name))

        psum = ctx.enter_context(nc.psum_tensor("psum", [P, 8, 512], F32))

        x_res = sb("x_res", [P, LAT, D])
        big = sb("big", [P, 8192])
        h_tok = big[:, 0:TT * D].rearrange("p (t d) -> p t d", t=TT)
        mod_ctx = big[:, TT * D:8192]
        cond_rep = big[:, 0:2 * D].rearrange("p (s k m) -> p s k m", s=2, k=KD)
        y_t = big[:, :].rearrange("p (k t) -> p k t", k=CI)
        h_t = sb("h_t", [P, KD, TT * P])
        mod_row = sb("mod_row", [P, 6 * D])
        scr = sb("scr", [P, 4096])
        x_ctx = scr[:, 0:CTX * D].rearrange("p (t d) -> p t d", t=CTX)
        nw_row = scr[:, 2048:4096]
        wbuf = sb("wbuf", [P, 2, 4096])
        ident = sb("ident", [P, P])
        ones = sb("ones", [P, P])
        zeros = sb("zeros", [P, P])
        mask_le = sb("mask_le", [P, P])
        mask_ge = sb("mask_ge", [P, P])
        mask_lt = sb("mask_lt", [P, P])
        mask_gt = sb("mask_gt", [P, P])
        cond = sb("cond", [P, 2, KD])
        eps = sb("eps", [P, 1])
        ssq = sb("ssq", [P, 8])
        rms = sb("rms", [P, 8])
        rinv = sb("rinv", [P, 8])

        w_full = [sem(f"w_full{i}") for i in range(2)]
        w_free = sem("w_free")
        in_x, in_ctx, in_cond, in_modb, in_nw, in_small, in_keys, in_row, in_fin = map(
            sem, ("in_x", "in_ctx", "in_cond", "in_modb", "in_nw", "in_small", "in_keys", "in_row", "in_fin"))
        phase = sem("phase")
        dve_step, act_step, pool_step, pe_step = map(sem, ("dve_step", "act_step", "pool_step", "pe_step"))
        masks_ready, cond_ready, rep_ready = map(sem, ("masks_ready", "cond_ready", "rep_ready"))
        mod_ps, mod_ev = sem("mod_ps"), sem("mod_ev")
        rms_ready, h_ready, tr_ps, ht_ready = map(sem, ("rms_ready", "h_ready", "tr_ps", "ht_ready"))
        dt_ps, dt_abs, dt_exp, a_ready, seg_ps, seg_exp, dec_ready = map(
            sem, ("dt_ps", "dt_abs", "dt_exp", "a_ready", "seg_ps", "seg_exp", "dec_ready"))
        pj_ps, pj_ev, conv_done, xs_ready = map(sem, ("pj_ps", "pj_ev", "conv_done", "xs_ready"))
        pe_group, dve_group = sem("pe_group"), sem("dve_group")
        tok_ps, tok_ready, xd_ready, st_ps, st_done = map(
            sem, ("tok_ps", "tok_ready", "xd_ready", "st_ps", "st_done"))
        r_ready, t1_ready, dee_ps, e_ready, cb_ps, m_ready, ce_ready, y_ps, y_ev, sq_ready, yz_ready = map(
            sem, ("r_ready", "t1_ready", "dee_ps", "e_ready", "cb_ps", "m_ready", "ce_ready", "y_ps",
                  "y_ev", "sq_ready", "yz_ready"))
        yn_ready, ysq_ps, ysq_rt, op_ps = map(sem, ("yn_ready", "ysq_ps", "ysq_rt", "op_ps"))
        q_ps, qt_ready, s_ps, s_ev, pl_ps, pl_ev, py_ps, x_ready = map(
            sem, ("q_ps", "qt_ready", "s_ps", "s_ev", "pl_ps", "pl_ev", "py_ps", "x_ready"))
        idx_ready, st_go, u_free, a_dots, gelu_ready, ex_in, ex_ready, w_ready, dg_ready, v_done, y_free = map(
            sem, ("idx_ready", "st_go", "u_free", "a_dots", "gelu_ready", "ex_in", "ex_ready", "w_ready",
                  "dg_ready", "v_done", "y_free"))
        u_full = [sem(f"u_full{i}") for i in range(RING)]
        v_full = [sem(f"v_full{i}") for i in range(RING)]
        stored = sem("stored")

        with ExitStack() as scope:
            def tmp(name, shape, dt=F32):
                return scope.enter_context(nc.sbuf_tensor(name, shape, dt))

            pre_l = tmp("pre_l", [P, 4, SEQ + 2 * HALO])
            pre_c = tmp("pre_c", [P, 3, CTX_LEN + 2 * HALO])
            cv_l = tmp("cv_l", [P, 4, SEQ])
            cv_c = tmp("cv_c", [P, 3, CTX_LEN])
            z_t = tmp("z_t", [P, 2, SEQ])
            tok = tmp("tok", [P, TT, 3 * P])
            st_tmp = tmp("st_tmp", [P, 2, 2, HPG * HD])
            r1 = tmp("r1", [P, 2, HPG, P])
            ef = tmp("ef", [P, 2, HPG, P])
            tw = tmp("tw", [P, HPG, P])
            dtv = tmp("dtv", [P, TT, 2 * HEADS])
            av = tmp("av", [P, TT, 2 * HEADS])
            ea = tmp("ea", [P, TT, 2 * HEADS])
            wd = tmp("wd", [P, TT, 2 * HEADS])
            alr = tmp("alr", [P, 2 * HEADS])
            dtb = tmp("dtb", [P, 2 * HEADS])
            cw = tmp("cw", [P, GROUPS * 4 * TAPS])
            cbias = tmp("cbias", [P, GROUPS * 4])
            dcol = tmp("dcol", [P, CI])
            nwcol = tmp("nwcol", [P, CI])
            sqacc = tmp("sqacc", [P, SEQ])
        s_in = mod_row[:, 0:2 * D].rearrange("p (w c n) -> p w c n", w=2, c=LAT)
        m_ce = scr[:, 0:3072].rearrange("p (b s h l) -> p b s h l", b=2, s=3, h=HPG)
        e_mat = scr[:, 3072:3584].rearrange("p (h l) -> p h l", h=HPG)
        t1 = scr[:, 3584:4096].rearrange("p (h l) -> p h l", h=HPG)
        xd = scr[:, 0:2560].rearrange("p (s w n) -> p s w n", s=5, w=2)
        n384 = TT * 2 * HEADS
        dt_x, dt_u, dt_z, dt_q, dt_r = (
            big[:, i * n384:(i + 1) * n384].rearrange("p (t h) -> p t h", t=TT) for i in range(5))

        with ExitStack() as scope:
            def tmp2(name, shape, dt=F32):
                return scope.enter_context(nc.sbuf_tensor(name, shape, dt))

            scores = tmp2("scores", [P, LAT - 1, HH * NKEY])
            u_more = tmp2("u_more", [P, 3, D])
            top_v = tmp2("top_v", [P, HH, TOPK])
            top_i = tmp2("top_i", [P, HH, TOPK], U32)
            top_f = tmp2("top_f", [P, HH, TOPK])
            best = tmp2("best", [P, PH, TOPK])
            pos = tmp2("pos", [P, PH, TOPK], U32)
            part = tmp2("part", [P, 2, SEL], U32)
            part_f = tmp2("part_f", [P, 2, SEL])
            ids_f = tmp2("ids_f", [P, 2, SEL])
            ids = tmp2("ids", [P, LAT * SEL], U32)
            stage = tmp2("stage", [P, 4, RING], U32)
            soft = tmp2("soft", [P, PH, TOPK])
            soft_e = tmp2("soft_e", [P, PH, TOPK])
            soft_s = tmp2("soft_s", [P, 2, PH])
            gate = tmp2("gate", [P, SEL])
            dots = tmp2("dots", [P, SEL])
            gelu = tmp2("gelu", [P, SEL])
            wts = tmp2("wts", [P, LAT * SEL])
            diag = tmp2("diag", [P, RING, P])
            iota_i = tmp2("iota_i", [P, TOPK])
        work = scr[:, 0:2048]
        pick = scr[:, 2048:4096].rearrange("p (s j) -> p s j", s=SEL)
        u_buf = [mod_row[:, j * D:(j + 1) * D] for j in range(5)] + [u_more[:, j, :] for j in range(3)]
        h_flat = h_t[:, :, :].rearrange("p k t -> p (k t)")
        v_buf = [h_flat[:, j * D:(j + 1) * D] for j in range(6)] + [
            big[:, 6 * D:7 * D], big[:, 7 * D:8 * D]]
        keys = big[:, 4 * D:6 * D]
        q_t = big[:, 6 * D:7 * D].rearrange("p (b t) -> p b t", b=2)
        q_0 = big[:, 7 * D:8 * D].rearrange("p (b t) -> p b t", b=2)
        y_tmp = big[:, 4 * D:5 * D]

        block = ctx.enter_context(nc.Block())

        def bc(ap, n):
            return ap.unsqueeze(2).to_broadcast([P, ap.shape[1], n])

        def rep(ap, n):
            return ap.unsqueeze(1).to_broadcast([P, n, ap.shape[1]])

        def rows(ap):
            return ap.unsqueeze(0).to_broadcast([P, ap.shape[0]])

        def meet(eng, n, own):
            for s in own:
                eng.wait_ge(s, n.own(s))
            eng.sem_inc(phase, 1)
            n.phases += 1
            eng.wait_ge(phase, ENGINES * n.phases)

        @block.sync
        def _(sp):
            n = Counts()

            def weights(b, src, cols):
                sp.wait_ge(w_free, n.take(w_free))
                sp.dma_start(wbuf[:, b, 0:cols], src).then_inc(w_full[b], n.post(w_full[b], 16))

            def layer_rows(layer):
                for r in range(6):
                    sp.dma_start(mod_row[:, r * D:(r + 1) * D],
                                 rows(a["mod_b"][layer, r * D:(r + 1) * D])).then_inc(in_modb, 16)
                for r in range(2):
                    sp.dma_start(nw_row[:, r * D:(r + 1) * D], rows(a["norm_w"][layer, r])).then_inc(in_nw, 16)

            def mod_weights(layer, first, pairs):
                with n.loop(sp, pairs, {w_full[0]: 16, w_full[1]: 16}, {w_free: 2}) as i:
                    for e in range(2):
                        weights(e, a["mod_w"][layer, i * 2 + (first + e)], 4096)

            for s, name in enumerate(("c", "c_ctx")):
                sp.dma_start(cond[:, s, :], a[name]).then_inc(in_cond, 16)
            for e in range(2):
                weights(e, a["mod_w"][0, e], 4096)
            layer_rows(0)
            for r in range(2):
                sp.dma_start(mod_ctx[:, r * D:(r + 1) * D],
                             rows(a["mod_b"][0, r * D:(r + 1) * D])).then_inc(in_modb, 16)
            sp.dma_start(x_ctx, a["ctx"].rearrange("(t p) d -> p t d", p=P)).then_inc(in_ctx, 16)
            sp.dma_start(x_res[:, :, :], a["x"].rearrange("(t p) d -> p t d", p=P)).then_inc(in_x, 16)
            mod_weights(0, 2, 5)
            for dst, src in ((cw[:, :], a["conv_w"]), (cbias[:, :], a["conv_b"]), (nwcol[:, :], a["ssd_norm_w"]),
                             (alr[:, :], rows(a["a_log"])), (dtb[:, :], rows(a["dt_bias"])),
                             (dcol[0:HD, :], a["ssd_d"][0].unsqueeze(0).to_broadcast([HD, CI])),
                             (dcol[HD:P, :], a["ssd_d"][1].unsqueeze(0).to_broadcast([HD, CI]))):
                sp.dma_start(dst, src).then_inc(in_small, 16)
            weights(0, a["dt_w"], KD * 2 * HEADS)
            weights(1, a["dt_w"], KD * 2 * HEADS)
            with n.loop(sp, GROUPS, {w_full[0]: 16, w_full[1]: 16}, {w_free: 2}) as g:
                weights(0, a["xbc_w"][g], 4096)
                weights(1, a["z_w"][g], 2048)
            for m in range(4):
                weights(m % 2, a["out_w"][m], 4096)
            meet(sp, n, [])

            def peer_loads(layer):
                sp.dma_start(keys, a["keys"][layer]).then_inc(in_keys, 16)
                for m in range(4):
                    weights(m % 2, a["q_w"][layer, m], 4096)
                with n.loop(sp, 2, {w_full[0]: 16, w_full[1]: 16}, {w_free: 2}) as i:
                    for e in range(2):
                        weights(e, a["q_w"][layer, i * 2 + e], 4096)
                meet(sp, n, [])

            peer_loads(0)
            if layers == 2:
                layer_rows(1)
                sp.dma_start(y_tmp, rows(a["pool_scale"])).then_inc(in_row, 16)
                mod_weights(1, 0, 6)
                for m in range(2):
                    weights(m, a["pool_m"][m], 4096)
                weights(0, a["pool_w"], 2048)
                weights(1, a["pool_w"], 2048)
                meet(sp, n, [])
                peer_loads(1)
            sp.dma_start(nw_row[:, 0:D], rows(a["final_norm_w"])).then_inc(in_fin, 16)
            for t in range(LAT):
                sp.wait_ge(x_ready, n.take(x_ready))
                sp.dma_start(out[t * P:(t + 1) * P, :], h_tok[:, t, :]).then_inc(stored, n.post(stored, 16))
            sp.wait_ge(stored, n.own(stored))

        @block.gpsimd
        def _(pool):
            n = Counts()
            g_ = nc.gpsimd

            def link(ins):
                ins.then_inc(pool_step, n.post(pool_step))
                pool.wait_ge(pool_step, n.own(pool_step))

            link(g_.memset(ones[:, :], 1.0))
            link(g_.memset(eps[:, :], EPS))
            link(g_.memset(zeros[:, :], 0.0))
            for dst, op, step in ((ident, ALU.is_equal, 1), (mask_le, ALU.is_ge, 1), (mask_ge, ALU.is_ge, -1),
                                  (mask_lt, ALU.is_gt, 1), (mask_gt, ALU.is_gt, -1)):
                ins = g_.affine_select(out=dst[:, :], in_=ones[:, :], compare_op=op, fill=0.0, base=0,
                                       pattern=[[step, P]], channel_multiplier=-step)
                link(ins)
            link(g_.memset(pre_l[:, :, :], 0.0))
            g_.memset(pre_c[:, :, :], 0.0).then_inc(masks_ready, n.post(masks_ready))
            pool.wait_ge(masks_ready, 1)

            pool.wait_ge(dec_ready, n.take(dec_ready))
            with n.loop(pool, GROUPS, {xd_ready: 10, r_ready: 2 * LAT, t1_ready: LAT},
                        {tok_ready: TT, pe_group: 1, dve_group: 1, dee_ps: 3 * LAT, m_ready: LAT}) as g:
                pool.wait_ge(pe_group, n.take(pe_group))
                pool.wait_ge(dve_group, n.take(dve_group))

                def spread(c):
                    if c > 0:
                        pool.wait_ge(dee_ps, n.take(dee_ps, 3))
                    for w, mask in ((0, mask_le), (1, mask_ge)):
                        g_.tensor_tensor(out=r1[:, w, :, :],
                                         in0=bc(av[:, CTX + c, bass.ds(g * HPG + w * HEADS, HPG)], P),
                                         in1=rep(mask[:, :], HPG), op=ALU.mult).then_inc(r_ready, n.post(r_ready))
                    if c > 0:
                        pool.wait_ge(m_ready, n.take(m_ready))
                    g_.tensor_tensor(out=t1, in0=bc(dtv[:, CTX + c, bass.ds(g * HPG, HPG)], P),
                                     in1=rep(mask_le[:, :], HPG), op=ALU.mult).then_inc(t1_ready, n.post(t1_ready))

                spread(0)
                for s in range(5):
                    for w, tile in ((0, F_TILES[s]), (1, B_TILES[s])):
                        if s == 0 and w == 0:
                            pool.wait_ge(tok_ready, n.take(tok_ready, TT))
                        g_.tensor_tensor(
                            out=xd[:, s, w, :].rearrange("p (h d) -> p h d", h=HPG),
                            in0=tok[:, tile, 0:2 * P].rearrange("p (h d) -> p h d", h=HPG),
                            in1=bc(wd[:, tile, bass.ds(g * HPG + w * HEADS, HPG)], HD),
                            op=ALU.mult).then_inc(xd_ready, n.post(xd_ready))
                for c in range(1, LAT):
                    spread(c)
                pool.wait_ge(dee_ps, n.take(dee_ps, 3))
                pool.wait_ge(m_ready, n.take(m_ready))
            meet(pool, n, [xd_ready, r_ready, t1_ready])

            def gather(table, col, buf, full, free, ahead):
                pool.wait_ge(free, n.take(free, 1, ahead))
                pool.sem_inc(st_go, 1)
                pool.indirect_dma_start(buf, None, table, bass.IndirectOffsetOnAxis(col, 0)).then_inc(
                    full, n.post(full, 16))

            def gathers(layer, first, tiles, do_u, do_v, lag):
                posts = {pool_step: 4 if do_u and do_v else 2}
                takes = {}
                if do_u:
                    posts.update({s: 32 for s in u_full})
                    takes[u_free] = 2 * RING
                if do_v:
                    posts.update({s: 32 for s in v_full})
                    takes[v_done] = 2 * RING
                with n.loop(pool, tiles * BATCHES // 2, posts, takes) as i:
                    for e in range(2):
                        if do_u:
                            link(g_.tensor_copy(stage[:, e, :], ids[:, bass.ds(i * (2 * RING) + (first * SEL + e * RING), RING)]))
                        if do_v:
                            link(g_.tensor_copy(stage[:, 2 + e, :], ids[:, bass.ds(i * (2 * RING) + ((first - lag) * SEL + e * RING), RING)]))
                        for j in range(RING):
                            if do_u:
                                gather(a["u"], stage[:, e, j:j + 1], u_buf[j], u_full[j], u_free, 0)
                            if do_v:
                                gather(a["v"], stage[:, 2 + e, j:j + 1], v_buf[j], v_full[j], v_done, 0)

            def peer(layer):
                for tile in range(LAT + 1):
                    if tile < LAT:
                        pool.wait_ge(idx_ready, n.take(idx_ready))
                    gathers(layer, tile, 1, tile < LAT, tile > 0, 1)
                meet(pool, n, [])

            peer(0)
            if layers == 2:
                meet(pool, n, [])
                peer(1)

        @block.scalar
        def _(act):
            n = Counts()
            s_ = nc.scalar

            def link(ins):
                ins.then_inc(act_step, n.post(act_step))
                act.wait_ge(act_step, n.own(act_step))

            act.sem_inc(pj_ev, n.post(pj_ev, 3))
            act.wait_ge(in_cond, 32)
            s_.activation(cond[:, :, :], cond[:, :, :], ACT.Silu).then_inc(cond_ready, n.post(cond_ready))
            act.wait_ge(masks_ready, 1)

            def norms(tiles):
                for c, (src, dump) in enumerate(tiles):
                    link(s_.activation(dump, src, ACT.Square, accum_out=ssq[:, c:c + 1]))
                s_.activation(rms[:, 0:len(tiles)], ssq[:, 0:len(tiles)], ACT.Sqrt, bias=eps[:, 0:1],
                              scale=1.0 / D).then_inc(rms_ready, n.post(rms_ready))

            def transposed(tiles, shift):
                for t in range(tiles):
                    for b in range(2):
                        act.wait_ge(tr_ps, n.take(tr_ps))
                        s_.copy(h_t[:, b * 4:(b + 1) * 4, (t + shift) * P:(t + shift + 1) * P],
                                psum[:, b, :].rearrange("p (k t) -> p k t", k=4)).then_inc(ht_ready, n.post(ht_ready))

            act.wait_ge(in_ctx, 16)
            act.wait_ge(in_x, 16)
            norms([(x_ctx[:, t, :], h_tok[:, CTX, :]) for t in range(CTX)] +
                  [(x_res[:, t, :], h_tok[:, CTX, :]) for t in range(LAT)])
            transposed(TT, 0)
            act.wait_ge(in_small, 7 * 16)
            link(s_.activation(alr[:, :], alr[:, :], ACT.Exp))
            act.wait_ge(dt_abs, n.take(dt_abs))
            s_.activation(dt_u, dt_u, ACT.Exp, scale=-1.0).then_inc(dt_exp, n.post(dt_exp))
            act.wait_ge(seg_ps, n.take(seg_ps))
            link(s_.activation(ea[:, :, :], psum[:, 1, 0:n384].rearrange("p (t h) -> p t h", t=TT), ACT.Exp))
            for w in range(2):
                ins = s_.activation(wd[:, :, w * HEADS:(w + 1) * HEADS],
                                    psum[:, 2 + w, 0:n384 // 2].rearrange("p (t h) -> p t h", t=TT), ACT.Exp)
                if w == 0:
                    link(ins)
            ins.then_inc(seg_exp, n.post(seg_exp))

            with n.loop(act, GROUPS, {pj_ev: NU, xs_ready: CONVS, tok_ready: TT,
                                      e_ready: 3 * LAT, sq_ready: 1, act_step: 1, yn_ready: 1},
                        {pj_ps: NU, conv_done: CONVS, tok_ps: TT, dee_ps: 3 * LAT, m_ready: LAT, ce_ready: LAT,
                         yz_ready: 1, dve_group: 1}) as g:
                def evacuate(unit):
                    kind, col = UNITS[unit]
                    act.wait_ge(pj_ps, n.take(pj_ps))
                    bank = UNIT_BANKS[unit]
                    if kind == "ctx":
                        src, dst = psum[:, bank, 0:CTX_LEN], pre_c[:, col, HALO:HALO + CTX_LEN]
                    elif kind == "lat":
                        src, dst = psum[:, bank, :], pre_l[:, col, HALO:HALO + SEQ]
                    else:
                        src = psum[:, bank, 0:2 * P]
                        dst = z_t[:, col // 2, col % 2 * 2 * P:(col % 2 + 1) * 2 * P]
                    s_.activation(dst, src, ACT.Silu if kind == "z" else ACT.Copy).then_inc(pj_ev, n.post(pj_ev))

                def silu(unit):
                    kind, col = UNITS[unit]
                    act.wait_ge(conv_done, n.take(conv_done))
                    buf = cv_c[:, col, :] if kind == "ctx" else cv_l[:, col, :]
                    s_.activation(buf, buf, ACT.Silu).then_inc(xs_ready, n.post(xs_ready))

                evacuate(0)
                evacuate(1)
                for k in range(2, CONVS):
                    evacuate(k)
                    silu(k - 2)
                silu(CONVS - 2)
                for t in range(TT):
                    act.wait_ge(tok_ps, n.take(tok_ps))
                    s_.copy(tok[:, t, :], psum[:, 6 + t % 2, 0:3 * P]).then_inc(tok_ready, n.post(tok_ready))
                silu(CONVS - 1)
                act.wait_ge(dve_group, n.take(dve_group))
                evacuate(7)
                evacuate(8)
                for c in range(LAT):
                    for w in range(3):
                        if c == 0 and w == 2:
                            evacuate(9)
                        act.wait_ge(dee_ps, n.take(dee_ps))
                        if c > 0 and w == 0:
                            act.wait_ge(m_ready, n.take(m_ready))
                            act.wait_ge(ce_ready, n.take(ce_ready))
                        dst = e_mat if w == 0 else ef[:, w - 1, :, :]
                        s_.activation(dst, psum[:, 3 + w, :].rearrange("p (h l) -> p h l", h=HPG),
                                      ACT.Exp).then_inc(e_ready, n.post(e_ready))
                evacuate(10)
                act.wait_ge(m_ready, n.take(m_ready))
                act.wait_ge(ce_ready, n.take(ce_ready))
                act.wait_ge(yz_ready, n.take(yz_ready))
                s_.activation(z_t[:, :, :], y_t[:, bass.ds(g * 2, 2), :], ACT.Square).then_inc(sq_ready, n.post(sq_ready))
                act.wait_ge(sq_ready, n.own(sq_ready))
                for j in range(2):
                    ins = s_.activation(y_t[:, bass.ds(g * 2 + j, 1), :], y_t[:, bass.ds(g * 2 + j, 1), :], ACT.Copy,
                                        scale=nwcol[:, bass.ds(g * 2 + j, 1)])
                    if j == 0:
                        ins.then_inc(act_step, n.post(act_step))
                ins.then_inc(yn_ready, n.post(yn_ready))
            act.wait_ge(ysq_ps, n.take(ysq_ps))
            s_.activation(rms[:, 0:LAT], psum[:, 0, 0:LAT], ACT.Sqrt, bias=eps[:, 0:1],
                          scale=1.0 / INNER).then_inc(ysq_rt, n.post(ysq_rt))
            meet(act, n, [ysq_rt])

            def peer(layer):
                norms([(x_res[:, t, :], h_tok[:, t, :]) for t in range(LAT)])
                transposed(LAT, 0)

                def q_copy(s):
                    act.wait_ge(q_ps, n.take(q_ps))
                    s_.copy(q_t[:, s % 2, 0:3 * P], psum[:, 2 + s % 2, 0:3 * P]).then_inc(qt_ready, n.post(qt_ready))

                def s_copy(i, s):
                    act.wait_ge(s_ps, n.take(s_ps))
                    s_.copy(scores[:, :, bass.ds(i * (8 * NKEY) + s * NKEY, NKEY)],
                            psum[:, 4 + s % 2, 0:3 * P].rearrange("p (t k) -> p t k", t=3)).then_inc(
                        s_ev, n.post(s_ev))

                for m in range(4):
                    act.wait_ge(q_ps, n.take(q_ps))
                    s_.copy(q_0[:, m % 2, :], psum[:, 2 + m % 2, :]).then_inc(qt_ready, n.post(qt_ready))
                    act.wait_ge(s_ps, n.take(s_ps))
                    s_.copy(work[:, m * 512:(m + 1) * 512], psum[:, 4 + m % 2, :]).then_inc(s_ev, n.post(s_ev))

                with n.loop(act, 2, {qt_ready: 8, s_ev: 8}, {q_ps: 8, s_ps: 8}) as i:
                    q_copy(0)
                    for s in range(1, 8):
                        if s >= 2:
                            s_copy(i, s - 2)
                        q_copy(s)
                    s_copy(i, 6)
                    s_copy(i, 7)

                def exps():
                    act.wait_ge(ex_in, n.take(ex_in))
                    s_.activation(soft_e[:, :, :], soft[:, :, :], ACT.Exp).then_inc(ex_ready, n.post(ex_ready))

                def gelus():
                    act.wait_ge(a_dots, n.take(a_dots))
                    s_.activation(gelu[:, :], dots[:, :], ACT.Gelu_apprx_tanh).then_inc(gelu_ready, n.post(gelu_ready))

                def diags(tile):
                    act.wait_ge(w_ready, n.take(w_ready))
                    with n.loop(act, BATCHES, {dg_ready: RING}, {v_done: RING}) as b:
                        for j in range(RING):
                            act.wait_ge(v_done, n.take(v_done))
                            s_.activation(diag[:, j, :], ident[:, :], ACT.Copy,
                                          scale=wts[:, bass.ds(b * RING + (tile * SEL + j), 1)]).then_inc(
                                dg_ready, n.post(dg_ready))

                exps()
                for tile in range(LAT):
                    if tile > 0:
                        diags(tile - 1)
                    gelus()
                    if tile < LAT - 1:
                        exps()
                diags(LAT - 1)
                meet(act, n, [dg_ready])

            peer(0)
            if layers == 2:
                norms([(x_res[:, t, :], h_tok[:, CTX, :]) for t in range(LAT)])
                for k in range(KD):
                    act.wait_ge(pl_ps, n.take(pl_ps))
                    s_.copy(h_t[:, k, 0:SEQ], psum[:, k % 4, :]).then_inc(pl_ev, n.post(pl_ev))
                meet(act, n, [pl_ev])
                peer(1)
            norms([(x_res[:, t, :], h_tok[:, t, :]) for t in range(LAT)])

        @block.tensor
        def _(pe):
            n = Counts()
            mm = nc.tensor.matmul

            pe.sem_inc(w_free, n.post(w_free, 2))
            pe.sem_inc(v_done, n.post(v_done, RING))
            pe.sem_inc(pe_group, n.post(pe_group))
            pe.wait_ge(masks_ready, 1)
            pe.wait_ge(rep_ready, 1)

            def product(dst, lhs, rhs, k):
                for j in range(k):
                    ins = mm(dst, lhs(j), rhs(j), start=(j == 0), stop=(j == k - 1))
                return ins

            def mod_blocks(pairs, both):
                per = 4 if both else 2
                with n.loop(pe, pairs, {mod_ps: per, w_free: 2}, {mod_ev: per, w_full[0]: 16, w_full[1]: 16}) as i:
                    for e in range(2):
                        w = wbuf[:, e, :].rearrange("p (k m) -> p k m", k=KD)
                        pe.wait_ge(w_full[e], n.take(w_full[e], 16))
                        for s in range(2 if both else 1):
                            pe.wait_ge(mod_ev, n.take(mod_ev))
                            bank = 2 * e + s
                            ins = product(psum[:, bank, :], lambda k: cond_rep[:, s, k, :], lambda k: w[:, k, :], KD)
                            ins.then_inc(mod_ps, n.post(mod_ps))
                        pe.wait_ge(mod_ps, n.own(mod_ps))
                        pe.sem_inc(w_free, n.post(w_free))

            def transposes(tiles, shift=0):
                for t in range(tiles):
                    pe.wait_ge(h_ready, n.take(h_ready))
                    for b in range(2):
                        if t > 0:
                            pe.wait_ge(ht_ready, n.take(ht_ready))
                        for k in range(4):
                            ins = nc.tensor.transpose(psum[:, b, k * P:(k + 1) * P],
                                                      h_tok[:, t, (b * 4 + k) * P:(b * 4 + k + 1) * P], ident[:, :])
                        ins.then_inc(tr_ps, n.post(tr_ps))
                pe.wait_ge(ht_ready, n.take(ht_ready, 2))

            mod_blocks(2, True)
            mod_blocks(4, False)
            transposes(TT)

            wdt = wbuf[:, 0, 0:KD * 2 * HEADS].rearrange("p (k m) -> p k m", k=KD)
            pe.wait_ge(w_full[0], n.take(w_full[0], 16))
            for t in range(TT):
                ins = product(psum[:, 2, t * 2 * HEADS:(t + 1) * 2 * HEADS],
                              lambda k: h_t[:, k, t * P:(t + 1) * P], lambda k: wdt[:, k, :], KD)
            ins.then_inc(dt_ps, n.post(dt_ps))
            pe.wait_ge(w_full[1], n.take(w_full[1], 16))
            pe.wait_ge(dt_ps, n.own(dt_ps))
            pe.sem_inc(w_free, n.post(w_free, 2))
            pe.wait_ge(a_ready, n.take(a_ready))
            mm(psum[:, 1, 0:n384], ones[:, :], av[:, :, :], start=True, stop=True)
            mm(psum[:, 2, 0:n384 // 2], mask_gt[:, :], av[:, :, 0:HEADS], start=True, stop=True)
            mm(psum[:, 3, 0:n384 // 2], mask_lt[:, :], av[:, :, HEADS:2 * HEADS], start=True,
               stop=True).then_inc(seg_ps, n.post(seg_ps))
            pe.wait_ge(seg_exp, n.take(seg_exp))

            with n.loop(pe, GROUPS,
                        {pj_ps: NU, w_free: 2, tok_ps: TT, st_ps: 1, dee_ps: 3 * LAT, cb_ps: LAT, y_ps: LAT,
                         pe_group: 1},
                        {w_full[0]: 16, w_full[1]: 16, pj_ev: NU, xs_ready: CONVS, tok_ready: TT, xd_ready: 10,
                         st_done: 1, r_ready: 2 * LAT, e_ready: 3 * LAT, m_ready: LAT, ce_ready: LAT,
                         y_ev: LAT}) as g:
                wx = wbuf[:, 0, :].rearrange("p (k m) -> p k m", k=KD)
                wz = wbuf[:, 1, 0:2048].rearrange("p (k m) -> p k m", k=KD)

                def project(unit):
                    kind, col = UNITS[unit]
                    lo, hi = (0, CTX_LEN) if kind == "ctx" else (CTX_LEN, TT * P)
                    if kind == "z":
                        lo, hi, col = CTX_LEN + col % 2 * 2 * P, CTX_LEN + (col % 2 + 1) * 2 * P, col // 2
                    if unit == 0:
                        pe.wait_ge(w_full[0], n.take(w_full[0], 16))
                    if unit == 7:
                        pe.wait_ge(pj_ps, n.own(pj_ps))
                        pe.sem_inc(w_free, n.post(w_free))
                        pe.wait_ge(w_full[1], n.take(w_full[1], 16))
                    pe.wait_ge(pj_ev, n.take(pj_ev, 1, 0 if unit else 2))
                    w = wz if kind == "z" else wx
                    ins = product(psum[:, UNIT_BANKS[unit], 0:hi - lo], lambda j: w[:, j, col * P:(col + 1) * P],
                                  lambda j: h_t[:, j, lo:hi], KD)
                    ins.then_inc(pj_ps, n.post(pj_ps))

                for unit in range(CONVS):
                    project(unit)
                for t in range(TT):
                    if t == 0:
                        pe.wait_ge(xs_ready, n.take(xs_ready, CONVS - 1))
                    if t >= 2:
                        pe.wait_ge(tok_ready, n.take(tok_ready))
                    for j in range(3):
                        src = cv_c[:, j, t * P:(t + 1) * P] if t < CTX else cv_l[:, j, (t - CTX) * P:(t - CTX + 1) * P]
                        ins = nc.tensor.transpose(psum[:, 6 + t % 2, j * P:(j + 1) * P], src, ident[:, :])
                    ins.then_inc(tok_ps, n.post(tok_ps))
                project(7)
                project(8)
                pe.wait_ge(tok_ready, n.take(tok_ready, 2))
                pe.wait_ge(pj_ev, n.take(pj_ev, 0, 3))
                for s in range(5):
                    for w, tile in ((0, F_TILES[s]), (1, B_TILES[s])):
                        pe.wait_ge(xd_ready, n.take(xd_ready))
                        ins = mm(psum[:, ST_BANKS[s], w * 256:(w + 1) * 256], tok[:, tile, 2 * P:3 * P], xd[:, s, w, :],
                                 start=True, stop=True)
                ins.then_inc(st_ps, n.post(st_ps))

                def decays(c):
                    pe.wait_ge(r_ready, n.take(r_ready, 2))
                    if c == 1:
                        pe.wait_ge(pj_ev, n.take(pj_ev, 0, 3))
                    if c > 0:
                        pe.wait_ge(e_ready, n.take(e_ready, 3))
                    mm(psum[:, 3, :], mask_gt[:, :], r1[:, 0, :, :], start=True, stop=False)
                    mm(psum[:, 3, :], mask_lt[:, :], r1[:, 1, :, :], start=False, stop=True).then_inc(
                        dee_ps, n.post(dee_ps))
                    for w in range(2):
                        if c == 0 and w == 1:
                            project(9)
                            pe.wait_ge(st_done, n.take(st_done))
                        mm(psum[:, 4 + w, :], ones[:, :], r1[:, w, :, :], start=True, stop=True).then_inc(
                            dee_ps, n.post(dee_ps))
                    if c == 0:
                        pe.wait_ge(xs_ready, n.take(xs_ready))
                    mm(psum[:, (7, 2)[c % 2], 0:P], cv_l[:, 2, c * P:(c + 1) * P], cv_l[:, 3, c * P:(c + 1) * P],
                       start=True, stop=True).then_inc(cb_ps, n.post(cb_ps))

                def outputs(c):
                    pe.wait_ge(m_ready, n.take(m_ready))
                    pe.wait_ge(ce_ready, n.take(ce_ready))
                    bank = (6, 1)[c % 2]
                    if c >= 2:
                        pe.wait_ge(y_ev, n.take(y_ev))
                    for r in range(HPG):
                        half, pair = r % 2, r // 2
                        dst = psum[half * HD:(half + 1) * HD, bank, pair * P:(pair + 1) * P]
                        cols = slice(r * HD, (r + 1) * HD)
                        mm(dst, tok[:, CTX + c, cols], m_ce[:, c % 2, 0, r, :], start=True, stop=False)
                        mm(dst, s_in[:, 0, c, cols], m_ce[:, c % 2, 1, r, :], start=False, stop=False)
                        ins = mm(dst, s_in[:, 1, c, cols], m_ce[:, c % 2, 2, r, :], start=False, stop=True)
                    ins.then_inc(y_ps, n.post(y_ps))

                decays(0)
                for c in range(1, LAT):
                    decays(c)
                    outputs(c - 1)
                project(10)
                pe.wait_ge(pj_ps, n.own(pj_ps))
                pe.sem_inc(w_free, n.post(w_free))
                outputs(LAT - 1)
                pe.wait_ge(e_ready, n.take(e_ready, 3))
                pe.wait_ge(y_ev, n.take(y_ev, 2))
                pe.wait_ge(y_ps, n.own(y_ps))
                pe.sem_inc(pe_group, n.post(pe_group))

            pe.wait_ge(dve_group, GROUPS + 1)
            pe.wait_ge(yn_ready, GROUPS)
            for t in range(LAT):
                ins = mm(psum[:, 0, t:t + 1], sqacc[:, t * P:(t + 1) * P], ones[:, 0:1], start=True, stop=True)
            ins.then_inc(ysq_ps, n.post(ysq_ps))
            pe.wait_ge(ysq_rt, 1)
            for m in range(4):
                w = wbuf[:, m % 2, :].rearrange("p (k d) -> p k d", k=4)
                pe.wait_ge(w_full[m % 2], n.take(w_full[m % 2], 16))
                for k in range(4):
                    for t in range(LAT):
                        for h in range(2):
                            ins = mm(psum[:, 2 * t + h, :], y_t[:, 4 * m + k, t * P:(t + 1) * P],
                                     w[:, k, h * 512:(h + 1) * 512], start=(m + k == 0), stop=(m == 3 and k == 3))
                if m < 3:
                    ins.then_inc(w_free, n.post(w_free))
                else:
                    ins.then_inc(op_ps, n.post(op_ps))
                    pe.wait_ge(op_ps, n.own(op_ps))
                    pe.sem_inc(w_free, n.post(w_free))
            meet(pe, n, [op_ps])

            def peer(layer):
                transposes(LAT)
                pe.wait_ge(in_keys, n.take(in_keys, 16))

                def queries(e, s):
                    w = wbuf[:, e, :].rearrange("p (k m) -> p k m", k=KD)
                    ins = product(psum[:, 2 + s % 2, 0:3 * P], lambda k: w[:, k, (s % 4) * P:(s % 4 + 1) * P],
                                  lambda k: h_t[:, k, P:SEQ], KD)
                    ins.then_inc(q_ps, n.post(q_ps))
                    if s % 4 == 3:
                        pe.wait_ge(q_ps, n.own(q_ps))
                        pe.sem_inc(w_free, n.post(w_free))

                def key_scores(i, s):
                    pe.wait_ge(qt_ready, n.take(qt_ready))
                    if s >= 2:
                        pe.wait_ge(s_ev, n.take(s_ev))
                    for t in range(LAT - 1):
                        ins = mm(psum[:, 4 + s % 2, t * P:(t + 1) * P], q_t[:, s % 2, t * P:(t + 1) * P],
                                 keys[:, bass.ds(i * (8 * NKEY) + s * NKEY, NKEY)], start=True, stop=True)
                    ins.then_inc(s_ps, n.post(s_ps))

                def first_queries(m):
                    w = wbuf[:, m % 2, :].rearrange("p (k m) -> p k m", k=KD)
                    pe.wait_ge(w_full[m % 2], n.take(w_full[m % 2], 16))
                    for s in range(4):
                        ins = product(psum[:, 2 + m % 2, s * P:(s + 1) * P], lambda k: w[:, k, s * P:(s + 1) * P],
                                      lambda k: h_t[:, k, 0:P], KD)
                    ins.then_inc(q_ps, n.post(q_ps))
                    pe.wait_ge(q_ps, n.own(q_ps))
                    pe.sem_inc(w_free, n.post(w_free))

                def first_scores(m):
                    pe.wait_ge(qt_ready, n.take(qt_ready))
                    if m >= 2:
                        pe.wait_ge(s_ev, n.take(s_ev))
                    for s in range(4):
                        ins = mm(psum[:, 4 + m % 2, s * P:(s + 1) * P], q_0[:, m % 2, s * P:(s + 1) * P],
                                 keys[:, (4 * m + s) * NKEY:(4 * m + s + 1) * NKEY], start=True, stop=True)
                    ins.then_inc(s_ps, n.post(s_ps))

                first_queries(0)
                for m in range(1, 4):
                    first_queries(m)
                    first_scores(m - 1)
                first_scores(3)
                pe.wait_ge(s_ev, n.take(s_ev, 2))
                with n.loop(pe, 2, {q_ps: 8, w_free: 2, s_ps: 8},
                            {w_full[0]: 16, w_full[1]: 16, qt_ready: 8, s_ev: 8}) as i:
                    for s in range(8):
                        if s % 4 == 0:
                            pe.wait_ge(w_full[s // 4], n.take(w_full[s // 4], 16))
                        queries(s // 4, s)
                        if s >= 1:
                            key_scores(i, s - 1)
                    key_scores(i, 7)
                    pe.wait_ge(s_ev, n.take(s_ev, 2))
                for tile in range(LAT):
                    pe.wait_ge(y_free, n.take(y_free))
                    for h in range(2):
                        mm(psum[:, h, :], zeros[:, :], h_tok[:, 0, 0:512], start=True, stop=True, skip_group_check=True)
                    with n.loop(pe, BATCHES, {v_done: RING},
                                {dg_ready: RING, **{s: 16 for s in v_full}}) as b:
                        for j in range(RING):
                            pe.wait_ge(v_full[j], n.take(v_full[j], 16))
                            pe.wait_ge(dg_ready, n.take(dg_ready))
                            for h in range(2):
                                ins = mm(psum[:, h, :], diag[:, j, :], v_buf[j][:, h * 512:(h + 1) * 512],
                                         start=False, stop=True, skip_group_check=True)
                            ins.then_inc(v_done, n.post(v_done))
                meet(pe, n, [v_done])

            peer(0)
            if layers == 2:
                pe.wait_ge(rep_ready, 2)
                mod_blocks(6, False)
                pe.wait_ge(h_ready, n.take(h_ready, LAT))
                for k in range(KD):
                    gidx, m = k // 2, k // 4
                    if k % 4 == 0:
                        pe.wait_ge(w_full[m], n.take(w_full[m], 16))
                    if k >= 4:
                        pe.wait_ge(pl_ev, n.take(pl_ev))
                    w = wbuf[:, m, :].rearrange("p (g t n) -> p g t n", g=2, t=LAT)
                    ins = product(psum[:, k % 4, :], lambda t: h_tok[:, t, k * P:(k + 1) * P],
                                  lambda t: w[:, gidx % 2, t, :], LAT)
                    ins.then_inc(pl_ps, n.post(pl_ps))
                    if k % 4 == 3:
                        pe.wait_ge(pl_ps, n.own(pl_ps))
                        pe.sem_inc(w_free, n.post(w_free))
                pe.wait_ge(pl_ev, n.take(pl_ev, 4))
                w = wbuf[:, 0, 0:2048].rearrange("p (g c n) -> p g c n", g=PGROUPS, c=2)
                pe.wait_ge(w_full[0], n.take(w_full[0], 16))
                for t in range(LAT):
                    for gi in range(PGROUPS):
                        for c in range(2):
                            ins = mm(psum[:, 2 * t + gi // 2, (gi % 2) * 256:(gi % 2 + 1) * 256],
                                     h_t[:, 2 * gi + c, t * P:(t + 1) * P], w[:, gi, c, :],
                                     start=(c == 0), stop=(c == 1))
                ins.then_inc(py_ps, n.post(py_ps))
                pe.wait_ge(py_ps, n.own(py_ps))
                pe.wait_ge(w_full[1], n.take(w_full[1], 16))
                pe.sem_inc(w_free, n.post(w_free, 2))
                meet(pe, n, [py_ps])
                peer(1)

        @block.vector
        def _(dve):
            n = Counts()
            v_ = nc.vector

            def step(ins):
                ins.then_inc(dve_step, n.post(dve_step))

            def link(ins):
                step(ins)
                dve.wait_ge(dve_step, n.own(dve_step))

            def tt(o, i0, i1, op):
                return v_.tensor_tensor(out=o, in0=i0, in1=i1, op=op)

            def stt(o, i0, s, i1, op0, op1):
                return v_.scalar_tensor_tensor(out=o, in0=i0, scalar=s, in1=i1, op0=op0, op1=op1)

            dve.sem_inc(mod_ev, n.post(mod_ev, 2))
            dve.sem_inc(dve_group, n.post(dve_group))
            dve.sem_inc(u_free, n.post(u_free, RING))
            dve.sem_inc(y_free, n.post(y_free))

            def replicate(s_count, last=True):
                for s in range(s_count):
                    ins = v_.tensor_copy(cond_rep[:, s, :, :], bc(cond[:, s, :], P))
                    if s < s_count - 1:
                        link(ins)
                ins.then_inc(rep_ready, n.post(rep_ready))
                dve.wait_ge(rep_ready, n.own(rep_ready))

            def mod_rows(pairs, first, both):
                per = 4 if both else 2
                with n.loop(dve, pairs, {mod_ev: per}, {mod_ps: per}) as i:
                    for e in range(2):
                        for s in range(2 if both else 1):
                            dve.wait_ge(mod_ps, n.take(mod_ps))
                            row = (mod_ctx if s else mod_row)[:, bass.ds(i * 1024 + (first + e) * 512, 512)]
                            tt(row, row, psum[:, 2 * e + s, :], ALU.add).then_inc(mod_ev, n.post(mod_ev))
                dve.wait_ge(mod_ev, n.own(mod_ev))

            def row(r):
                return mod_row[:, r * D:(r + 1) * D]

            def scale_rows():
                for r, k in ((1, 0), (4, 1)):
                    link(stt(row(r), row(r), 1.0, nw_row[:, k * D:(k + 1) * D], ALU.add, ALU.mult))

            def modulated(tiles):
                dve.wait_ge(rms_ready, n.take(rms_ready))
                link(v_.reciprocal(rinv[:, 0:len(tiles)], rms[:, 0:len(tiles)]))
                for c, (src, arow, brow, dst) in enumerate(tiles):
                    link(stt(dst, src, rinv[:, c:c + 1], arow, ALU.mult, ALU.mult))
                    tt(dst, dst, brow, ALU.add).then_inc(h_ready, n.post(h_ready))

            dve.wait_ge(cond_ready, n.take(cond_ready))
            dve.wait_ge(masks_ready, 1)
            replicate(2)
            dve.wait_ge(in_modb, 8 * 16)
            mod_rows(2, 0, True)
            mod_rows(4, 4, False)
            dve.wait_ge(in_nw, 2 * 16)
            link(stt(mod_ctx[:, D:2 * D], mod_ctx[:, D:2 * D], 1.0, nw_row[:, 0:D], ALU.add, ALU.mult))
            scale_rows()
            modulated([(x_ctx[:, t, :], mod_ctx[:, D:2 * D], mod_ctx[:, 0:D], h_tok[:, t, :]) for t in range(CTX)] +
                      [(x_res[:, t, :], row(1), row(0), h_tok[:, CTX + t, :]) for t in range(LAT)])

            dve.wait_ge(in_small, 7 * 16)
            dve.wait_ge(dt_ps, n.take(dt_ps))
            dve.wait_ge(h_ready, n.own(h_ready))
            link(tt(dt_x, psum[:, 2, 0:n384].rearrange("p (t h) -> p t h", t=TT), rep(dtb[:, :], TT), ALU.add))
            stt(dt_u, dt_x, -1.0, dt_x, ALU.mult, ALU.max).then_inc(dt_abs, n.post(dt_abs))
            dve.wait_ge(dt_exp, n.take(dt_exp))
            link(v_.tensor_scalar(dt_z, dt_u, 2.0, None, ALU.add))
            link(v_.reciprocal(dt_q, dt_z))
            link(tt(dt_z, dt_u, dt_q, ALU.mult))
            link(tt(dt_u, dt_z, dt_z, ALU.mult))
            link(v_.tensor_scalar(dt_q, dt_u, 1.0 / (2 * SERIES + 1), None, ALU.mult))
            for k in range(SERIES - 1, 0, -1):
                link(stt(dt_q, dt_q, 1.0 / (2 * k + 1), dt_u, ALU.add, ALU.mult))
            link(stt(dt_q, dt_q, 1.0, dt_z, ALU.add, ALU.mult))
            link(v_.tensor_scalar(dt_x, dt_x, 0.0, None, ALU.max))
            link(stt(dtv[:, :, :], dt_q, 2.0, dt_x, ALU.mult, ALU.add))
            stt(av[:, :, :], dtv[:, :, :], -1.0, rep(alr[:, :], TT), ALU.mult, ALU.mult).then_inc(
                a_ready, n.post(a_ready))
            dve.wait_ge(seg_exp, n.take(seg_exp))
            link(v_.memset(sqacc[:, :], 0.0))
            tt(wd[:, :, :], wd[:, :, :], dtv[:, :, :], ALU.mult).then_inc(dec_ready, n.post(dec_ready))
            dve.wait_ge(dec_ready, n.own(dec_ready))

            steps = CONVS * (TAPS - 1) + 17 + LAT * 7 + 1
            with n.loop(dve, GROUPS, {dve_step: steps, conv_done: CONVS, st_done: 1, m_ready: LAT, ce_ready: LAT,
                                      y_ev: LAT, yz_ready: 1, dve_group: 1},
                        {pj_ev: NU, pe_group: 1, st_ps: 1, t1_ready: LAT, e_ready: 3 * LAT, cb_ps: LAT,
                         y_ps: LAT, xs_ready: CONVS, sq_ready: 1}) as g:

                dve.wait_ge(pe_group, n.take(pe_group))
                for k in range(CONVS):
                    dve.wait_ge(pj_ev, n.take(pj_ev, 1, 3))
                    kind, j = UNITS[k]
                    width = CTX_LEN if kind == "ctx" else SEQ
                    src, dst = (pre_c, cv_c[:, j, :]) if kind == "ctx" else (pre_l, cv_l[:, j, :])

                    def weight(tap):
                        return cw[:, bass.ds(g * (4 * TAPS) + (j * TAPS + tap), 1)]

                    link(v_.tensor_scalar(dst, src[:, j, 0:width], weight(0), cbias[:, bass.ds(g * 4 + j, 1)],
                                           ALU.mult, ALU.add))
                    for tap in range(1, TAPS):
                        ins = stt(dst, src[:, j, tap:tap + width], weight(tap), dst, ALU.mult, ALU.add)
                        if tap < TAPS - 1:
                            link(ins)
                        else:
                            ins.then_inc(conv_done, n.post(conv_done))
                dve.wait_ge(st_ps, n.take(st_ps))
                where = {}
                for s in range(5):
                    for w, tile in ((0, F_TILES[s]), (1, B_TILES[s])):
                        new = psum[:, ST_BANKS[s], w * 256:(w + 1) * 256]
                        if s == 0:
                            dst = st_tmp[:, w, 0, :]
                            link(v_.tensor_copy(dst, new))
                        else:
                            dst = s_in[:, w, s - 1 if w == 0 else LAT - s, :]
                            old, mid = where[w], st_tmp[:, w, 1, :]
                            link(tt(mid.rearrange("p (h d) -> p h d", h=HPG),
                                     old.rearrange("p (h d) -> p h d", h=HPG),
                                     bc(ea[:, tile, bass.ds(g * HPG + w * HEADS, HPG)], HD), ALU.mult))
                            ins = tt(dst, mid, new, ALU.add)
                            if s == 4 and w == 1:
                                ins.then_inc(st_done, n.post(st_done))
                            else:
                                link(ins)
                        where[w] = dst
                dve.wait_ge(st_done, n.own(st_done))
                dve.wait_ge(xs_ready, n.take(xs_ready, CONVS))

                def prepare(c):
                    b = c % 2
                    dve.wait_ge(t1_ready, n.take(t1_ready))
                    for r in range(HPG):
                        ins = stt(tw[:, r, :], mask_ge[:, :], dtv[:, CTX + c, bass.ds(g * HPG + (HEADS + r), 1)],
                                  t1[:, r, :], ALU.mult, ALU.add)
                        link(ins)
                    dve.wait_ge(e_ready, n.take(e_ready, 3))
                    link(tt(m_ce[:, b, 0, :, :], tw[:, :, :], e_mat, ALU.mult))
                    dve.wait_ge(cb_ps, n.take(cb_ps))
                    tt(m_ce[:, b, 0, :, :], m_ce[:, b, 0, :, :], rep(psum[:, (7, 2)[b], 0:P], HPG),
                       ALU.mult).then_inc(m_ready, n.post(m_ready))
                    link(tt(m_ce[:, b, 1, :, :], ef[:, 0, :, :], rep(cv_l[:, 3, c * P:(c + 1) * P], HPG), ALU.mult))
                    tt(m_ce[:, b, 2, :, :], ef[:, 1, :, :], rep(cv_l[:, 3, c * P:(c + 1) * P], HPG),
                       ALU.mult).then_inc(ce_ready, n.post(ce_ready))

                def finish(c):
                    dve.wait_ge(y_ps, n.take(y_ps))
                    for pair in range(2):
                        ins = stt(y_t[:, bass.ds(g * 2 + pair, 1), c * P:(c + 1) * P].rearrange("p o t -> p (o t)"),
                                  cv_l[:, pair, c * P:(c + 1) * P],
                                  dcol[:, bass.ds(g * 2 + pair, 1)], psum[:, (6, 1)[c % 2], pair * P:(pair + 1) * P],
                                  ALU.mult, ALU.add)
                        if pair == 0:
                            link(ins)
                        else:
                            ins.then_inc(y_ev, n.post(y_ev))

                prepare(0)
                for c in range(1, LAT):
                    prepare(c)
                    finish(c - 1)
                finish(LAT - 1)
                dve.wait_ge(y_ev, n.own(y_ev))
                dve.wait_ge(pj_ev, n.take(pj_ev, NU - CONVS, 3))
                both = y_t[:, bass.ds(g * 2, 2), :]
                tt(both, both, z_t[:, :, :], ALU.mult).then_inc(yz_ready, n.post(yz_ready))
                dve.wait_ge(sq_ready, n.take(sq_ready))
                link(tt(sqacc[:, :], sqacc[:, :], z_t[:, 0, :], ALU.add))
                tt(sqacc[:, :], sqacc[:, :], z_t[:, 1, :], ALU.add).then_inc(dve_group, n.post(dve_group))
                dve.wait_ge(dve_group, n.own(dve_group))

            dve.wait_ge(ysq_rt, 1)
            link(v_.reciprocal(rinv[:, 0:LAT], rms[:, 0:LAT]))
            dve.wait_ge(op_ps, n.take(op_ps))
            for t in range(LAT):
                for h in range(2):
                    o = slice(h * 512, (h + 1) * 512)
                    link(stt(scr[:, o], psum[:, 2 * t + h, :], rinv[:, t:t + 1],
                             mod_row[:, 2 * D + h * 512:2 * D + (h + 1) * 512], ALU.mult, ALU.mult))
                    link(tt(x_res[:, t, o], x_res[:, t, o], scr[:, o], ALU.add))
            meet(dve, n, [dve_step])

            def peer(layer):
                modulated([(x_res[:, t, :], row(4), row(3), h_tok[:, t, :]) for t in range(LAT)])
                dve.wait_ge(h_ready, n.own(h_ready))

                def load_scores(tile, lo, hi):
                    if tile == 1:
                        dve.wait_ge(s_ev, n.take(s_ev, hi - lo))
                    o = slice(lo * NKEY, hi * NKEY)
                    link(v_.tensor_copy(work[:, o], scores[:, tile - 1, o]))

                def top16(val, idx, src):
                    link(v_.max(val[:, 0:8], src))
                    link(v_.max_index(idx[:, 0:8], val[:, 0:8], src))
                    link(v_.match_replace(src, val[:, 0:8], src, LOWEST))
                    link(v_.max(val[:, 8:16], src))
                    link(v_.max_index(idx[:, 8:16], val[:, 8:16], src))

                def key_rows(lo, hi):
                    for r in range(lo, hi):
                        top16(top_v[:, r, :], top_i[:, r, :], work[:, r * NKEY:(r + 1) * NKEY])

                def candidates():
                    link(v_.tensor_copy(top_f[:, :, :], top_i[:, :, :]))
                    for h in range(PH):
                        step(tt(work[:, h * 256:(h + 1) * 256].rearrange("p (i j) -> p i j", i=TOPK),
                                bc(top_v[:, 2 * h, :], TOPK), rep(top_v[:, 2 * h + 1, :], TOPK), ALU.add))
                    dve.wait_ge(dve_step, n.own(dve_step))

                def best_rows(lo, hi):
                    for h in range(lo, hi):
                        top16(best[:, h, :], pos[:, h, :], work[:, h * 256:(h + 1) * 256])

                def indices(tile, which):
                    flat = pos[:, :, :].rearrange("p h k -> p (h k)")
                    if which == 0:
                        link(v_.tensor_scalar(part[:, 0, :], flat, 4, None, ALU.logical_shift_right))
                        link(v_.tensor_scalar(part[:, 1, :], flat, 15, None, ALU.bitwise_and))
                        link(v_.tensor_copy(part_f[:, :, :], part[:, :, :]))
                    link(tt(pick, bc(part_f[:, which, :], TOPK), rep(iota_i[:, :], SEL), ALU.is_equal))
                    for h in range(PH):
                        sl = pick[:, h * TOPK:(h + 1) * TOPK, :]
                        step(tt(sl, sl, rep(top_f[:, 2 * h + which, :], TOPK), ALU.mult))
                    dve.wait_ge(dve_step, n.own(dve_step))
                    link(v_.tensor_reduce(ids_f[:, which, :], pick, AX.X, ALU.add))
                    if which == 1:
                        link(stt(ids_f[:, 0, :], ids_f[:, 0, :], float(NKEY), ids_f[:, 1, :], ALU.mult, ALU.add))
                        v_.tensor_scalar(ids[:, tile * SEL:(tile + 1) * SEL], ids_f[:, 0, :], float(layer * NEXP), None,
                                         ALU.add).then_inc(idx_ready, n.post(idx_ready))
                        dve.wait_ge(idx_ready, n.own(idx_ready))

                def soft_in():
                    tt(soft[:, :, :], best[:, :, :], best[:, :, 0:1].to_broadcast([P, PH, TOPK]),
                       ALU.subtract).then_inc(ex_in, n.post(ex_in))

                def soft_out():
                    dve.wait_ge(ex_ready, n.take(ex_ready))
                    link(v_.tensor_reduce(soft_s[:, 0, :], soft_e[:, :, :], AX.X, ALU.add))
                    link(v_.reciprocal(soft_s[:, 1, :], soft_s[:, 0, :]))
                    link(tt(gate[:, :].rearrange("p (h k) -> p h k", h=PH), soft_e[:, :, :],
                            bc(soft_s[:, 1, :], TOPK), ALU.mult))

                def piece(tile, b):
                    if tile == 0 and b % 2 == 0 and b < 8:
                        dve.wait_ge(s_ev, n.take(s_ev))
                    if tile > 0 and b < 8:
                        load_scores(tile, 2 * b, 2 * b + 2)
                    if b < 8:
                        key_rows(2 * b, 2 * b + 2)
                    if b == 8:
                        candidates()
                    if 9 <= b < 13:
                        best_rows(2 * (b - 9), 2 * (b - 9) + 2)
                    if b == 13:
                        indices(tile, 0)
                    if b == 14:
                        indices(tile, 1)
                        soft_in()

                def add_experts(tile):
                    dve.wait_ge(v_done, n.take(v_done, SEL, RING))
                    for h in range(2):
                        o = slice(h * 512, (h + 1) * 512)
                        ins = tt(y_tmp[:, o], psum[:, h, :], mod_row[:, 5 * D + h * 512:5 * D + (h + 1) * 512],
                                 ALU.mult)
                        if h == 0:
                            link(ins)
                        else:
                            ins.then_inc(y_free, n.post(y_free))
                    dve.wait_ge(y_free, n.own(y_free))
                    link(tt(x_res[:, tile, :], x_res[:, tile, :], y_tmp, ALU.add))

                if layer == 0:
                    for k in range(TOPK):
                        link(v_.memset(iota_i[:, k:k + 1], float(k)))
                for b in range(16):
                    piece(0, b)
                soft_out()
                for tile in range(LAT):
                    for b in range(BATCHES):
                        for j in range(RING):
                            col = b * RING + j
                            dve.wait_ge(u_full[j], n.take(u_full[j], 16))
                            v_.tensor_tensor_reduce(out=u_buf[j], in0=u_buf[j], in1=h_tok[:, tile, :], scale=1.0,
                                                    scalar=0.0, op0=ALU.mult, op1=ALU.add,
                                                    accum_out=dots[:, col:col + 1]).then_inc(u_free, n.post(u_free))
                        if tile < LAT - 1:
                            piece(tile + 1, b)
                    dve.wait_ge(u_free, n.own(u_free))
                    dve.sem_inc(a_dots, n.post(a_dots))
                    dve.wait_ge(gelu_ready, n.take(gelu_ready))
                    tt(wts[:, tile * SEL:(tile + 1) * SEL], gelu[:, :], gate[:, :], ALU.mult).then_inc(
                        w_ready, n.post(w_ready))
                    dve.wait_ge(w_ready, n.own(w_ready))
                    if tile > 0:
                        add_experts(tile - 1)
                    if tile < LAT - 1:
                        soft_out()
                add_experts(LAT - 1)
                meet(dve, n, [dve_step])

            peer(0)
            if layers == 2:
                replicate(1)
                dve.wait_ge(in_modb, 14 * 16)
                mod_rows(6, 0, False)
                dve.wait_ge(in_nw, 4 * 16)
                scale_rows()
                dve.wait_ge(in_row, 16)
                link(tt(row(2), row(2), y_tmp, ALU.mult))
                modulated([(x_res[:, t, :], row(1), row(0), h_tok[:, t, :]) for t in range(LAT)])
                dve.wait_ge(py_ps, n.take(py_ps))
                for t in range(LAT):
                    for h in range(2):
                        o = slice(h * 512, (h + 1) * 512)
                        link(tt(scr[:, o], psum[:, 2 * t + h, :], mod_row[:, 2 * D + h * 512:2 * D + (h + 1) * 512],
                                ALU.mult))
                        link(tt(x_res[:, t, o], x_res[:, t, o], scr[:, o], ALU.add))
                meet(dve, n, [dve_step])
                peer(1)
            dve.wait_ge(in_fin, 16)
            dve.wait_ge(rms_ready, n.take(rms_ready))
            link(v_.reciprocal(rinv[:, 0:LAT], rms[:, 0:LAT]))
            for t in range(LAT):
                stt(h_tok[:, t, :], x_res[:, t, :], rinv[:, t:t + 1], nw_row[:, 0:D], ALU.mult,
                    ALU.mult).then_inc(x_ready, n.post(x_ready))


_ORDER = ("x", "c", "ctx", "c_ctx", "mod_w", "mod_b", "norm_w", "xbc_w", "z_w", "dt_w", "conv_w", "conv_b",
          "dt_bias", "a_log", "ssd_d", "ssd_norm_w", "out_w", "pool_w", "pool_m", "pool_scale", "q_w", "keys",
          "u", "v", "final_norm_w")


def pool_matrices(rows=8, width=64, windows=(2, 4, 8, 16)):
    import numpy as np

    def line(count, k):
        lo = k // 2
        hi = k - 1 - lo
        m = np.zeros((count, count))
        for t in range(count):
            a, b = max(t - lo, 0), min(t + hi + 1, count)
            m[a:b, t] = 1.0 / (b - a)
        return m

    mats = [np.kron(line(rows, k), line(width, k)) - np.eye(rows * width) for k in windows]
    m = np.stack(mats).astype(np.float32)
    m = m.reshape(2, 2, LAT, P, SEQ).transpose(0, 3, 1, 2, 4)
    return np.ascontiguousarray(m.reshape(2, P, 2 * LAT * SEQ))


def kernel(x, c, ctx, c_ctx, mod_w, mod_b, norm_w, ssd_in_w, ssd_conv_w, ssd_conv_b, ssd_dt_bias,
           ssd_a_log, ssd_d, ssd_norm_w, ssd_out_w, pool_w, pool_scale, peer_q_w, peer_keys,
           peer_u, peer_v, final_norm_w):
    import numpy as _np
    import concourse.bacc as _bacc
    from concourse import mybir as _mybir
    from concourse.bass_utils import run_bass_kernel_spmd as _run

    def cols(w, blocks, width):
        k = w.shape[0] // P
        return w.reshape(k, P, blocks, width).transpose(2, 1, 0, 3).reshape(blocks, P, k * width)

    in_w = _np.asarray(ssd_in_w)[0]
    z_w, x_w, b_w, c_w, dt_w = _np.split(in_w, [INNER, 2 * INNER, 2 * INNER + D, 2 * INNER + 2 * D], axis=1)
    kd = D // P
    xbc = _np.concatenate([x_w.reshape(kd, P, GROUPS, 2 * P), b_w.reshape(kd, P, GROUPS, P),
                           c_w.reshape(kd, P, GROUPS, P)], axis=3)
    xbc = xbc.transpose(2, 1, 0, 3).reshape(GROUPS, P, kd * 4 * P)

    def channels(v):
        v = _np.asarray(v)
        xx = v[:, :INNER].reshape(-1, GROUPS, 2, P)
        bb = v[:, INNER:INNER + D].reshape(-1, GROUPS, 1, P)
        cc = v[:, INNER + D:].reshape(-1, GROUPS, 1, P)
        return _np.concatenate([xx, bb, cc], axis=2).transpose(3, 1, 2, 0).reshape(P, -1)

    mod_w = _np.asarray(mod_w)
    q_w = _np.asarray(peer_q_w)
    arrays = {
        "x": _np.asarray(x)[0], "ctx": _np.asarray(ctx)[0],
        "c": _np.asarray(c).reshape(KD, P).T, "c_ctx": _np.asarray(c_ctx).reshape(KD, P).T,
        "mod_w": _np.stack([cols(mod_w[i], 12, 512) for i in range(2)]),
        "mod_b": mod_b, "norm_w": norm_w,
        "xbc_w": xbc, "z_w": cols(z_w, GROUPS, 2 * P), "dt_w": cols(dt_w, 1, 2 * HEADS)[0],
        "conv_w": channels(_np.asarray(ssd_conv_w)[0]), "conv_b": channels(ssd_conv_b),
        "dt_bias": _np.asarray(ssd_dt_bias).reshape(-1), "a_log": _np.asarray(ssd_a_log).reshape(-1),
        "ssd_d": _np.asarray(ssd_d).reshape(CI, 2).T, "ssd_norm_w": _np.asarray(ssd_norm_w).reshape(CI, P).T,
        "out_w": _np.asarray(ssd_out_w)[0].reshape(4, 4, P, D).transpose(0, 2, 1, 3).reshape(4, P, 4 * D),
        "pool_w": _np.asarray(pool_w)[0].reshape(PGROUPS, 2, P, 2 * P).transpose(2, 0, 1, 3).reshape(P, -1),
        "pool_m": pool_matrices(), "pool_scale": _np.asarray(pool_scale)[0],
        "q_w": _np.stack([cols(q_w[i], 4, 512) for i in range(2)]),
        "keys": _np.asarray(peer_keys).reshape(2, HH, NKEY, P).transpose(0, 3, 1, 2).reshape(2, P, HH * NKEY),
        "u": _np.asarray(peer_u).reshape(2 * NEXP, D), "v": _np.asarray(peer_v).reshape(2 * NEXP, D),
        "final_norm_w": final_norm_w,
    }
    nc = _bacc.Bacc("TRN2", target_bir_lowering=False, num_devices=1)
    given, aps = {}, {}
    for name in _ORDER:
        array = _np.ascontiguousarray(arrays[name])
        given[f"in_{name}"] = array
        aps[name] = nc.dram_tensor(f"in_{name}", array.shape, _mybir.dt.from_np(array.dtype),
                                   kind="ExternalInput").ap()
    out = nc.dram_tensor("out_0", (SEQ, D), _mybir.dt.from_np(_np.dtype("float32")), kind="ExternalOutput").ap()
    hybrid(nc, aps, out)
    r = _run(nc, [given], core_ids=[0])
    return r.results[0]["out_0"].reshape(1, SEQ, D)
```

```python
from contextlib import ExitStack, contextmanager

import concourse.bass as bass
from concourse import mybir

F32 = mybir.dt.float32
U32 = mybir.dt.uint32
ALU = mybir.AluOpType
ACT = mybir.ActivationFunctionType
AX = mybir.AxisListType

P = 128
D = 1024
KD = D // P
LAT = 4
CTX = 2
TT = LAT + CTX
SEQ = LAT * P
CTX_LEN = CTX * P
GROUPS = 8
HPG = 4
HEADS = GROUPS * HPG
HD = 64
INNER = HEADS * HD
CI = INNER // P
TAPS = 5
HALO = TAPS // 2
PH = 8
HH = 2 * PH
NKEY = 128
TOPK = 16
SEL = PH * TOPK
CHUNKS = 2 * LAT
CHEADS = PH // 2
CROWS = 2 * CHEADS
CSEL = CHEADS * TOPK
NEXP = NKEY * NKEY
RING = 8
BATCHES = CSEL // RING
PGROUPS = 4
EPS = 1e-6
LOWEST = -3.0e38
ENGINES = 5
UNITS = [("lat", 0), ("lat", 1), ("lat", 2), ("ctx", 0), ("ctx", 1), ("ctx", 2), ("lat", 3),
         ("z", 0), ("z", 1), ("z", 2), ("z", 3)]
UNIT_BANKS = (0, 1, 2, 0, 1, 2, 0, 1, 2, 2, 0)
CONVS = 7
NU = len(UNITS)
MOD_BLOCKS = 6 * D // 512
MOD_COLS = 6 * D // P
MOD_PER = MOD_COLS // GROUPS
ST_BANKS = (0, 1, 5, 6, 7)
F_TILES, B_TILES = (0, 1, 2, 3, 4), (1, 0, 5, 4, 3)
SERIES = 9


class Counts:

    def __init__(self):
        self.posted, self.taken, self.phases = {}, {}, 0

    @staticmethod
    def add(table, sem, unit):
        entry = table.setdefault(sem.name, [0, 0])
        entry[1] += unit
        return entry[0] + entry[1]

    def post(self, sem, unit=1):
        self.add(self.posted, sem, unit)
        return unit

    def own(self, sem):
        return self.add(self.posted, sem, 0)

    def take(self, sem, unit=1, ahead=0):
        return self.add(self.taken, sem, unit) + ahead

    @contextmanager
    def loop(self, eng, rounds, posts, takes):
        starts = []
        with eng.Fori(0, rounds) as i:
            for table, per in ((self.posted, posts), (self.taken, takes)):
                start = {name: sum(entry) for name, entry in table.items()}
                per = {s.name: k for s, k in per.items()}
                starts.append((table, start, per))
                for name in set(start) | set(per):
                    base, k = start.get(name, 0), per.get(name, 0)
                    table[name] = [i * k + base if k else base, 0]
            yield i
        for table, start, per in starts:
            wrong = {name: entry[1] for name, entry in table.items() if entry[1] != per.get(name, 0)}
            assert not wrong, f"the round adds {wrong}"
            for name in table:
                table[name] = [start.get(name, 0) + rounds * per.get(name, 0), 0]


def hybrid(nc, a, out, layers=2):
    with ExitStack() as ctx:
        def sb(name, shape, dt=F32):
            return ctx.enter_context(nc.sbuf_tensor(name, shape, dt))

        def sem(name):
            return ctx.enter_context(nc.semaphore(name))

        psum = ctx.enter_context(nc.psum_tensor("psum", [P, 8, 512], F32))

        x_res = sb("x_res", [P, LAT, D])
        big = sb("big", [P, 8192])
        h_tok = big[:, 0:TT * D].rearrange("p (t d) -> p t d", t=TT)
        mod_ctx = big[:, TT * D:8192]
        cond_rep = big[:, 0:D].rearrange("p (k m) -> p k m", k=KD)
        y_t = big[:, :].rearrange("p (k t) -> p k t", k=CI)
        h_t = sb("h_t", [P, KD, TT * P])
        mod_acc = h_t
        mod_row = sb("mod_row", [P, 6 * D])
        scr = sb("scr", [P, 4096])
        x_ctx = scr[:, 0:CTX * D].rearrange("p (t d) -> p t d", t=CTX)
        nw_row = scr[:, 2048:4096]
        wbuf = sb("wbuf", [P, 2, 4096])
        ident = sb("ident", [P, P])
        ones = sb("ones", [P, P])
        zeros = sb("zeros", [P, P])
        mask_le = sb("mask_le", [P, P])
        mask_ge = sb("mask_ge", [P, P])
        mask_lt = sb("mask_lt", [P, P])
        mask_gt = sb("mask_gt", [P, P])
        cond = sb("cond", [P, 2, KD])
        eps = sb("eps", [P, 1])
        mod_col = sb("mod_col", [P, MOD_COLS])
        mod_six = sb("mod_six", [P, MOD_PER])
        ssq = sb("ssq", [P, 8])
        rms = sb("rms", [P, 8])
        rinv = sb("rinv", [P, 8])

        w_full = [sem(f"w_full{i}") for i in range(2)]
        w_free = sem("w_free")
        in_x, in_ctx, in_cond, in_modb, in_nw, in_small, in_keys, in_row, in_fin = map(
            sem, ("in_x", "in_ctx", "in_cond", "in_modb", "in_nw", "in_small", "in_keys", "in_row", "in_fin"))
        phase = sem("phase")
        dve_step, act_step, pool_step, pe_step = map(sem, ("dve_step", "act_step", "pool_step", "pe_step"))
        masks_ready, cond_ready, rep_ready = map(sem, ("masks_ready", "cond_ready", "rep_ready"))
        mod_acc_ready, mod_ps, mod_ev = map(sem, ("mod_acc_ready", "mod_ps", "mod_ev"))
        mw_full, mw_free = [sem(f"mw_full{i}") for i in range(2)], sem("mw_free")
        in_crow, crow_ready, u_used, row_dg, row_ps, row_ev = map(
            sem, ("in_crow", "crow_ready", "u_used", "row_dg", "row_ps", "row_ev"))
        rms_ready, h_ready, tr_ps, ht_ready = map(sem, ("rms_ready", "h_ready", "tr_ps", "ht_ready"))
        dt_ps, dt_abs, dt_exp, a_ready, seg_ps, seg_exp, dec_ready = map(
            sem, ("dt_ps", "dt_abs", "dt_exp", "a_ready", "seg_ps", "seg_exp", "dec_ready"))
        pj_ps, pj_ev, conv_done, xs_ready = map(sem, ("pj_ps", "pj_ev", "conv_done", "xs_ready"))
        pe_group, dve_group = sem("pe_group"), sem("dve_group")
        tok_ps, tok_ready, xd_ready, st_ps, st_done = map(
            sem, ("tok_ps", "tok_ready", "xd_ready", "st_ps", "st_done"))
        r_ready, t1_ready, dee_ps, e_ready, cb_ps, m_ready, ce_ready, y_ps, y_ev, sq_ready, yz_ready = map(
            sem, ("r_ready", "t1_ready", "dee_ps", "e_ready", "cb_ps", "m_ready", "ce_ready", "y_ps",
                  "y_ev", "sq_ready", "yz_ready"))
        yn_ready, ysq_ps, ysq_rt, op_ps = map(sem, ("yn_ready", "ysq_ps", "ysq_rt", "op_ps"))
        q_ps, qt_ready, s_ps, s_ev, pl_ps, pl_ev, py_ps, x_ready = map(
            sem, ("q_ps", "qt_ready", "s_ps", "s_ev", "pl_ps", "pl_ev", "py_ps", "x_ready"))
        scored = sem("scored")
        idx_ready, st_go, u_free, a_dots, gelu_ready, ex_in, ex_ready, w_ready, dg_ready, v_done, y_free = map(
            sem, ("idx_ready", "st_go", "u_free", "a_dots", "gelu_ready", "ex_in", "ex_ready", "w_ready",
                  "dg_ready", "v_done", "y_free"))
        u_full = [sem(f"u_full{i}") for i in range(RING)]
        v_full = [sem(f"v_full{i}") for i in range(RING)]
        stored = sem("stored")

        with ExitStack() as scope:
            def tmp(name, shape, dt=F32):
                return scope.enter_context(nc.sbuf_tensor(name, shape, dt))

            pre_l = tmp("pre_l", [P, 4, SEQ + 2 * HALO])
            pre_c = tmp("pre_c", [P, 3, CTX_LEN + 2 * HALO])
            cv_l = tmp("cv_l", [P, 4, SEQ])
            cv_c = tmp("cv_c", [P, 3, CTX_LEN])
            z_t = tmp("z_t", [P, 2, SEQ])
            tok = tmp("tok", [P, TT, 3 * P])
            r1 = tmp("r1", [P, 2, HPG, P])
            ef = tmp("ef", [P, 2, HPG, P])
            tw = tmp("tw", [P, HPG, P])
            dtv = tmp("dtv", [P, TT, 2 * HEADS])
            av = tmp("av", [P, TT, 2 * HEADS])
            ea = tmp("ea", [P, TT, 2 * HEADS])
            wd = tmp("wd", [P, TT, 2 * HEADS])
            alr = tmp("alr", [P, 2 * HEADS])
            dtb = tmp("dtb", [P, 2 * HEADS])
            cw = tmp("cw", [P, GROUPS * 4 * TAPS])
            cbias = tmp("cbias", [P, GROUPS * 4])
            dcol = tmp("dcol", [P, CI])
            nwcol = tmp("nwcol", [P, CI])
            sqacc = tmp("sqacc", [P, SEQ])
            c_row = tmp("c_row", [P, D])
        st_tmp = ef[:, :, :, :].rearrange("p w (b h) l -> p w b (h l)", b=2)
        mw_buf = [wbuf[:, 1, (2 + j) * D:(3 + j) * D] for j in range(2)]
        s_in = mod_row[:, 0:2 * D].rearrange("p (w c n) -> p w c n", w=2, c=LAT)
        m_ce = scr[:, 0:3072].rearrange("p (b s h l) -> p b s h l", b=2, s=3, h=HPG)
        e_mat = scr[:, 3072:3584].rearrange("p (h l) -> p h l", h=HPG)
        t1 = scr[:, 3584:4096].rearrange("p (h l) -> p h l", h=HPG)
        xd = scr[:, 0:2560].rearrange("p (s w n) -> p s w n", s=5, w=2)
        n384 = TT * 2 * HEADS
        dt_x, dt_u, dt_z, dt_q, dt_r = (
            big[:, i * n384:(i + 1) * n384].rearrange("p (t h) -> p t h", t=TT) for i in range(5))

        with ExitStack() as scope:
            def tmp2(name, shape, dt=F32):
                return scope.enter_context(nc.sbuf_tensor(name, shape, dt))

            scores = tmp2("scores", [P, LAT - 1, HH * NKEY])
            u_more = tmp2("u_more", [P, 3, D])
            top_v = tmp2("top_v", [P, CROWS, TOPK])
            top_i = tmp2("top_i", [P, CROWS, TOPK], U32)
            top_f = tmp2("top_f", [P, CROWS, TOPK])
            best = tmp2("best", [P, CHEADS, TOPK])
            pos = tmp2("pos", [P, CHEADS, TOPK], U32)
            part = tmp2("part", [P, 2, CSEL], U32)
            part_f = tmp2("part_f", [P, 2, CSEL])
            ids_f = tmp2("ids_f", [P, 2, CSEL])
            ids = tmp2("ids", [P, LAT * SEL], U32)
            stage = tmp2("stage", [P, 4, RING], U32)
            soft = tmp2("soft", [P, CHEADS, TOPK])
            soft_e = tmp2("soft_e", [P, CHEADS, TOPK])
            soft_s = tmp2("soft_s", [P, 2, CHEADS])
            gate = tmp2("gate", [P, CSEL])
            dots = tmp2("dots", [P, CSEL])
            gelu = tmp2("gelu", [P, CSEL])
            wts = tmp2("wts", [P, LAT * SEL])
            diag = tmp2("diag", [P, RING, P])
            iota_i = tmp2("iota_i", [P, TOPK])
        work = scr[:, 0:2048]
        pick = scr[:, 2048:2048 + CSEL * TOPK].rearrange("p (s j) -> p s j", s=CSEL)
        u_buf = [mod_row[:, j * D:(j + 1) * D] for j in range(5)] + [u_more[:, j, :] for j in range(3)]
        h_flat = h_t[:, :, :].rearrange("p k t -> p (k t)")
        v_buf = [h_flat[:, j * D:(j + 1) * D] for j in range(6)] + [
            big[:, 6 * D:7 * D], big[:, 7 * D:8 * D]]
        keys = big[:, 4 * D:6 * D]
        q_t = big[:, 6 * D:7 * D].rearrange("p (b t) -> p b t", b=2)
        q_0 = big[:, 7 * D:8 * D].rearrange("p (b t) -> p b t", b=2)
        y_tmp = big[:, 4 * D:5 * D]

        block = ctx.enter_context(nc.Block())

        def bc(ap, n):
            return ap.unsqueeze(2).to_broadcast([P, ap.shape[1], n])

        def rep(ap, n):
            return ap.unsqueeze(1).to_broadcast([P, n, ap.shape[1]])

        def rows(ap):
            return ap.unsqueeze(0).to_broadcast([P, ap.shape[0]])

        def meet(eng, n, own):
            for s in own:
                eng.wait_ge(s, n.own(s))
            eng.sem_inc(phase, 1)
            n.phases += 1
            eng.wait_ge(phase, ENGINES * n.phases)

        @block.sync
        def _(sp):
            n = Counts()

            def weights(b, src, cols):
                sp.wait_ge(w_free, n.take(w_free))
                sp.dma_start(wbuf[:, b, 0:cols], src).then_inc(w_full[b], n.post(w_full[b], 16))

            def bias_rows(layer, lo, hi):
                for r in range(lo, hi):
                    sp.dma_start(mod_row[:, r * D:(r + 1) * D],
                                 rows(a["mod_b"][layer, r * D:(r + 1) * D])).then_inc(in_modb, 16)

            def norm_rows(layer):
                for r in range(2):
                    sp.dma_start(nw_row[:, r * D:(r + 1) * D], rows(a["norm_w"][layer, r])).then_inc(in_nw, 16)

            def mod_columns(g, lo, hi):
                for k in range(lo, hi):
                    sp.wait_ge(mw_free, n.take(mw_free))
                    sp.dma_start(mw_buf[k % 2], a["mod_wt"][g * MOD_PER + k]).then_inc(
                        mw_full[k % 2], n.post(mw_full[k % 2], 16))

            for s, name in enumerate(("c", "c_ctx")):
                sp.dma_start(cond[:, s, :], a[name]).then_inc(in_cond, 16)
            for e in range(2):
                weights(e, a["mod_w"][e], 4096)
            bias_rows(0, 0, 6)
            norm_rows(0)
            for r in range(2):
                sp.dma_start(mod_ctx[:, r * D:(r + 1) * D],
                             rows(a["mod_b"][0, r * D:(r + 1) * D])).then_inc(in_modb, 16)
            sp.dma_start(x_ctx, a["ctx"].rearrange("(t p) d -> p t d", p=P)).then_inc(in_ctx, 16)
            sp.dma_start(x_res[:, :, :], a["x"].rearrange("(t p) d -> p t d", p=P)).then_inc(in_x, 16)
            with n.loop(sp, MOD_BLOCKS // 2 - 1, {w_full[0]: 16, w_full[1]: 16}, {w_free: 2}) as i:
                for e in range(2):
                    weights(e, a["mod_w"][i * 2 + (2 + e)], 4096)
            sp.dma_start(c_row[:, :], rows(a["c_row"])).then_inc(in_crow, 16)
            for dst, src in ((cw[:, :], a["conv_w"]), (cbias[:, :], a["conv_b"]), (nwcol[:, :], a["ssd_norm_w"]),
                             (alr[:, :], rows(a["a_log"])), (dtb[:, :], rows(a["dt_bias"])),
                             (dcol[0:HD, :], a["ssd_d"][0].unsqueeze(0).to_broadcast([HD, CI])),
                             (dcol[HD:P, :], a["ssd_d"][1].unsqueeze(0).to_broadcast([HD, CI]))):
                sp.dma_start(dst, src).then_inc(in_small, 16)
            weights(0, a["dt_w"], KD * 2 * HEADS)
            weights(1, a["dt_w"], KD * 2 * HEADS)
            with n.loop(sp, GROUPS, {w_full[0]: 16, w_full[1]: 16, **{s: 8 * MOD_PER for s in mw_full}},
                        {w_free: 2, mw_free: MOD_PER}) as g:
                weights(0, a["xbc_w"][g], 4096)
                mod_columns(g, 0, 2)
                weights(1, a["z_w"][g], 2048)
                mod_columns(g, 2, MOD_PER)
            sp.wait_ge(mw_free, n.take(mw_free, 2))
            for m in range(4):
                weights(m % 2, a["out_w"][m], 4096)
            meet(sp, n, [])

            def peer_loads(layer):
                sp.dma_start(keys, a["keys"][layer]).then_inc(in_keys, 16)
                for m in range(4):
                    weights(m % 2, a["q_w"][layer, m], 4096)
                with n.loop(sp, 2, {w_full[0]: 16, w_full[1]: 16}, {w_free: 2}) as i:
                    for e in range(2):
                        weights(e, a["q_w"][layer, i * 2 + e], 4096)
                sp.wait_ge(u_used, n.take(u_used))
                if layer == 0:
                    bias_rows(1, 0, 5)
                    norm_rows(1)
                    for m in range(2):
                        weights(m, a["pool_m"][m], 4096)
                meet(sp, n, [])

            peer_loads(0)
            if layers == 2:
                bias_rows(1, 5, 6)
                sp.dma_start(y_tmp, rows(a["pool_scale"])).then_inc(in_row, 16)
                weights(0, a["pool_w"], 2048)
                weights(1, a["pool_w"], 2048)
                meet(sp, n, [])
                peer_loads(1)
            sp.dma_start(nw_row[:, 0:D], rows(a["final_norm_w"])).then_inc(in_fin, 16)
            for t in range(LAT):
                sp.wait_ge(x_ready, n.take(x_ready))
                sp.dma_start(out[t * P:(t + 1) * P, :], h_tok[:, t, :]).then_inc(stored, n.post(stored, 16))
            sp.wait_ge(stored, n.own(stored))

        @block.gpsimd
        def _(pool):
            n = Counts()
            g_ = nc.gpsimd

            def link(ins):
                ins.then_inc(pool_step, n.post(pool_step))
                pool.wait_ge(pool_step, n.own(pool_step))

            link(g_.memset(ones[:, :], 1.0))
            link(g_.memset(eps[:, :], EPS))
            link(g_.memset(zeros[:, :], 0.0))
            for dst, op, step in ((ident, ALU.is_equal, 1), (mask_le, ALU.is_ge, 1), (mask_ge, ALU.is_ge, -1),
                                  (mask_lt, ALU.is_gt, 1), (mask_gt, ALU.is_gt, -1)):
                ins = g_.affine_select(out=dst[:, :], in_=ones[:, :], compare_op=op, fill=0.0, base=0,
                                       pattern=[[step, P]], channel_multiplier=-step)
                link(ins)
            link(g_.memset(pre_l[:, :, :], 0.0))
            g_.memset(pre_c[:, :, :], 0.0).then_inc(masks_ready, n.post(masks_ready))
            pool.wait_ge(masks_ready, 1)

            pool.wait_ge(dec_ready, n.take(dec_ready))
            with n.loop(pool, GROUPS, {xd_ready: 10, r_ready: 2 * LAT, t1_ready: LAT},
                        {tok_ready: TT, pe_group: 1, dve_group: 1, dee_ps: 3 * LAT, m_ready: LAT}) as g:
                pool.wait_ge(pe_group, n.take(pe_group))
                pool.wait_ge(dve_group, n.take(dve_group))

                def spread(c):
                    if c > 0:
                        pool.wait_ge(dee_ps, n.take(dee_ps, 3))
                    for w, mask in ((0, mask_le), (1, mask_ge)):
                        g_.tensor_tensor(out=r1[:, w, :, :],
                                         in0=bc(av[:, CTX + c, bass.ds(g * HPG + w * HEADS, HPG)], P),
                                         in1=rep(mask[:, :], HPG), op=ALU.mult).then_inc(r_ready, n.post(r_ready))
                    if c > 0:
                        pool.wait_ge(m_ready, n.take(m_ready))
                    g_.tensor_tensor(out=t1, in0=bc(dtv[:, CTX + c, bass.ds(g * HPG, HPG)], P),
                                     in1=rep(mask_le[:, :], HPG), op=ALU.mult).then_inc(t1_ready, n.post(t1_ready))

                spread(0)
                for s in range(5):
                    for w, tile in ((0, F_TILES[s]), (1, B_TILES[s])):
                        if s == 0 and w == 0:
                            pool.wait_ge(tok_ready, n.take(tok_ready, TT))
                        g_.tensor_tensor(
                            out=xd[:, s, w, :].rearrange("p (h d) -> p h d", h=HPG),
                            in0=tok[:, tile, 0:2 * P].rearrange("p (h d) -> p h d", h=HPG),
                            in1=bc(wd[:, tile, bass.ds(g * HPG + w * HEADS, HPG)], HD),
                            op=ALU.mult).then_inc(xd_ready, n.post(xd_ready))
                for c in range(1, LAT):
                    spread(c)
                pool.wait_ge(dee_ps, n.take(dee_ps, 3))
                pool.wait_ge(m_ready, n.take(m_ready))
            meet(pool, n, [xd_ready, r_ready, t1_ready])

            def gather(table, col, buf, full, free, ahead):
                pool.wait_ge(free, n.take(free, 1, ahead))
                pool.sem_inc(st_go, 1)
                pool.indirect_dma_start(buf, None, table, bass.IndirectOffsetOnAxis(col, 0)).then_inc(
                    full, n.post(full, 16))

            def gathers(chunk):
                do_u, do_v = chunk < CHUNKS, chunk > 0
                posts = {pool_step: 4 if do_u and do_v else 2}
                takes = {}
                if do_u:
                    posts.update({s: 32 for s in u_full})
                    takes[u_free] = 2 * RING
                if do_v:
                    posts.update({s: 32 for s in v_full})
                    takes[v_done] = 2 * RING
                with n.loop(pool, BATCHES // 2, posts, takes) as i:
                    for e in range(2):
                        if do_u:
                            link(g_.tensor_copy(
                                stage[:, e, :], ids[:, bass.ds(i * (2 * RING) + (chunk * CSEL + e * RING), RING)]))
                        if do_v:
                            link(g_.tensor_copy(
                                stage[:, 2 + e, :],
                                ids[:, bass.ds(i * (2 * RING) + ((chunk - 1) * CSEL + e * RING), RING)]))
                        for j in range(RING):
                            if do_u:
                                gather(a["u"], stage[:, e, j:j + 1], u_buf[j], u_full[j], u_free, 0)
                            if do_v:
                                gather(a["v"], stage[:, 2 + e, j:j + 1], v_buf[j], v_full[j], v_done, 0)

            def peer():
                for chunk in range(CHUNKS + 1):
                    if chunk < CHUNKS:
                        pool.wait_ge(idx_ready, n.take(idx_ready))
                    if chunk == 1:
                        pool.wait_ge(scored, n.take(scored))
                    gathers(chunk)
                meet(pool, n, [])

            peer()
            if layers == 2:
                meet(pool, n, [])
                peer()

        @block.scalar
        def _(act):
            n = Counts()
            s_ = nc.scalar

            def link(ins):
                ins.then_inc(act_step, n.post(act_step))
                act.wait_ge(act_step, n.own(act_step))

            act.sem_inc(pj_ev, n.post(pj_ev, 3))
            act.wait_ge(in_cond, 32)
            s_.activation(cond[:, :, :], cond[:, :, :], ACT.Silu).then_inc(cond_ready, n.post(cond_ready))
            act.wait_ge(masks_ready, 1)

            def diagonals(rounds, first):
                with n.loop(act, rounds, {row_dg: 8}, {row_ps: 2}) as i:
                    for j in range(8):
                        if j % 4 == 0:
                            act.wait_ge(row_ps, n.take(row_ps))
                        s_.activation(diag[:, j, :], ident[:, :], ACT.Copy,
                                      scale=mod_col[:, bass.ds(i * 8 + (4 * first + j), 1)]).then_inc(
                            row_dg, n.post(row_dg))

            def norms(tiles):
                for c, (src, dump) in enumerate(tiles):
                    link(s_.activation(dump, src, ACT.Square, accum_out=ssq[:, c:c + 1]))
                s_.activation(rms[:, 0:len(tiles)], ssq[:, 0:len(tiles)], ACT.Sqrt, bias=eps[:, 0:1],
                              scale=1.0 / D).then_inc(rms_ready, n.post(rms_ready))

            def transposed(tiles, shift):
                for t in range(tiles):
                    for b in range(2):
                        act.wait_ge(tr_ps, n.take(tr_ps))
                        s_.copy(h_t[:, b * 4:(b + 1) * 4, (t + shift) * P:(t + shift + 1) * P],
                                psum[:, b, :].rearrange("p (k t) -> p k t", k=4)).then_inc(ht_ready, n.post(ht_ready))

            act.wait_ge(in_ctx, 16)
            act.wait_ge(in_x, 16)
            norms([(x_ctx[:, t, :], h_tok[:, CTX, :]) for t in range(CTX)] +
                  [(x_res[:, t, :], h_tok[:, CTX, :]) for t in range(LAT)])
            transposed(TT, 0)
            act.wait_ge(in_crow, 16)
            s_.activation(c_row[:, :], c_row[:, :], ACT.Silu).then_inc(crow_ready, n.post(crow_ready))
            act.wait_ge(in_small, 7 * 16)
            link(s_.activation(alr[:, :], alr[:, :], ACT.Exp))
            act.wait_ge(dt_abs, n.take(dt_abs))
            s_.activation(dt_u, dt_u, ACT.Exp, scale=-1.0).then_inc(dt_exp, n.post(dt_exp))
            act.wait_ge(seg_ps, n.take(seg_ps))
            link(s_.activation(ea[:, :, :], psum[:, 1, 0:n384].rearrange("p (t h) -> p t h", t=TT), ACT.Exp))
            for w in range(2):
                ins = s_.activation(wd[:, :, w * HEADS:(w + 1) * HEADS],
                                    psum[:, 2 + w, 0:n384 // 2].rearrange("p (t h) -> p t h", t=TT), ACT.Exp)
                if w == 0:
                    link(ins)
            ins.then_inc(seg_exp, n.post(seg_exp))

            with n.loop(act, GROUPS, {pj_ev: NU, xs_ready: CONVS, tok_ready: TT,
                                      e_ready: 3 * LAT, sq_ready: 1, act_step: 1, yn_ready: 1},
                        {pj_ps: NU, conv_done: CONVS, tok_ps: TT, st_done: 1, dee_ps: 3 * LAT, m_ready: LAT, ce_ready: LAT,
                         yz_ready: 1, dve_group: 1}) as g:
                def evacuate(unit):
                    kind, col = UNITS[unit]
                    act.wait_ge(pj_ps, n.take(pj_ps))
                    bank = UNIT_BANKS[unit]
                    if kind == "ctx":
                        src, dst = psum[:, bank, 0:CTX_LEN], pre_c[:, col, HALO:HALO + CTX_LEN]
                    elif kind == "lat":
                        src, dst = psum[:, bank, :], pre_l[:, col, HALO:HALO + SEQ]
                    else:
                        src = psum[:, bank, 0:2 * P]
                        dst = z_t[:, col // 2, col % 2 * 2 * P:(col % 2 + 1) * 2 * P]
                    s_.activation(dst, src, ACT.Silu if kind == "z" else ACT.Copy).then_inc(pj_ev, n.post(pj_ev))

                def silu(unit):
                    kind, col = UNITS[unit]
                    act.wait_ge(conv_done, n.take(conv_done))
                    buf = cv_c[:, col, :] if kind == "ctx" else cv_l[:, col, :]
                    s_.activation(buf, buf, ACT.Silu).then_inc(xs_ready, n.post(xs_ready))

                evacuate(0)
                evacuate(1)
                for k in range(2, CONVS):
                    evacuate(k)
                    silu(k - 2)
                silu(CONVS - 2)
                for t in range(TT):
                    act.wait_ge(tok_ps, n.take(tok_ps))
                    s_.copy(tok[:, t, :], psum[:, 6 + t % 2, 0:3 * P]).then_inc(tok_ready, n.post(tok_ready))
                silu(CONVS - 1)
                act.wait_ge(dve_group, n.take(dve_group))
                evacuate(7)
                evacuate(8)
                for c in range(LAT):
                    for w in range(3):
                        if c == 0 and w == 2:
                            evacuate(9)
                        if c == 0 and w == 1:
                            act.wait_ge(st_done, n.take(st_done))
                        act.wait_ge(dee_ps, n.take(dee_ps))
                        if c > 0 and w == 0:
                            act.wait_ge(m_ready, n.take(m_ready))
                            act.wait_ge(ce_ready, n.take(ce_ready))
                        dst = e_mat if w == 0 else ef[:, w - 1, :, :]
                        s_.activation(dst, psum[:, 3 + w, :].rearrange("p (h l) -> p h l", h=HPG),
                                      ACT.Exp).then_inc(e_ready, n.post(e_ready))
                evacuate(10)
                act.wait_ge(m_ready, n.take(m_ready))
                act.wait_ge(ce_ready, n.take(ce_ready))
                act.wait_ge(yz_ready, n.take(yz_ready))
                s_.activation(z_t[:, :, :], y_t[:, bass.ds(g * 2, 2), :], ACT.Square).then_inc(sq_ready, n.post(sq_ready))
                act.wait_ge(sq_ready, n.own(sq_ready))
                for j in range(2):
                    ins = s_.activation(y_t[:, bass.ds(g * 2 + j, 1), :], y_t[:, bass.ds(g * 2 + j, 1), :], ACT.Copy,
                                        scale=nwcol[:, bass.ds(g * 2 + j, 1)])
                    if j == 0:
                        ins.then_inc(act_step, n.post(act_step))
                ins.then_inc(yn_ready, n.post(yn_ready))
            act.wait_ge(ysq_ps, n.take(ysq_ps))
            s_.activation(rms[:, 0:LAT], psum[:, 0, 0:LAT], ACT.Sqrt, bias=eps[:, 0:1],
                          scale=1.0 / INNER).then_inc(ysq_rt, n.post(ysq_rt))
            meet(act, n, [ysq_rt])

            def peer(layer):
                norms([(x_res[:, t, :], h_tok[:, t, :]) for t in range(LAT)])
                transposed(LAT, 0)

                def q_copy(s):
                    act.wait_ge(q_ps, n.take(q_ps))
                    s_.copy(q_t[:, s % 2, 0:3 * P], psum[:, 2 + s % 2, 0:3 * P]).then_inc(qt_ready, n.post(qt_ready))

                def s_copy(i, s):
                    act.wait_ge(s_ps, n.take(s_ps))
                    s_.copy(scores[:, :, bass.ds(i * (8 * NKEY) + s * NKEY, NKEY)],
                            psum[:, 4 + s % 2, 0:3 * P].rearrange("p (t k) -> p t k", t=3)).then_inc(
                        s_ev, n.post(s_ev))

                for m in range(4):
                    act.wait_ge(q_ps, n.take(q_ps))
                    s_.copy(q_0[:, m % 2, :], psum[:, 2 + m % 2, :]).then_inc(qt_ready, n.post(qt_ready))
                    act.wait_ge(s_ps, n.take(s_ps))
                    s_.copy(work[:, m * 512:(m + 1) * 512], psum[:, 4 + m % 2, :]).then_inc(s_ev, n.post(s_ev))

                with n.loop(act, 2, {qt_ready: 8, s_ev: 8}, {q_ps: 8, s_ps: 8}) as i:
                    q_copy(0)
                    for s in range(1, 8):
                        if s >= 2:
                            s_copy(i, s - 2)
                        q_copy(s)
                    s_copy(i, 6)
                    s_copy(i, 7)

                def exps():
                    act.wait_ge(ex_in, n.take(ex_in))
                    s_.activation(soft_e[:, :, :], soft[:, :, :], ACT.Exp).then_inc(ex_ready, n.post(ex_ready))

                def gelus():
                    act.wait_ge(a_dots, n.take(a_dots))
                    s_.activation(gelu[:, :], dots[:, :], ACT.Gelu_apprx_tanh).then_inc(gelu_ready, n.post(gelu_ready))

                def diags(chunk):
                    act.wait_ge(w_ready, n.take(w_ready))
                    with n.loop(act, BATCHES, {dg_ready: RING}, {v_done: RING}) as b:
                        for j in range(RING):
                            act.wait_ge(v_done, n.take(v_done))
                            s_.activation(diag[:, j, :], ident[:, :], ACT.Copy,
                                          scale=wts[:, bass.ds(b * RING + (chunk * CSEL + j), 1)]).then_inc(
                                dg_ready, n.post(dg_ready))

                exps()
                for chunk in range(CHUNKS):
                    if chunk > 0:
                        diags(chunk - 1)
                    gelus()
                    if chunk < CHUNKS - 1:
                        exps()
                diags(CHUNKS - 1)
                meet(act, n, [dg_ready])

            peer(0)
            if layers == 2:
                diagonals(2, 0)
                norms([(x_res[:, t, :], h_tok[:, CTX, :]) for t in range(LAT)])
                diagonals(4, 4)
                for k in range(KD):
                    act.wait_ge(pl_ps, n.take(pl_ps))
                    s_.copy(h_t[:, k, 0:SEQ], psum[:, 4 + k % 4, :]).then_inc(pl_ev, n.post(pl_ev))
                meet(act, n, [pl_ev])
                peer(1)
            norms([(x_res[:, t, :], h_tok[:, t, :]) for t in range(LAT)])

        @block.tensor
        def _(pe):
            n = Counts()
            mm = nc.tensor.matmul

            pe.sem_inc(w_free, n.post(w_free, 2))
            pe.sem_inc(v_done, n.post(v_done, RING))
            pe.sem_inc(row_ps, n.post(row_ps, 2))
            pe.sem_inc(pe_group, n.post(pe_group))
            pe.wait_ge(masks_ready, 1)
            pe.wait_ge(rep_ready, 1)

            def product(dst, lhs, rhs, k):
                for j in range(k):
                    ins = mm(dst, lhs(j), rhs(j), start=(j == 0), stop=(j == k - 1))
                return ins

            def mod_blocks(pairs, both):
                per, shared = (4, 2) if both else (2, 1)
                with n.loop(pe, pairs, {mod_ps: per, w_free: 2},
                            {mod_ev: per, mod_acc_ready: shared, w_full[0]: 16, w_full[1]: 16}) as i:
                    for e in range(2):
                        w = wbuf[:, e, :].rearrange("p (k m) -> p k m", k=KD)
                        pe.wait_ge(w_full[e], n.take(w_full[e], 16))
                        if both or e == 0:
                            pe.wait_ge(mod_ev, n.take(mod_ev))
                            product(psum[:, 2 * e, :], lambda k: cond_rep[:, k, :], lambda k: w[:, k, :],
                                    KD).then_inc(mod_ps, n.post(mod_ps))
                        if both or e == 1:
                            pe.wait_ge(mod_ev, n.take(mod_ev))
                            pe.wait_ge(mod_acc_ready, n.take(mod_acc_ready))
                            mm(psum[:, 2 * e + 1, :], ones[:, :], mod_acc[:, e, 0:512], start=True,
                               stop=True).then_inc(mod_ps, n.post(mod_ps))
                        pe.wait_ge(mod_ps, n.own(mod_ps))
                        pe.sem_inc(w_free, n.post(w_free))

            def transposes(tiles, shift=0):
                for t in range(tiles):
                    pe.wait_ge(h_ready, n.take(h_ready))
                    for b in range(2):
                        if t > 0:
                            pe.wait_ge(ht_ready, n.take(ht_ready))
                        for k in range(4):
                            ins = nc.tensor.transpose(psum[:, b, k * P:(k + 1) * P],
                                                      h_tok[:, t, (b * 4 + k) * P:(b * 4 + k + 1) * P], ident[:, :])
                        ins.then_inc(tr_ps, n.post(tr_ps))
                pe.wait_ge(ht_ready, n.take(ht_ready, 2))

            mod_blocks(2, True)
            mod_blocks(4, False)
            transposes(TT)

            wdt = wbuf[:, 0, 0:KD * 2 * HEADS].rearrange("p (k m) -> p k m", k=KD)
            pe.wait_ge(w_full[0], n.take(w_full[0], 16))
            for t in range(TT):
                ins = product(psum[:, 2, t * 2 * HEADS:(t + 1) * 2 * HEADS],
                              lambda k: h_t[:, k, t * P:(t + 1) * P], lambda k: wdt[:, k, :], KD)
            ins.then_inc(dt_ps, n.post(dt_ps))
            pe.wait_ge(w_full[1], n.take(w_full[1], 16))
            pe.wait_ge(dt_ps, n.own(dt_ps))
            pe.sem_inc(w_free, n.post(w_free, 2))
            pe.wait_ge(a_ready, n.take(a_ready))
            mm(psum[:, 1, 0:n384], ones[:, :], av[:, :, :], start=True, stop=True)
            mm(psum[:, 2, 0:n384 // 2], mask_gt[:, :], av[:, :, 0:HEADS], start=True, stop=True)
            mm(psum[:, 3, 0:n384 // 2], mask_lt[:, :], av[:, :, HEADS:2 * HEADS], start=True,
               stop=True).then_inc(seg_ps, n.post(seg_ps))
            pe.wait_ge(seg_exp, n.take(seg_exp))

            with n.loop(pe, GROUPS,
                        {pj_ps: NU, w_free: 2, tok_ps: TT, st_ps: 1, dee_ps: 3 * LAT, cb_ps: LAT, y_ps: LAT,
                         pe_group: 1},
                        {w_full[0]: 16, w_full[1]: 16, pj_ev: NU, xs_ready: CONVS, tok_ready: TT, xd_ready: 10,
                         st_done: 1, r_ready: 2 * LAT, e_ready: 3 * LAT, m_ready: LAT, ce_ready: LAT,
                         y_ev: LAT}) as g:
                wx = wbuf[:, 0, :].rearrange("p (k m) -> p k m", k=KD)
                wz = wbuf[:, 1, 0:2048].rearrange("p (k m) -> p k m", k=KD)

                def project(unit):
                    kind, col = UNITS[unit]
                    lo, hi = (0, CTX_LEN) if kind == "ctx" else (CTX_LEN, TT * P)
                    if kind == "z":
                        lo, hi, col = CTX_LEN + col % 2 * 2 * P, CTX_LEN + (col % 2 + 1) * 2 * P, col // 2
                    if unit == 0:
                        pe.wait_ge(w_full[0], n.take(w_full[0], 16))
                    if unit == 7:
                        pe.wait_ge(pj_ps, n.own(pj_ps))
                        pe.sem_inc(w_free, n.post(w_free))
                        pe.wait_ge(w_full[1], n.take(w_full[1], 16))
                    pe.wait_ge(pj_ev, n.take(pj_ev, 1, 0 if unit else 2))
                    w = wz if kind == "z" else wx
                    ins = product(psum[:, UNIT_BANKS[unit], 0:hi - lo], lambda j: w[:, j, col * P:(col + 1) * P],
                                  lambda j: h_t[:, j, lo:hi], KD)
                    ins.then_inc(pj_ps, n.post(pj_ps))

                for unit in range(CONVS):
                    project(unit)
                for t in range(TT):
                    if t == 0:
                        pe.wait_ge(xs_ready, n.take(xs_ready, CONVS - 1))
                    if t >= 2:
                        pe.wait_ge(tok_ready, n.take(tok_ready))
                    for j in range(3):
                        src = cv_c[:, j, t * P:(t + 1) * P] if t < CTX else cv_l[:, j, (t - CTX) * P:(t - CTX + 1) * P]
                        ins = nc.tensor.transpose(psum[:, 6 + t % 2, j * P:(j + 1) * P], src, ident[:, :])
                    ins.then_inc(tok_ps, n.post(tok_ps))
                project(7)
                project(8)
                pe.wait_ge(tok_ready, n.take(tok_ready, 2))
                pe.wait_ge(pj_ev, n.take(pj_ev, 0, 3))
                for s in range(5):
                    for w, tile in ((0, F_TILES[s]), (1, B_TILES[s])):
                        pe.wait_ge(xd_ready, n.take(xd_ready))
                        ins = mm(psum[:, ST_BANKS[s], w * 256:(w + 1) * 256], tok[:, tile, 2 * P:3 * P], xd[:, s, w, :],
                                 start=True, stop=True)
                ins.then_inc(st_ps, n.post(st_ps))

                def decays(c):
                    pe.wait_ge(r_ready, n.take(r_ready, 2))
                    if c == 1:
                        pe.wait_ge(pj_ev, n.take(pj_ev, 0, 3))
                    if c > 0:
                        pe.wait_ge(e_ready, n.take(e_ready, 3))
                    mm(psum[:, 3, :], mask_gt[:, :], r1[:, 0, :, :], start=True, stop=False)
                    mm(psum[:, 3, :], mask_lt[:, :], r1[:, 1, :, :], start=False, stop=True).then_inc(
                        dee_ps, n.post(dee_ps))
                    for w in range(2):
                        if c == 0 and w == 1:
                            project(9)
                            pe.wait_ge(st_done, n.take(st_done))
                        mm(psum[:, 4 + w, :], ones[:, :], r1[:, w, :, :], start=True, stop=True).then_inc(
                            dee_ps, n.post(dee_ps))
                    if c == 0:
                        pe.wait_ge(xs_ready, n.take(xs_ready))
                    mm(psum[:, (7, 2)[c % 2], 0:P], cv_l[:, 2, c * P:(c + 1) * P], cv_l[:, 3, c * P:(c + 1) * P],
                       start=True, stop=True).then_inc(cb_ps, n.post(cb_ps))

                def outputs(c):
                    pe.wait_ge(m_ready, n.take(m_ready))
                    pe.wait_ge(ce_ready, n.take(ce_ready))
                    bank = (6, 1)[c % 2]
                    if c >= 2:
                        pe.wait_ge(y_ev, n.take(y_ev))
                    for r in range(HPG):
                        half, pair = r % 2, r // 2
                        dst = psum[half * HD:(half + 1) * HD, bank, pair * P:(pair + 1) * P]
                        cols = slice(r * HD, (r + 1) * HD)
                        mm(dst, tok[:, CTX + c, cols], m_ce[:, c % 2, 0, r, :], start=True, stop=False)
                        mm(dst, s_in[:, 0, c, cols], m_ce[:, c % 2, 1, r, :], start=False, stop=False)
                        ins = mm(dst, s_in[:, 1, c, cols], m_ce[:, c % 2, 2, r, :], start=False, stop=True)
                    ins.then_inc(y_ps, n.post(y_ps))

                decays(0)
                for c in range(1, LAT):
                    decays(c)
                    outputs(c - 1)
                project(10)
                pe.wait_ge(pj_ps, n.own(pj_ps))
                pe.sem_inc(w_free, n.post(w_free))
                outputs(LAT - 1)
                pe.wait_ge(e_ready, n.take(e_ready, 3))
                pe.wait_ge(y_ev, n.take(y_ev, 2))
                pe.wait_ge(y_ps, n.own(y_ps))
                pe.sem_inc(pe_group, n.post(pe_group))

            pe.wait_ge(dve_group, GROUPS + 1)
            pe.wait_ge(yn_ready, GROUPS)
            for t in range(LAT):
                ins = mm(psum[:, 0, t:t + 1], sqacc[:, t * P:(t + 1) * P], ones[:, 0:1], start=True, stop=True)
            ins.then_inc(ysq_ps, n.post(ysq_ps))
            pe.wait_ge(ysq_rt, 1)
            for m in range(4):
                w = wbuf[:, m % 2, :].rearrange("p (k d) -> p k d", k=4)
                pe.wait_ge(w_full[m % 2], n.take(w_full[m % 2], 16))
                for k in range(4):
                    for t in range(LAT):
                        for h in range(2):
                            ins = mm(psum[:, 2 * t + h, :], y_t[:, 4 * m + k, t * P:(t + 1) * P],
                                     w[:, k, h * 512:(h + 1) * 512], start=(m + k == 0), stop=(m == 3 and k == 3))
                if m < 3:
                    ins.then_inc(w_free, n.post(w_free))
                else:
                    ins.then_inc(op_ps, n.post(op_ps))
                    pe.wait_ge(op_ps, n.own(op_ps))
                    pe.sem_inc(w_free, n.post(w_free))
            meet(pe, n, [op_ps])

            def peer(layer):
                transposes(LAT)
                pe.wait_ge(in_keys, n.take(in_keys, 16))

                def queries(e, s):
                    w = wbuf[:, e, :].rearrange("p (k m) -> p k m", k=KD)
                    ins = product(psum[:, 2 + s % 2, 0:3 * P], lambda k: w[:, k, (s % 4) * P:(s % 4 + 1) * P],
                                  lambda k: h_t[:, k, P:SEQ], KD)
                    ins.then_inc(q_ps, n.post(q_ps))
                    if s % 4 == 3:
                        pe.wait_ge(q_ps, n.own(q_ps))
                        pe.sem_inc(w_free, n.post(w_free))

                def key_scores(i, s):
                    pe.wait_ge(qt_ready, n.take(qt_ready))
                    if s >= 2:
                        pe.wait_ge(s_ev, n.take(s_ev))
                    for t in range(LAT - 1):
                        ins = mm(psum[:, 4 + s % 2, t * P:(t + 1) * P], q_t[:, s % 2, t * P:(t + 1) * P],
                                 keys[:, bass.ds(i * (8 * NKEY) + s * NKEY, NKEY)], start=True, stop=True)
                    ins.then_inc(s_ps, n.post(s_ps))

                def first_queries(m):
                    w = wbuf[:, m % 2, :].rearrange("p (k m) -> p k m", k=KD)
                    pe.wait_ge(w_full[m % 2], n.take(w_full[m % 2], 16))
                    for s in range(4):
                        ins = product(psum[:, 2 + m % 2, s * P:(s + 1) * P], lambda k: w[:, k, s * P:(s + 1) * P],
                                      lambda k: h_t[:, k, 0:P], KD)
                    ins.then_inc(q_ps, n.post(q_ps))
                    pe.wait_ge(q_ps, n.own(q_ps))
                    pe.sem_inc(w_free, n.post(w_free))

                def first_scores(m):
                    pe.wait_ge(qt_ready, n.take(qt_ready))
                    if m >= 2:
                        pe.wait_ge(s_ev, n.take(s_ev))
                    for s in range(4):
                        ins = mm(psum[:, 4 + m % 2, s * P:(s + 1) * P], q_0[:, m % 2, s * P:(s + 1) * P],
                                 keys[:, (4 * m + s) * NKEY:(4 * m + s + 1) * NKEY], start=True, stop=True)
                    ins.then_inc(s_ps, n.post(s_ps))

                first_queries(0)
                for m in range(1, 4):
                    first_queries(m)
                    first_scores(m - 1)
                first_scores(3)
                pe.wait_ge(s_ev, n.take(s_ev, 2))
                with n.loop(pe, 2, {q_ps: 8, w_free: 2, s_ps: 8},
                            {w_full[0]: 16, w_full[1]: 16, qt_ready: 8, s_ev: 8}) as i:
                    for s in range(8):
                        if s % 4 == 0:
                            pe.wait_ge(w_full[s // 4], n.take(w_full[s // 4], 16))
                        queries(s // 4, s)
                        if s >= 1:
                            key_scores(i, s - 1)
                    key_scores(i, 7)
                    pe.wait_ge(s_ev, n.take(s_ev, 2))
                pe.sem_inc(scored, n.post(scored))
                for tile in range(LAT):
                    pe.wait_ge(y_free, n.take(y_free))
                    for h in range(2):
                        mm(psum[:, h, :], zeros[:, :], h_tok[:, 0, 0:512], start=True, stop=True, skip_group_check=True)
                    with n.loop(pe, 2 * BATCHES, {v_done: RING},
                                {dg_ready: RING, **{s: 16 for s in v_full}}) as b:
                        for j in range(RING):
                            pe.wait_ge(v_full[j], n.take(v_full[j], 16))
                            pe.wait_ge(dg_ready, n.take(dg_ready))
                            for h in range(2):
                                ins = mm(psum[:, h, :], diag[:, j, :], v_buf[j][:, h * 512:(h + 1) * 512],
                                         start=False, stop=True, skip_group_check=True)
                            ins.then_inc(v_done, n.post(v_done))
                meet(pe, n, [v_done])

            peer(0)
            if layers == 2:
                for b in range(MOD_BLOCKS):
                    pe.wait_ge(row_dg, n.take(row_dg, 4))
                    if b >= 8:
                        pe.wait_ge(row_ev, n.take(row_ev))
                    mm(psum[:, b % 8, :], ones[:, :], diag[:, b % 2 * 4:b % 2 * 4 + 4, :], start=True,
                       stop=True).then_inc(row_ps, n.post(row_ps))
                pe.wait_ge(h_ready, n.take(h_ready, LAT))
                for k in range(KD):
                    gidx, m = k // 2, k // 4
                    if k % 4 == 0:
                        pe.wait_ge(w_full[m], n.take(w_full[m], 16))
                    if k < 4:
                        pe.wait_ge(row_ev, n.take(row_ev))
                    else:
                        pe.wait_ge(pl_ev, n.take(pl_ev))
                    w = wbuf[:, m, :].rearrange("p (g t n) -> p g t n", g=2, t=LAT)
                    ins = product(psum[:, 4 + k % 4, :], lambda t: h_tok[:, t, k * P:(k + 1) * P],
                                  lambda t: w[:, gidx % 2, t, :], LAT)
                    ins.then_inc(pl_ps, n.post(pl_ps))
                    if k % 4 == 3:
                        pe.wait_ge(pl_ps, n.own(pl_ps))
                        pe.sem_inc(w_free, n.post(w_free))
                pe.wait_ge(pl_ev, n.take(pl_ev, 4))
                pe.wait_ge(row_ev, n.take(row_ev, 4))
                w = wbuf[:, 0, 0:2048].rearrange("p (g c n) -> p g c n", g=PGROUPS, c=2)
                pe.wait_ge(w_full[0], n.take(w_full[0], 16))
                for t in range(LAT):
                    for gi in range(PGROUPS):
                        for c in range(2):
                            ins = mm(psum[:, 2 * t + gi // 2, (gi % 2) * 256:(gi % 2 + 1) * 256],
                                     h_t[:, 2 * gi + c, t * P:(t + 1) * P], w[:, gi, c, :],
                                     start=(c == 0), stop=(c == 1))
                ins.then_inc(py_ps, n.post(py_ps))
                pe.wait_ge(py_ps, n.own(py_ps))
                pe.wait_ge(w_full[1], n.take(w_full[1], 16))
                pe.sem_inc(w_free, n.post(w_free, 2))
                meet(pe, n, [py_ps])
                peer(1)

        @block.vector
        def _(dve):
            n = Counts()
            v_ = nc.vector

            def step(ins):
                ins.then_inc(dve_step, n.post(dve_step))

            def link(ins):
                step(ins)
                dve.wait_ge(dve_step, n.own(dve_step))

            def tt(o, i0, i1, op):
                return v_.tensor_tensor(out=o, in0=i0, in1=i1, op=op)

            def stt(o, i0, s, i1, op0, op1):
                return v_.scalar_tensor_tensor(out=o, in0=i0, scalar=s, in1=i1, op0=op0, op1=op1)

            dve.sem_inc(mod_ev, n.post(mod_ev, 2))
            dve.sem_inc(dve_group, n.post(dve_group))
            dve.sem_inc(u_free, n.post(u_free, RING))
            dve.sem_inc(y_free, n.post(y_free))
            dve.sem_inc(mw_free, n.post(mw_free, 2))

            def replicate():
                v_.tensor_copy(cond_rep, bc(cond[:, 0, :], P)).then_inc(rep_ready, n.post(rep_ready))
                dve.wait_ge(rep_ready, n.own(rep_ready))

            def mod_rows(pairs, first, both):
                per, shared = (4, 2) if both else (2, 1)

                def accumulate(e, s):
                    w = wbuf[:, e, :].rearrange("p (k m) -> p k m", k=KD)
                    acc = mod_acc[:, e, 0:512]
                    dve.wait_ge(w_full[e], n.take(w_full[e], 16))
                    link(v_.tensor_scalar(acc, w[:, 0, :], cond[:, s, 0:1], None, ALU.mult))
                    for k in range(1, KD):
                        ins = stt(acc, w[:, k, :], cond[:, s, k:k + 1], acc, ALU.mult, ALU.add)
                        if k < KD - 1:
                            link(ins)
                        else:
                            ins.then_inc(mod_acc_ready, n.post(mod_acc_ready))

                def add_block(i, e, s, bank):
                    dve.wait_ge(mod_ps, n.take(mod_ps))
                    to = (mod_ctx if s else mod_row)[:, bass.ds(i * 1024 + (first + e) * 512, 512)]
                    tt(to, to, psum[:, bank, :], ALU.add).then_inc(mod_ev, n.post(mod_ev))

                posts = {mod_ev: per, mod_acc_ready: shared, dve_step: shared * (KD - 1)}
                takes = {mod_ps: per, w_full[1]: 16}
                if both:
                    takes[w_full[0]] = 16
                with n.loop(dve, pairs, posts, takes) as i:
                    if both:
                        for e in range(2):
                            accumulate(e, 1)
                            add_block(i, e, 0, 2 * e)
                            add_block(i, e, 1, 2 * e + 1)
                    else:
                        accumulate(1, 0)
                        add_block(i, 0, 0, 0)
                        add_block(i, 1, 0, 3)
                dve.wait_ge(mod_ev, n.own(mod_ev))

            def row(r):
                return mod_row[:, r * D:(r + 1) * D]

            def scale_row(sub):
                r = row(1 + 3 * sub)
                link(stt(r, r, 1.0, nw_row[:, sub * D:(sub + 1) * D], ALU.add, ALU.mult))

            def modulated(tiles):
                dve.wait_ge(rms_ready, n.take(rms_ready))
                link(v_.reciprocal(rinv[:, 0:len(tiles)], rms[:, 0:len(tiles)]))
                for c, (src, arow, brow, dst) in enumerate(tiles):
                    link(stt(dst, src, rinv[:, c:c + 1], arow, ALU.mult, ALU.mult))
                    tt(dst, dst, brow, ALU.add).then_inc(h_ready, n.post(h_ready))

            dve.wait_ge(cond_ready, n.take(cond_ready))
            dve.wait_ge(masks_ready, 1)
            replicate()
            dve.wait_ge(in_modb, 8 * 16)
            mod_rows(2, 0, True)
            mod_rows(4, 4, False)
            dve.wait_ge(in_nw, 2 * 16)
            link(stt(mod_ctx[:, D:2 * D], mod_ctx[:, D:2 * D], 1.0, nw_row[:, 0:D], ALU.add, ALU.mult))
            scale_row(0)
            scale_row(1)
            modulated([(x_ctx[:, t, :], mod_ctx[:, D:2 * D], mod_ctx[:, 0:D], h_tok[:, t, :]) for t in range(CTX)] +
                      [(x_res[:, t, :], row(1), row(0), h_tok[:, CTX + t, :]) for t in range(LAT)])

            dve.wait_ge(in_small, 7 * 16)
            dve.wait_ge(dt_ps, n.take(dt_ps))
            dve.wait_ge(h_ready, n.own(h_ready))
            link(tt(dt_x, psum[:, 2, 0:n384].rearrange("p (t h) -> p t h", t=TT), rep(dtb[:, :], TT), ALU.add))
            stt(dt_u, dt_x, -1.0, dt_x, ALU.mult, ALU.max).then_inc(dt_abs, n.post(dt_abs))
            dve.wait_ge(dt_exp, n.take(dt_exp))
            link(v_.tensor_scalar(dt_z, dt_u, 2.0, None, ALU.add))
            link(v_.reciprocal(dt_q, dt_z))
            link(tt(dt_z, dt_u, dt_q, ALU.mult))
            link(tt(dt_u, dt_z, dt_z, ALU.mult))
            link(v_.tensor_scalar(dt_q, dt_u, 1.0 / (2 * SERIES + 1), None, ALU.mult))
            for k in range(SERIES - 1, 0, -1):
                link(stt(dt_q, dt_q, 1.0 / (2 * k + 1), dt_u, ALU.add, ALU.mult))
            link(stt(dt_q, dt_q, 1.0, dt_z, ALU.add, ALU.mult))
            link(v_.tensor_scalar(dt_x, dt_x, 0.0, None, ALU.max))
            link(stt(dtv[:, :, :], dt_q, 2.0, dt_x, ALU.mult, ALU.add))
            stt(av[:, :, :], dtv[:, :, :], -1.0, rep(alr[:, :], TT), ALU.mult, ALU.mult).then_inc(
                a_ready, n.post(a_ready))
            dve.wait_ge(seg_exp, n.take(seg_exp))
            link(v_.memset(sqacc[:, :], 0.0))
            tt(wd[:, :, :], wd[:, :, :], dtv[:, :, :], ALU.mult).then_inc(dec_ready, n.post(dec_ready))
            dve.wait_ge(dec_ready, n.own(dec_ready))

            dve.wait_ge(crow_ready, n.take(crow_ready))
            steps = CONVS * (TAPS - 1) + 17 + LAT * 7 + 2
            with n.loop(dve, GROUPS, {dve_step: steps, mw_free: MOD_PER, conv_done: CONVS, st_done: 1, m_ready: LAT, ce_ready: LAT,
                                      y_ev: LAT, yz_ready: 1, dve_group: 1},
                        {pj_ev: NU, pe_group: 1, st_ps: 1, t1_ready: LAT, e_ready: 3 * LAT, cb_ps: LAT,
                         y_ps: LAT, xs_ready: CONVS, sq_ready: 1, **{s: 8 * MOD_PER for s in mw_full}}) as g:

                def mod_column(k):
                    buf = mw_buf[k % 2]
                    dve.wait_ge(mw_full[k % 2], n.take(mw_full[k % 2], 16))
                    v_.tensor_tensor_reduce(out=buf, in0=buf, in1=c_row[:, :], scale=1.0, scalar=0.0, op0=ALU.mult,
                                            op1=ALU.add, accum_out=mod_six[:, k:k + 1]).then_inc(
                        mw_free, n.post(mw_free))

                dve.wait_ge(pe_group, n.take(pe_group))
                for k in range(MOD_PER // 2):
                    mod_column(k)
                for k in range(CONVS):
                    dve.wait_ge(pj_ev, n.take(pj_ev, 1, 3))
                    kind, j = UNITS[k]
                    width = CTX_LEN if kind == "ctx" else SEQ
                    src, dst = (pre_c, cv_c[:, j, :]) if kind == "ctx" else (pre_l, cv_l[:, j, :])

                    def weight(tap):
                        return cw[:, bass.ds(g * (4 * TAPS) + (j * TAPS + tap), 1)]

                    link(v_.tensor_scalar(dst, src[:, j, 0:width], weight(0), cbias[:, bass.ds(g * 4 + j, 1)],
                                           ALU.mult, ALU.add))
                    for tap in range(1, TAPS):
                        ins = stt(dst, src[:, j, tap:tap + width], weight(tap), dst, ALU.mult, ALU.add)
                        if tap < TAPS - 1:
                            link(ins)
                        else:
                            ins.then_inc(conv_done, n.post(conv_done))
                    if k < MOD_PER // 2:
                        mod_column(MOD_PER // 2 + k)
                dve.wait_ge(mw_free, n.own(mw_free))
                link(v_.tensor_copy(mod_col[:, bass.ds(g * MOD_PER, MOD_PER)], mod_six[:, :]))
                dve.wait_ge(st_ps, n.take(st_ps))
                where = {}
                for s in range(5):
                    for w, tile in ((0, F_TILES[s]), (1, B_TILES[s])):
                        new = psum[:, ST_BANKS[s], w * 256:(w + 1) * 256]
                        if s == 0:
                            dst = st_tmp[:, w, 0, :]
                            link(v_.tensor_copy(dst, new))
                        else:
                            dst = s_in[:, w, s - 1 if w == 0 else LAT - s, :]
                            old, mid = where[w], st_tmp[:, w, 1, :]
                            link(tt(mid.rearrange("p (h d) -> p h d", h=HPG),
                                     old.rearrange("p (h d) -> p h d", h=HPG),
                                     bc(ea[:, tile, bass.ds(g * HPG + w * HEADS, HPG)], HD), ALU.mult))
                            ins = tt(dst, mid, new, ALU.add)
                            if s == 4 and w == 1:
                                ins.then_inc(st_done, n.post(st_done))
                            else:
                                link(ins)
                        where[w] = dst
                dve.wait_ge(st_done, n.own(st_done))
                dve.wait_ge(xs_ready, n.take(xs_ready, CONVS))

                def prepare(c):
                    b = c % 2
                    dve.wait_ge(t1_ready, n.take(t1_ready))
                    for r in range(HPG):
                        ins = stt(tw[:, r, :], mask_ge[:, :], dtv[:, CTX + c, bass.ds(g * HPG + (HEADS + r), 1)],
                                  t1[:, r, :], ALU.mult, ALU.add)
                        link(ins)
                    dve.wait_ge(e_ready, n.take(e_ready, 3))
                    link(tt(m_ce[:, b, 0, :, :], tw[:, :, :], e_mat, ALU.mult))
                    dve.wait_ge(cb_ps, n.take(cb_ps))
                    tt(m_ce[:, b, 0, :, :], m_ce[:, b, 0, :, :], rep(psum[:, (7, 2)[b], 0:P], HPG),
                       ALU.mult).then_inc(m_ready, n.post(m_ready))
                    link(tt(m_ce[:, b, 1, :, :], ef[:, 0, :, :], rep(cv_l[:, 3, c * P:(c + 1) * P], HPG), ALU.mult))
                    tt(m_ce[:, b, 2, :, :], ef[:, 1, :, :], rep(cv_l[:, 3, c * P:(c + 1) * P], HPG),
                       ALU.mult).then_inc(ce_ready, n.post(ce_ready))

                def finish(c):
                    dve.wait_ge(y_ps, n.take(y_ps))
                    for pair in range(2):
                        ins = stt(y_t[:, bass.ds(g * 2 + pair, 1), c * P:(c + 1) * P].rearrange("p o t -> p (o t)"),
                                  cv_l[:, pair, c * P:(c + 1) * P],
                                  dcol[:, bass.ds(g * 2 + pair, 1)], psum[:, (6, 1)[c % 2], pair * P:(pair + 1) * P],
                                  ALU.mult, ALU.add)
                        if pair == 0:
                            link(ins)
                        else:
                            ins.then_inc(y_ev, n.post(y_ev))

                prepare(0)
                for c in range(1, LAT):
                    prepare(c)
                    finish(c - 1)
                finish(LAT - 1)
                dve.wait_ge(y_ev, n.own(y_ev))
                dve.wait_ge(pj_ev, n.take(pj_ev, NU - CONVS, 3))
                both = y_t[:, bass.ds(g * 2, 2), :]
                tt(both, both, z_t[:, :, :], ALU.mult).then_inc(yz_ready, n.post(yz_ready))
                dve.wait_ge(sq_ready, n.take(sq_ready))
                link(tt(sqacc[:, :], sqacc[:, :], z_t[:, 0, :], ALU.add))
                tt(sqacc[:, :], sqacc[:, :], z_t[:, 1, :], ALU.add).then_inc(dve_group, n.post(dve_group))
                dve.wait_ge(dve_group, n.own(dve_group))

            dve.wait_ge(ysq_rt, 1)
            link(v_.reciprocal(rinv[:, 0:LAT], rms[:, 0:LAT]))
            dve.wait_ge(op_ps, n.take(op_ps))
            for t in range(LAT):
                for h in range(2):
                    o = slice(h * 512, (h + 1) * 512)
                    link(stt(scr[:, o], psum[:, 2 * t + h, :], rinv[:, t:t + 1],
                             mod_row[:, 2 * D + h * 512:2 * D + (h + 1) * 512], ALU.mult, ALU.mult))
                    link(tt(x_res[:, t, o], x_res[:, t, o], scr[:, o], ALU.add))
            meet(dve, n, [dve_step])

            def peer(layer):
                modulated([(x_res[:, t, :], row(4), row(3), h_tok[:, t, :]) for t in range(LAT)])
                dve.wait_ge(h_ready, n.own(h_ready))

                def load_scores(tile, lo, hi):
                    if tile == 1:
                        dve.wait_ge(s_ev, n.take(s_ev, hi - lo))
                    o = slice(lo * NKEY, hi * NKEY)
                    link(v_.tensor_copy(work[:, o], scores[:, tile - 1, o]))

                def top16(val, idx, src):
                    link(v_.max(val[:, 0:8], src))
                    link(v_.max_index(idx[:, 0:8], val[:, 0:8], src))
                    link(v_.match_replace(src, val[:, 0:8], src, LOWEST))
                    link(v_.max(val[:, 8:16], src))
                    link(v_.max_index(idx[:, 8:16], val[:, 8:16], src))

                def key_rows(lo, hi):
                    for r in range(lo, hi):
                        top16(top_v[:, r % CROWS, :], top_i[:, r % CROWS, :], work[:, r * NKEY:(r + 1) * NKEY])

                def pairs(chunk, h):
                    o = (chunk % 2 * CHEADS + h) * 2 * NKEY
                    return work[:, o:o + TOPK * TOPK]

                def candidates(chunk):
                    link(v_.tensor_copy(top_f[:, :, :], top_i[:, :, :]))
                    for h in range(CHEADS):
                        step(tt(pairs(chunk, h).rearrange("p (i j) -> p i j", i=TOPK),
                                bc(top_v[:, 2 * h, :], TOPK), rep(top_v[:, 2 * h + 1, :], TOPK), ALU.add))
                    dve.wait_ge(dve_step, n.own(dve_step))

                def best_rows(chunk, lo, hi):
                    for h in range(lo, hi):
                        top16(best[:, h, :], pos[:, h, :], pairs(chunk, h))

                def indices(chunk, which):
                    flat = pos[:, :, :].rearrange("p h k -> p (h k)")
                    if which == 0:
                        link(v_.tensor_scalar(part[:, 0, :], flat, 4, None, ALU.logical_shift_right))
                        link(v_.tensor_scalar(part[:, 1, :], flat, 15, None, ALU.bitwise_and))
                        link(v_.tensor_copy(part_f[:, :, :], part[:, :, :]))
                    link(tt(pick, bc(part_f[:, which, :], TOPK), rep(iota_i[:, :], CSEL), ALU.is_equal))
                    for h in range(CHEADS):
                        sl = pick[:, h * TOPK:(h + 1) * TOPK, :]
                        step(tt(sl, sl, rep(top_f[:, 2 * h + which, :], TOPK), ALU.mult))
                    dve.wait_ge(dve_step, n.own(dve_step))
                    link(v_.tensor_reduce(ids_f[:, which, :], pick, AX.X, ALU.add))
                    if which == 1:
                        link(stt(ids_f[:, 0, :], ids_f[:, 0, :], float(NKEY), ids_f[:, 1, :], ALU.mult, ALU.add))
                        v_.tensor_scalar(ids[:, chunk * CSEL:(chunk + 1) * CSEL], ids_f[:, 0, :],
                                         float(layer * NEXP), None, ALU.add).then_inc(idx_ready, n.post(idx_ready))
                        dve.wait_ge(idx_ready, n.own(idx_ready))

                def soft_in():
                    tt(soft[:, :, :], best[:, :, :], best[:, :, 0:1].to_broadcast([P, CHEADS, TOPK]),
                       ALU.subtract).then_inc(ex_in, n.post(ex_in))

                def soft_out():
                    dve.wait_ge(ex_ready, n.take(ex_ready))
                    link(v_.tensor_reduce(soft_s[:, 0, :], soft_e[:, :, :], AX.X, ALU.add))
                    link(v_.reciprocal(soft_s[:, 1, :], soft_s[:, 0, :]))
                    link(tt(gate[:, :].rearrange("p (h k) -> p h k", h=CHEADS), soft_e[:, :, :],
                            bc(soft_s[:, 1, :], TOPK), ALU.mult))

                def piece(chunk, b):
                    tile, row = chunk // 2, chunk % 2 * CROWS + 2 * b
                    if tile == 0 and b in (0, 2):
                        dve.wait_ge(s_ev, n.take(s_ev))
                    if b < 4:
                        if tile > 0:
                            load_scores(tile, row, row + 2)
                        key_rows(row, row + 2)
                    if b == 4:
                        candidates(chunk)
                        best_rows(chunk, 0, 1)
                    if b == 5:
                        best_rows(chunk, 1, 3)
                    if b == 6:
                        best_rows(chunk, 3, 4)
                        indices(chunk, 0)
                    if b == 7:
                        indices(chunk, 1)
                        soft_in()

                def add_experts(tile):
                    dve.wait_ge(v_done, n.take(v_done, SEL, RING))
                    for h in range(2):
                        o = slice(h * 512, (h + 1) * 512)
                        ins = tt(y_tmp[:, o], psum[:, h, :], mod_row[:, 5 * D + h * 512:5 * D + (h + 1) * 512],
                                 ALU.mult)
                        if h == 0:
                            link(ins)
                        else:
                            ins.then_inc(y_free, n.post(y_free))
                    dve.wait_ge(y_free, n.own(y_free))
                    link(tt(x_res[:, tile, :], x_res[:, tile, :], y_tmp, ALU.add))

                if layer == 0:
                    for k in range(TOPK):
                        link(v_.memset(iota_i[:, k:k + 1], float(k)))
                for b in range(BATCHES):
                    piece(0, b)
                for chunk in range(CHUNKS):
                    for b in range(BATCHES):
                        if b == BATCHES - 1:
                            soft_out()
                        if chunk < CHUNKS - 1:
                            piece(chunk + 1, b)
                        for j in range(RING):
                            col = b * RING + j
                            dve.wait_ge(u_full[j], n.take(u_full[j], 16))
                            v_.tensor_tensor_reduce(out=u_buf[j], in0=u_buf[j], in1=h_tok[:, chunk // 2, :], scale=1.0,
                                                    scalar=0.0, op0=ALU.mult, op1=ALU.add,
                                                    accum_out=dots[:, col:col + 1]).then_inc(u_free, n.post(u_free))
                    dve.wait_ge(u_free, n.own(u_free))
                    dve.sem_inc(a_dots, n.post(a_dots))
                    if chunk == CHUNKS - 1:
                        dve.sem_inc(u_used, n.post(u_used))
                    dve.wait_ge(gelu_ready, n.take(gelu_ready))
                    tt(wts[:, chunk * CSEL:(chunk + 1) * CSEL], gelu[:, :], gate[:, :], ALU.mult).then_inc(
                        w_ready, n.post(w_ready))
                    dve.wait_ge(w_ready, n.own(w_ready))
                    if chunk % 2 == 0 and chunk > 0:
                        add_experts(chunk // 2 - 1)
                add_experts(LAT - 1)
                meet(dve, n, [dve_step])

            peer(0)
            if layers == 2:
                def add_rows(lo, hi):
                    for b in range(lo, hi):
                        dve.wait_ge(row_ps, n.take(row_ps, 1, 2))
                        to = mod_row[:, b * 512:(b + 1) * 512]
                        tt(to, to, psum[:, b % 8, :], ALU.add).then_inc(row_ev, n.post(row_ev))
                    dve.wait_ge(row_ev, n.own(row_ev))

                dve.wait_ge(in_modb, 14 * 16)
                dve.wait_ge(in_nw, 4 * 16)
                add_rows(0, 4)
                scale_row(0)
                modulated([(x_res[:, t, :], row(1), row(0), h_tok[:, t, :]) for t in range(LAT)])
                add_rows(4, MOD_BLOCKS)
                scale_row(1)
                dve.wait_ge(in_row, 16)
                link(tt(row(2), row(2), y_tmp, ALU.mult))
                dve.wait_ge(py_ps, n.take(py_ps))
                for t in range(LAT):
                    for h in range(2):
                        o = slice(h * 512, (h + 1) * 512)
                        link(tt(scr[:, o], psum[:, 2 * t + h, :], mod_row[:, 2 * D + h * 512:2 * D + (h + 1) * 512],
                                ALU.mult))
                        link(tt(x_res[:, t, o], x_res[:, t, o], scr[:, o], ALU.add))
                meet(dve, n, [dve_step])
                peer(1)
            dve.wait_ge(in_fin, 16)
            dve.wait_ge(rms_ready, n.take(rms_ready))
            link(v_.reciprocal(rinv[:, 0:LAT], rms[:, 0:LAT]))
            for t in range(LAT):
                stt(h_tok[:, t, :], x_res[:, t, :], rinv[:, t:t + 1], nw_row[:, 0:D], ALU.mult,
                    ALU.mult).then_inc(x_ready, n.post(x_ready))


_ORDER = ("x", "c", "ctx", "c_ctx", "c_row", "mod_w", "mod_wt", "mod_b", "norm_w", "xbc_w", "z_w", "dt_w", "conv_w", "conv_b",
          "dt_bias", "a_log", "ssd_d", "ssd_norm_w", "out_w", "pool_w", "pool_m", "pool_scale", "q_w", "keys",
          "u", "v", "final_norm_w")


def pool_matrices(rows=8, width=64, windows=(2, 4, 8, 16)):
    import numpy as np

    def line(count, k):
        lo = k // 2
        hi = k - 1 - lo
        m = np.zeros((count, count))
        for t in range(count):
            a, b = max(t - lo, 0), min(t + hi + 1, count)
            m[a:b, t] = 1.0 / (b - a)
        return m

    mats = [np.kron(line(rows, k), line(width, k)) - np.eye(rows * width) for k in windows]
    m = np.stack(mats).astype(np.float32)
    m = m.reshape(2, 2, LAT, P, SEQ).transpose(0, 3, 1, 2, 4)
    return np.ascontiguousarray(m.reshape(2, P, 2 * LAT * SEQ))


def kernel(x, c, ctx, c_ctx, mod_w, mod_b, norm_w, ssd_in_w, ssd_conv_w, ssd_conv_b, ssd_dt_bias,
           ssd_a_log, ssd_d, ssd_norm_w, ssd_out_w, pool_w, pool_scale, peer_q_w, peer_keys,
           peer_u, peer_v, final_norm_w):
    import numpy as _np
    import concourse.bacc as _bacc
    from concourse import mybir as _mybir
    from concourse.bass_utils import run_bass_kernel_spmd as _run

    def cols(w, blocks, width):
        k = w.shape[0] // P
        return w.reshape(k, P, blocks, width).transpose(2, 1, 0, 3).reshape(blocks, P, k * width)

    in_w = _np.asarray(ssd_in_w)[0]
    z_w, x_w, b_w, c_w, dt_w = _np.split(in_w, [INNER, 2 * INNER, 2 * INNER + D, 2 * INNER + 2 * D], axis=1)
    kd = D // P
    xbc = _np.concatenate([x_w.reshape(kd, P, GROUPS, 2 * P), b_w.reshape(kd, P, GROUPS, P),
                           c_w.reshape(kd, P, GROUPS, P)], axis=3)
    xbc = xbc.transpose(2, 1, 0, 3).reshape(GROUPS, P, kd * 4 * P)

    def channels(v):
        v = _np.asarray(v)
        xx = v[:, :INNER].reshape(-1, GROUPS, 2, P)
        bb = v[:, INNER:INNER + D].reshape(-1, GROUPS, 1, P)
        cc = v[:, INNER + D:].reshape(-1, GROUPS, 1, P)
        return _np.concatenate([xx, bb, cc], axis=2).transpose(3, 1, 2, 0).reshape(P, -1)

    mod_w = _np.asarray(mod_w)
    q_w = _np.asarray(peer_q_w)
    arrays = {
        "x": _np.asarray(x)[0], "ctx": _np.asarray(ctx)[0],
        "c": _np.asarray(c).reshape(KD, P).T, "c_ctx": _np.asarray(c_ctx).reshape(KD, P).T,
        "c_row": _np.asarray(c).reshape(-1), "mod_w": cols(mod_w[0], MOD_BLOCKS, 512),
        "mod_wt": mod_w[1].T.reshape(MOD_COLS, P, D),
        "mod_b": mod_b, "norm_w": norm_w,
        "xbc_w": xbc, "z_w": cols(z_w, GROUPS, 2 * P), "dt_w": cols(dt_w, 1, 2 * HEADS)[0],
        "conv_w": channels(_np.asarray(ssd_conv_w)[0]), "conv_b": channels(ssd_conv_b),
        "dt_bias": _np.asarray(ssd_dt_bias).reshape(-1), "a_log": _np.asarray(ssd_a_log).reshape(-1),
        "ssd_d": _np.asarray(ssd_d).reshape(CI, 2).T, "ssd_norm_w": _np.asarray(ssd_norm_w).reshape(CI, P).T,
        "out_w": _np.asarray(ssd_out_w)[0].reshape(4, 4, P, D).transpose(0, 2, 1, 3).reshape(4, P, 4 * D),
        "pool_w": _np.asarray(pool_w)[0].reshape(PGROUPS, 2, P, 2 * P).transpose(2, 0, 1, 3).reshape(P, -1),
        "pool_m": pool_matrices(), "pool_scale": _np.asarray(pool_scale)[0],
        "q_w": _np.stack([cols(q_w[i], 4, 512) for i in range(2)]),
        "keys": _np.asarray(peer_keys).reshape(2, HH, NKEY, P).transpose(0, 3, 1, 2).reshape(2, P, HH * NKEY),
        "u": _np.asarray(peer_u).reshape(2 * NEXP, D), "v": _np.asarray(peer_v).reshape(2 * NEXP, D),
        "final_norm_w": final_norm_w,
    }
    nc = _bacc.Bacc("TRN2", target_bir_lowering=False, num_devices=1)
    given, aps = {}, {}
    for name in _ORDER:
        array = _np.ascontiguousarray(arrays[name])
        given[f"in_{name}"] = array
        aps[name] = nc.dram_tensor(f"in_{name}", array.shape, _mybir.dt.from_np(array.dtype),
                                   kind="ExternalInput").ap()
    out = nc.dram_tensor("out_0", (SEQ, D), _mybir.dt.from_np(_np.dtype("float32")), kind="ExternalOutput").ap()
    hybrid(nc, aps, out)
    r = _run(nc, [given], core_ids=[0])
    return r.results[0]["out_0"].reshape(1, SEQ, D)
```

```python
from contextlib import ExitStack, contextmanager

import concourse.bass as bass
from concourse import mybir

F32 = mybir.dt.float32
U32 = mybir.dt.uint32
ALU = mybir.AluOpType
ACT = mybir.ActivationFunctionType
AX = mybir.AxisListType

P = 128
D = 1024
KD = D // P
LAT = 4
CTX = 2
TT = LAT + CTX
SEQ = LAT * P
CTX_LEN = CTX * P
GROUPS = 8
HPG = 4
HEADS = GROUPS * HPG
HD = 64
INNER = HEADS * HD
CI = INNER // P
TAPS = 5
HALO = TAPS // 2
PH = 8
HH = 2 * PH
NKEY = 128
TOPK = 16
SEL = PH * TOPK
CHUNKS = 2 * LAT
CHEADS = PH // 2
CROWS = 2 * CHEADS
CSEL = CHEADS * TOPK
NEXP = NKEY * NKEY
RING = 8
BATCHES = CSEL // RING
PGROUPS = 4
HALVES = (1, 0)
EPS = 1e-6
LOWEST = -3.0e38
ENGINES = 5
UNITS = [("lat", 0), ("lat", 1), ("lat", 2), ("ctx", 0), ("ctx", 1), ("ctx", 2), ("lat", 3),
         ("z", 0), ("z", 1), ("z", 2), ("z", 3)]
UNIT_BANKS = (0, 1, 2, 0, 1, 2, 0, 1, 2, 2, 0)
CONVS = 7
NU = len(UNITS)
MOD_BLOCKS = 6 * D // 512
MOD_COLS = 6 * D // P
MOD_PER = MOD_COLS // GROUPS
ST_BANKS = (0, 1, 5, 6, 7)
F_TILES, B_TILES = (0, 1, 2, 3, 4), (1, 0, 5, 4, 3)
SERIES = 9


class Counts:

    def __init__(self):
        self.posted, self.taken, self.phases = {}, {}, 0

    @staticmethod
    def add(table, sem, unit):
        entry = table.setdefault(sem.name, [0, 0])
        entry[1] += unit
        return entry[0] + entry[1]

    def post(self, sem, unit=1):
        self.add(self.posted, sem, unit)
        return unit

    def own(self, sem):
        return self.add(self.posted, sem, 0)

    def take(self, sem, unit=1, ahead=0):
        return self.add(self.taken, sem, unit) + ahead

    @contextmanager
    def loop(self, eng, rounds, posts, takes):
        starts = []
        with eng.Fori(0, rounds) as i:
            for table, per in ((self.posted, posts), (self.taken, takes)):
                start = {name: sum(entry) for name, entry in table.items()}
                per = {s.name: k for s, k in per.items()}
                starts.append((table, start, per))
                for name in set(start) | set(per):
                    base, k = start.get(name, 0), per.get(name, 0)
                    table[name] = [i * k + base if k else base, 0]
            yield i
        for table, start, per in starts:
            wrong = {name: entry[1] for name, entry in table.items() if entry[1] != per.get(name, 0)}
            assert not wrong, f"the round adds {wrong}"
            for name in table:
                table[name] = [start.get(name, 0) + rounds * per.get(name, 0), 0]


def hybrid(nc, a, out, layers=2):
    with ExitStack() as ctx:
        def sb(name, shape, dt=F32):
            return ctx.enter_context(nc.sbuf_tensor(name, shape, dt))

        def sem(name):
            return ctx.enter_context(nc.semaphore(name))

        psum = ctx.enter_context(nc.psum_tensor("psum", [P, 8, 512], F32))

        x_res = sb("x_res", [P, LAT, D])
        big = sb("big", [P, 8192])
        h_tok = big[:, 0:TT * D].rearrange("p (t d) -> p t d", t=TT)
        mod_ctx = big[:, TT * D:8192]
        cond_rep = big[:, 0:D].rearrange("p (k m) -> p k m", k=KD)
        y_t = big[:, :].rearrange("p (k t) -> p k t", k=CI)
        h_t = sb("h_t", [P, KD, TT * P])
        mod_acc = h_t
        mod_row = sb("mod_row", [P, 6 * D])
        scr = sb("scr", [P, 4096])
        x_ctx = scr[:, 0:CTX * D].rearrange("p (t d) -> p t d", t=CTX)
        nw_row = scr[:, 2048:4096]
        wbuf = sb("wbuf", [P, 2, 4096])
        ident = sb("ident", [P, P])
        ones = sb("ones", [P, P])
        zeros = sb("zeros", [P, P])
        mask_le = sb("mask_le", [P, P])
        mask_ge = sb("mask_ge", [P, P])
        mask_lt = sb("mask_lt", [P, P])
        mask_gt = sb("mask_gt", [P, P])
        cond = sb("cond", [P, 2, KD])
        eps = sb("eps", [P, 1])
        mod_col = sb("mod_col", [P, MOD_COLS])
        mod_six = sb("mod_six", [P, MOD_PER])
        ssq = sb("ssq", [P, 8])
        rms = sb("rms", [P, 8])
        rinv = sb("rinv", [P, 8])

        w_full = [sem(f"w_full{i}") for i in range(2)]
        w_free = sem("w_free")
        in_x, in_ctx, in_cond, in_modb, in_nw, in_small, in_keys, in_row, in_fin = map(
            sem, ("in_x", "in_ctx", "in_cond", "in_modb", "in_nw", "in_small", "in_keys", "in_row", "in_fin"))
        phase = sem("phase")
        dve_step, act_step, pool_step = map(sem, ("dve_step", "act_step", "pool_step"))
        masks_ready, cond_ready, rep_ready = map(sem, ("masks_ready", "cond_ready", "rep_ready"))
        mod_acc_ready, mod_ps, mod_ev = map(sem, ("mod_acc_ready", "mod_ps", "mod_ev"))
        mw_full, mw_free = [sem(f"mw_full{i}") for i in range(2)], sem("mw_free")
        in_crow, crow_ready, u_used, row_dg, row_ps, row_ev = map(
            sem, ("in_crow", "crow_ready", "u_used", "row_dg", "row_ps", "row_ev"))
        avb_ready = sem("avb_ready")
        res_ready, in_poolw = sem("res_ready"), sem("in_poolw")
        rms_ready, h_ready, tr_ps, ht_ready = map(sem, ("rms_ready", "h_ready", "tr_ps", "ht_ready"))
        dt_ps, dt_abs, dt_exp, a_ready, seg_ps, seg_exp, dec_ready = map(
            sem, ("dt_ps", "dt_abs", "dt_exp", "a_ready", "seg_ps", "seg_exp", "dec_ready"))
        pj_ps, pj_ev, conv_done, xs_ready = map(sem, ("pj_ps", "pj_ev", "conv_done", "xs_ready"))
        pe_group, dve_group = sem("pe_group"), sem("dve_group")
        tok_ps, tok_ready, xd_ready, st_ps, st_done = map(
            sem, ("tok_ps", "tok_ready", "xd_ready", "st_ps", "st_done"))
        r_ready, t1_ready, dee_ps, e_ready, cb_ps, m_ready, y_ps, y_ev, sq_ready, yz_ready = map(
            sem, ("r_ready", "t1_ready", "dee_ps", "e_ready", "cb_ps", "m_ready", "y_ps",
                  "y_ev", "sq_ready", "yz_ready"))
        yn_ready, ysq_ps, ysq_rt, op_ps = map(sem, ("yn_ready", "ysq_ps", "ysq_rt", "op_ps"))
        q_ps, qt_ready, s_ps, s_ev, pl_ps, pl_ev, py_ps, x_ready = map(
            sem, ("q_ps", "qt_ready", "s_ps", "s_ev", "pl_ps", "pl_ev", "py_ps", "x_ready"))
        scored = sem("scored")
        idx_ready, st_go, u_free, a_dots, gelu_ready, ex_in, ex_ready, w_ready, dg_ready, v_done, y_free = map(
            sem, ("idx_ready", "st_go", "u_free", "a_dots", "gelu_ready", "ex_in", "ex_ready", "w_ready",
                  "dg_ready", "v_done", "y_free"))
        u_full = [sem(f"u_full{i}") for i in range(RING)]
        v_full = [sem(f"v_full{i}") for i in range(RING)]
        stored = sem("stored")

        with ExitStack() as scope:
            def tmp(name, shape, dt=F32):
                return scope.enter_context(nc.sbuf_tensor(name, shape, dt))

            pre_l = tmp("pre_l", [P, 4, SEQ + 2 * HALO])
            pre_c = tmp("pre_c", [P, 3, CTX_LEN + 2 * HALO])
            cv_l = tmp("cv_l", [P, 4, SEQ])
            cv_c = tmp("cv_c", [P, 3, CTX_LEN])
            z_t = tmp("z_t", [P, 2, SEQ])
            tok = tmp("tok", [P, TT, 3 * P])
            r1 = tmp("r1", [P, 2, HPG, P])
            ef = tmp("ef", [P, 2, 2 * 2 * P])
            tw = tmp("tw", [P, HPG, P])
            dtv = tmp("dtv", [P, TT, 2 * HEADS])
            av = tmp("av", [P, TT, 2 * HEADS])
            ea = tmp("ea", [P, TT, 2 * HEADS])
            wd = tmp("wd", [P, TT, 2 * HEADS])
            alr = tmp("alr", [P, 2 * HEADS])
            dtb = tmp("dtb", [P, 2 * HEADS])
            cw = tmp("cw", [P, GROUPS * 4 * TAPS])
            cbias = tmp("cbias", [P, GROUPS * 4])
            dcol = tmp("dcol", [P, CI])
            nwcol = tmp("nwcol", [P, CI])
            sqacc = tmp("sqacc", [P, SEQ])
            c_row = tmp("c_row", [P, D])
        st_tmp = ef[:, :, :].rearrange("p w (b n) -> p w b n", b=2)
        mw_buf = [wbuf[:, 1, (2 + j) * D:(3 + j) * D] for j in range(2)]
        s_in = mod_row[:, 0:2 * D].rearrange("p (w c n) -> p w c n", w=2, c=LAT)
        m_mat = scr[:, 0:1024].rearrange("p (b h l) -> p b h l", b=2, h=HPG)
        y_st = scr[:, 1024:1536]
        avb = scr[:, 2560:3072].rearrange("p (w n) -> p w n", w=2)
        e_mat = scr[:, 3072:3584].rearrange("p (h l) -> p h l", h=HPG)
        t1 = scr[:, 3584:4096].rearrange("p (h l) -> p h l", h=HPG)
        xd = scr[:, 0:2560].rearrange("p (s w n) -> p s w n", s=5, w=2)
        n384 = TT * 2 * HEADS
        dt_x, dt_u, dt_z, dt_q, dt_r = (
            big[:, i * n384:(i + 1) * n384].rearrange("p (t h) -> p t h", t=TT) for i in range(5))

        with ExitStack() as scope:
            def tmp2(name, shape, dt=F32):
                return scope.enter_context(nc.sbuf_tensor(name, shape, dt))

            scores = tmp2("scores", [P, LAT - 1, HH * NKEY])
            u_more = tmp2("u_more", [P, 3, D])
            top_v = tmp2("top_v", [P, CROWS, TOPK])
            top_i = tmp2("top_i", [P, CROWS, TOPK], U32)
            top_f = tmp2("top_f", [P, CROWS, TOPK])
            best = tmp2("best", [P, CHEADS, TOPK])
            pos = tmp2("pos", [P, CHEADS, TOPK], U32)
            part = tmp2("part", [P, 2, CSEL], U32)
            part_f = tmp2("part_f", [P, 2, CSEL])
            ids_f = tmp2("ids_f", [P, 2, CSEL])
            ids = tmp2("ids", [P, LAT * SEL], U32)
            stage = tmp2("stage", [P, 4, RING], U32)
            soft = tmp2("soft", [P, CHEADS, TOPK])
            soft_e = tmp2("soft_e", [P, CHEADS, TOPK])
            soft_s = tmp2("soft_s", [P, 2, CHEADS])
            gate = tmp2("gate", [P, CSEL])
            dots = tmp2("dots", [P, CSEL])
            gelu = tmp2("gelu", [P, CSEL])
            wts = tmp2("wts", [P, LAT * SEL])
            diag = tmp2("diag", [P, RING, P])
            iota_i = tmp2("iota_i", [P, TOPK])
        work = scr[:, 0:2048]
        pick = scr[:, 2048:2048 + CSEL * TOPK].rearrange("p (s j) -> p s j", s=CSEL)
        u_buf = [mod_row[:, j * D:(j + 1) * D] for j in range(5)] + [u_more[:, j, :] for j in range(3)]
        h_flat = h_t[:, :, :].rearrange("p k t -> p (k t)")
        v_buf = [h_flat[:, j * D:(j + 1) * D] for j in range(6)] + [
            big[:, 6 * D:7 * D], big[:, 7 * D:8 * D]]
        keys = big[:, 4 * D:6 * D]
        q_t = big[:, 6 * D:7 * D].rearrange("p (b t) -> p b t", b=2)
        q_0 = big[:, 7 * D:8 * D].rearrange("p (b t) -> p b t", b=2)
        y_tmp = big[:, 4 * D:5 * D]
        pool_w = u_more[:, 0:2, :].rearrange("p a d -> p (a d)")

        block = ctx.enter_context(nc.Block())

        def bc(ap, n):
            return ap.unsqueeze(2).to_broadcast([P, ap.shape[1], n])

        def rep(ap, n):
            return ap.unsqueeze(1).to_broadcast([P, n, ap.shape[1]])

        def rows(ap):
            return ap.unsqueeze(0).to_broadcast([P, ap.shape[0]])

        def meet(eng, n, own):
            for s in own:
                eng.wait_ge(s, n.own(s))
            eng.sem_inc(phase, 1)
            n.phases += 1
            eng.wait_ge(phase, ENGINES * n.phases)

        @block.sync
        def _(sp):
            n = Counts()

            def weights(b, src, cols):
                sp.wait_ge(w_free, n.take(w_free))
                sp.dma_start(wbuf[:, b, 0:cols], src).then_inc(w_full[b], n.post(w_full[b], 16))

            def bias_rows(layer, lo, hi):
                for r in range(lo, hi):
                    sp.dma_start(mod_row[:, r * D:(r + 1) * D],
                                 rows(a["mod_b"][layer, r * D:(r + 1) * D])).then_inc(in_modb, 16)

            def norm_rows(layer):
                for r in range(2):
                    sp.dma_start(nw_row[:, r * D:(r + 1) * D], rows(a["norm_w"][layer, r])).then_inc(in_nw, 16)

            def mod_columns(g, lo, hi):
                for k in range(lo, hi):
                    sp.wait_ge(mw_free, n.take(mw_free))
                    sp.dma_start(mw_buf[k % 2], a["mod_wt"][g * MOD_PER + k]).then_inc(
                        mw_full[k % 2], n.post(mw_full[k % 2], 16))

            for s, name in enumerate(("c", "c_ctx")):
                sp.dma_start(cond[:, s, :], a[name]).then_inc(in_cond, 16)
            for e in range(2):
                weights(e, a["mod_w"][e], 4096)
            bias_rows(0, 0, 6)
            norm_rows(0)
            for r in range(2):
                sp.dma_start(mod_ctx[:, r * D:(r + 1) * D],
                             rows(a["mod_b"][0, r * D:(r + 1) * D])).then_inc(in_modb, 16)
            sp.dma_start(x_ctx, a["ctx"].rearrange("(t p) d -> p t d", p=P)).then_inc(in_ctx, 16)
            sp.dma_start(x_res[:, :, :], a["x"].rearrange("(t p) d -> p t d", p=P)).then_inc(in_x, 16)
            with n.loop(sp, MOD_BLOCKS // 2 - 1, {w_full[0]: 16, w_full[1]: 16}, {w_free: 2}) as i:
                for e in range(2):
                    weights(e, a["mod_w"][i * 2 + (2 + e)], 4096)
            sp.dma_start(c_row[:, :], rows(a["c_row"])).then_inc(in_crow, 16)
            for dst, src in ((cw[:, :], a["conv_w"]), (cbias[:, :], a["conv_b"]), (nwcol[:, :], a["ssd_norm_w"]),
                             (alr[:, :], rows(a["a_log"])), (dtb[:, :], rows(a["dt_bias"])),
                             (dcol[0:HD, :], a["ssd_d"][0].unsqueeze(0).to_broadcast([HD, CI])),
                             (dcol[HD:P, :], a["ssd_d"][1].unsqueeze(0).to_broadcast([HD, CI]))):
                sp.dma_start(dst, src).then_inc(in_small, 16)
            weights(0, a["dt_w"], KD * 2 * HEADS)
            weights(1, a["dt_w"], KD * 2 * HEADS)
            with n.loop(sp, GROUPS, {w_full[0]: 16, w_full[1]: 16, **{s: 8 * MOD_PER for s in mw_full}},
                        {w_free: 2, mw_free: MOD_PER}) as g:
                weights(0, a["xbc_w"][g], 4096)
                mod_columns(g, 0, 2)
                weights(1, a["z_w"][g], 2048)
                mod_columns(g, 2, MOD_PER)
            sp.wait_ge(mw_free, n.take(mw_free, 2))
            for m in range(4):
                weights(m % 2, a["out_w"][m], 4096)

            def store(t):
                sp.wait_ge(x_ready, n.take(x_ready))
                sp.dma_start(out[t * P:(t + 1) * P, :], h_tok[:, t, :]).then_inc(stored, n.post(stored, 16))

            def peer_loads(layer):
                for m in range(2):
                    weights(m, a["q_w"][layer, m], 4096)
                meet(sp, n, [])
                sp.dma_start(keys, a["keys"][layer]).then_inc(in_keys, 16)
                for m in (2, 3, 0, 1):
                    weights(m % 2, a["q_w"][layer, m], 4096)
                sp.wait_ge(u_used, n.take(u_used))
                if layer == 0:
                    bias_rows(1, 0, 5)
                    norm_rows(1)
                    sp.dma_start(pool_w, a["pool_w"]).then_inc(in_poolw, 16)
                    for m in range(2):
                        weights(m, a["pool_m"][m], 4096)
                else:
                    sp.dma_start(nw_row[:, 0:D], rows(a["final_norm_w"])).then_inc(in_fin, 16)
                    for t in range(LAT - 1):
                        store(t)
                meet(sp, n, [])

            peer_loads(0)
            if layers == 2:
                bias_rows(1, 5, 6)
                sp.dma_start(y_tmp, rows(a["pool_scale"])).then_inc(in_row, 16)
                peer_loads(1)
            store(LAT - 1)
            sp.wait_ge(stored, n.own(stored))

        @block.gpsimd
        def _(pool):
            n = Counts()
            g_ = nc.gpsimd

            def link(ins):
                ins.then_inc(pool_step, n.post(pool_step))
                pool.wait_ge(pool_step, n.own(pool_step))

            link(g_.memset(ones[:, :], 1.0))
            link(g_.memset(eps[:, :], EPS))
            link(g_.memset(zeros[:, :], 0.0))
            for dst, op, step in ((ident, ALU.is_equal, 1), (mask_le, ALU.is_ge, 1), (mask_ge, ALU.is_ge, -1),
                                  (mask_lt, ALU.is_gt, 1), (mask_gt, ALU.is_gt, -1)):
                ins = g_.affine_select(out=dst[:, :], in_=ones[:, :], compare_op=op, fill=0.0, base=0,
                                       pattern=[[step, P]], channel_multiplier=-step)
                link(ins)
            link(g_.memset(pre_l[:, :, :], 0.0))
            g_.memset(pre_c[:, :, :], 0.0).then_inc(masks_ready, n.post(masks_ready))
            pool.wait_ge(masks_ready, 1)

            pool.wait_ge(dec_ready, n.take(dec_ready))
            with n.loop(pool, GROUPS, {xd_ready: 10, r_ready: 2 * LAT, t1_ready: LAT},
                        {tok_ready: TT, pe_group: 1, dve_group: 1, dee_ps: 2 * LAT, m_ready: LAT}) as g:
                pool.wait_ge(pe_group, n.take(pe_group))
                pool.wait_ge(dve_group, n.take(dve_group))

                def spread(c):
                    if c > 0:
                        pool.wait_ge(dee_ps, n.take(dee_ps, 2))
                    for w, mask in ((0, mask_le), (1, mask_ge)):
                        g_.tensor_tensor(out=r1[:, w, :, :],
                                         in0=bc(av[:, CTX + c, bass.ds(g * HPG + w * HEADS, HPG)], P),
                                         in1=rep(mask[:, :], HPG), op=ALU.mult).then_inc(r_ready, n.post(r_ready))
                    if c > 0:
                        pool.wait_ge(m_ready, n.take(m_ready))
                    g_.tensor_tensor(out=t1, in0=bc(dtv[:, CTX + c, bass.ds(g * HPG, HPG)], P),
                                     in1=rep(mask_le[:, :], HPG), op=ALU.mult).then_inc(t1_ready, n.post(t1_ready))

                spread(0)
                for s in range(5):
                    for w, tile in ((0, F_TILES[s]), (1, B_TILES[s])):
                        if s == 0 and w == 0:
                            pool.wait_ge(tok_ready, n.take(tok_ready, TT))
                        g_.tensor_tensor(
                            out=xd[:, s, w, :].rearrange("p (h d) -> p h d", h=HPG),
                            in0=tok[:, tile, 0:2 * P].rearrange("p (h d) -> p h d", h=HPG),
                            in1=bc(wd[:, tile, bass.ds(g * HPG + w * HEADS, HPG)], HD),
                            op=ALU.mult).then_inc(xd_ready, n.post(xd_ready))
                for c in range(1, LAT):
                    spread(c)
                pool.wait_ge(dee_ps, n.take(dee_ps, 2))
                pool.wait_ge(m_ready, n.take(m_ready))
            meet(pool, n, [xd_ready, r_ready, t1_ready])

            def gather(table, col, buf, full, free, ahead):
                pool.wait_ge(free, n.take(free, 1, ahead))
                pool.sem_inc(st_go, 1)
                pool.indirect_dma_start(buf, None, table, bass.IndirectOffsetOnAxis(col, 0)).then_inc(
                    full, n.post(full, 16))

            def gathers(chunk):
                do_u, do_v = chunk < CHUNKS, chunk > 0
                posts = {pool_step: 4 if do_u and do_v else 2}
                takes = {}
                if do_u:
                    posts.update({s: 32 for s in u_full})
                    takes[u_free] = 2 * RING
                if do_v:
                    posts.update({s: 32 for s in v_full})
                    takes[v_done] = 2 * RING
                with n.loop(pool, BATCHES // 2, posts, takes) as i:
                    for e in range(2):
                        if do_u:
                            link(g_.tensor_copy(
                                stage[:, e, :], ids[:, bass.ds(i * (2 * RING) + (chunk * CSEL + e * RING), RING)]))
                        if do_v:
                            link(g_.tensor_copy(
                                stage[:, 2 + e, :],
                                ids[:, bass.ds(i * (2 * RING) + ((chunk - 1) * CSEL + e * RING), RING)]))
                        for j in range(RING):
                            if do_u:
                                gather(a["u"], stage[:, e, j:j + 1], u_buf[j], u_full[j], u_free, 0)
                            if do_v:
                                gather(a["v"], stage[:, 2 + e, j:j + 1], v_buf[j], v_full[j], v_done, 0)

            def peer():
                for chunk in range(CHUNKS + 1):
                    if chunk < CHUNKS:
                        pool.wait_ge(idx_ready, n.take(idx_ready))
                    if chunk == 1:
                        pool.wait_ge(scored, n.take(scored))
                    gathers(chunk)
                meet(pool, n, [])

            peer()
            if layers == 2:
                meet(pool, n, [])
                peer()

        @block.scalar
        def _(act):
            n = Counts()
            s_ = nc.scalar

            def link(ins):
                ins.then_inc(act_step, n.post(act_step))
                act.wait_ge(act_step, n.own(act_step))

            act.sem_inc(pj_ev, n.post(pj_ev, 3))
            act.wait_ge(in_cond, 32)
            s_.activation(cond[:, :, :], cond[:, :, :], ACT.Silu).then_inc(cond_ready, n.post(cond_ready))
            act.wait_ge(masks_ready, 1)

            def diagonals(rounds, first):
                with n.loop(act, rounds, {row_dg: 8}, {row_ps: 2}) as i:
                    for j in range(8):
                        if j % 4 == 0:
                            act.wait_ge(row_ps, n.take(row_ps))
                        s_.activation(diag[:, j, :], ident[:, :], ACT.Copy,
                                      scale=mod_col[:, bass.ds(i * 8 + (4 * first + j), 1)]).then_inc(
                            row_dg, n.post(row_dg))

            def norms(tiles, ready=None, first=0):
                last = first + len(tiles)
                for c, (src, dump) in enumerate(tiles, first):
                    if ready is not None:
                        act.wait_ge(ready, n.take(ready))
                    link(s_.activation(dump, src, ACT.Square, accum_out=ssq[:, c:c + 1]))
                s_.activation(rms[:, first:last], ssq[:, first:last], ACT.Sqrt, bias=eps[:, 0:1],
                              scale=1.0 / D).then_inc(rms_ready, n.post(rms_ready))

            def residual_norms():
                norms([(x_res[:, t, :].rearrange("p (a b) -> p a b", a=4), h_t[:, 0:4, SEQ:TT * P])
                       for t in range(LAT)], res_ready)

            def transposed(lo, hi):
                for t in range(lo, hi):
                    for b in range(2):
                        act.wait_ge(tr_ps, n.take(tr_ps))
                        s_.copy(h_t[:, b * 4:(b + 1) * 4, t * P:(t + 1) * P],
                                psum[:, b, :].rearrange("p (k t) -> p k t", k=4)).then_inc(ht_ready, n.post(ht_ready))

            act.wait_ge(in_ctx, 16)
            act.wait_ge(in_x, 16)
            norms([(x_ctx[:, t, :], h_tok[:, CTX, :]) for t in range(CTX)] +
                  [(x_res[:, t, :], h_tok[:, CTX, :]) for t in range(LAT)])
            transposed(0, TT)
            act.wait_ge(in_crow, 16)
            s_.activation(c_row[:, :], c_row[:, :], ACT.Silu).then_inc(crow_ready, n.post(crow_ready))
            act.wait_ge(in_small, 7 * 16)
            link(s_.activation(alr[:, :], alr[:, :], ACT.Exp))
            act.wait_ge(dt_abs, n.take(dt_abs))
            s_.activation(dt_u, dt_u, ACT.Exp, scale=-1.0).then_inc(dt_exp, n.post(dt_exp))
            act.wait_ge(seg_ps, n.take(seg_ps))
            link(s_.activation(ea[:, :, :], psum[:, 1, 0:n384].rearrange("p (t h) -> p t h", t=TT), ACT.Exp))
            for w in range(2):
                ins = s_.activation(wd[:, :, w * HEADS:(w + 1) * HEADS],
                                    psum[:, 2 + w, 0:n384 // 2].rearrange("p (t h) -> p t h", t=TT), ACT.Exp)
                if w == 0:
                    link(ins)
            ins.then_inc(seg_exp, n.post(seg_exp))

            with n.loop(act, GROUPS, {avb_ready: 2 * LAT, pj_ev: NU, xs_ready: CONVS, tok_ready: TT,
                                      e_ready: 2 * LAT, sq_ready: 1, act_step: 1, yn_ready: 1},
                        {pj_ps: NU, conv_done: CONVS, tok_ps: TT, st_done: 1, dee_ps: 2 * LAT, m_ready: LAT, y_ev: LAT,
                         yz_ready: 1, dve_group: 1}) as g:
                def evacuate(unit):
                    kind, col = UNITS[unit]
                    act.wait_ge(pj_ps, n.take(pj_ps))
                    bank = UNIT_BANKS[unit]
                    if kind == "ctx":
                        src, dst = psum[:, bank, 0:CTX_LEN], pre_c[:, col, HALO:HALO + CTX_LEN]
                    elif kind == "lat":
                        src, dst = psum[:, bank, :], pre_l[:, col, HALO:HALO + SEQ]
                    else:
                        src = psum[:, bank, 0:2 * P]
                        dst = z_t[:, col // 2, col % 2 * 2 * P:(col % 2 + 1) * 2 * P]
                    s_.activation(dst, src, ACT.Silu if kind == "z" else ACT.Copy).then_inc(pj_ev, n.post(pj_ev))

                def silu(unit):
                    kind, col = UNITS[unit]
                    act.wait_ge(conv_done, n.take(conv_done))
                    buf = cv_c[:, col, :] if kind == "ctx" else cv_l[:, col, :]
                    s_.activation(buf, buf, ACT.Silu).then_inc(xs_ready, n.post(xs_ready))

                def widen(c):
                    for w in range(2):
                        s_.copy(avb[:, w, :].rearrange("p (h d) -> p h d", h=HPG),
                                bc(av[:, CTX + c, bass.ds(g * HPG + w * HEADS, HPG)], HD)).then_inc(
                            avb_ready, n.post(avb_ready))

                widen(0)
                evacuate(0)
                evacuate(1)
                for k in range(2, CONVS):
                    evacuate(k)
                    silu(k - 2)
                silu(CONVS - 2)
                for t in range(TT):
                    act.wait_ge(tok_ps, n.take(tok_ps))
                    s_.copy(tok[:, t, :], psum[:, 6 + t % 2, 0:3 * P]).then_inc(tok_ready, n.post(tok_ready))
                silu(CONVS - 1)
                act.wait_ge(dve_group, n.take(dve_group))
                evacuate(7)
                evacuate(8)
                for c in range(LAT):
                    for w in range(2):
                        if c == 0 and w == 1:
                            act.wait_ge(st_done, n.take(st_done))
                        act.wait_ge(dee_ps, n.take(dee_ps))
                        if c > 0 and w == 0:
                            act.wait_ge(m_ready, n.take(m_ready))
                        if c > 1 and w == 1:
                            act.wait_ge(y_ev, n.take(y_ev))
                        if w == 0:
                            ins = s_.activation(e_mat, psum[:, 3, :].rearrange("p (h l) -> p h l", h=HPG), ACT.Exp)
                        else:
                            ins = s_.activation(ef[:, c % 2, :], psum[:, 4, :], ACT.Exp)
                        ins.then_inc(e_ready, n.post(e_ready))
                        if c == 0 and w == 0:
                            evacuate(9)
                    if c < LAT - 1:
                        widen(c + 1)
                evacuate(10)
                act.wait_ge(m_ready, n.take(m_ready))
                act.wait_ge(y_ev, n.take(y_ev, 2))
                act.wait_ge(yz_ready, n.take(yz_ready))
                s_.activation(z_t[:, :, :], y_t[:, bass.ds(g * 2, 2), :], ACT.Square).then_inc(
                    sq_ready, n.post(sq_ready))
                act.wait_ge(sq_ready, n.own(sq_ready))
                for j in range(2):
                    ins = s_.activation(y_t[:, bass.ds(g * 2 + j, 1), :], y_t[:, bass.ds(g * 2 + j, 1), :], ACT.Copy,
                                        scale=nwcol[:, bass.ds(g * 2 + j, 1)])
                    if j == 0:
                        ins.then_inc(act_step, n.post(act_step))
                ins.then_inc(yn_ready, n.post(yn_ready))
            act.wait_ge(ysq_ps, n.take(ysq_ps))
            s_.activation(rms[:, 0:LAT], psum[:, 0, 0:LAT], ACT.Sqrt, bias=eps[:, 0:1],
                          scale=1.0 / INNER).then_inc(ysq_rt, n.post(ysq_rt))
            residual_norms()
            meet(act, n, [ysq_rt, rms_ready])

            def peer(layer):
                transposed(0, 1)

                def q_copy(s):
                    act.wait_ge(q_ps, n.take(q_ps))
                    s_.copy(q_t[:, s % 2, 0:3 * P], psum[:, 2 + s % 2, 0:3 * P]).then_inc(qt_ready, n.post(qt_ready))

                def s_copy(i, s):
                    act.wait_ge(s_ps, n.take(s_ps))
                    row = HALVES[i] * 8 + s
                    s_.copy(scores[:, :, row * NKEY:(row + 1) * NKEY],
                            psum[:, 4 + s % 2, 0:3 * P].rearrange("p (t k) -> p t k", t=3)).then_inc(
                        s_ev, n.post(s_ev))

                for m in range(4):
                    act.wait_ge(q_ps, n.take(q_ps))
                    s_.copy(q_0[:, m % 2, :], psum[:, 2 + m % 2, :]).then_inc(qt_ready, n.post(qt_ready))
                    act.wait_ge(s_ps, n.take(s_ps))
                    s_.copy(work[:, m * 512:(m + 1) * 512], psum[:, 4 + m % 2, :]).then_inc(s_ev, n.post(s_ev))
                transposed(1, LAT)

                for i in range(2):
                    q_copy(0)
                    for s in range(1, 8):
                        if s >= 2:
                            s_copy(i, s - 2)
                        q_copy(s)
                    s_copy(i, 6)
                    s_copy(i, 7)

                def exps():
                    act.wait_ge(ex_in, n.take(ex_in))
                    s_.activation(soft_e[:, :, :], soft[:, :, :], ACT.Exp).then_inc(ex_ready, n.post(ex_ready))

                def gelus():
                    act.wait_ge(a_dots, n.take(a_dots))
                    s_.activation(gelu[:, :], dots[:, :], ACT.Gelu_apprx_tanh).then_inc(gelu_ready, n.post(gelu_ready))

                def diags(chunk):
                    act.wait_ge(w_ready, n.take(w_ready))
                    with n.loop(act, BATCHES, {dg_ready: RING}, {v_done: RING}) as b:
                        for j in range(RING):
                            act.wait_ge(v_done, n.take(v_done))
                            s_.activation(diag[:, j, :], ident[:, :], ACT.Copy,
                                          scale=wts[:, bass.ds(b * RING + (chunk * CSEL + j), 1)]).then_inc(
                                dg_ready, n.post(dg_ready))

                exps()
                for chunk in range(CHUNKS):
                    if chunk > 0:
                        diags(chunk - 1)
                    gelus()
                    if chunk < CHUNKS - 1:
                        exps()
                norms([(x_res[:, t, :], scr[:, 0:D]) for t in range(LAT - 1)], res_ready)
                diags(CHUNKS - 1)
                norms([(x_res[:, LAT - 1, :], scr[:, 0:D])], res_ready, LAT - 1)
                meet(act, n, [dg_ready, rms_ready])

            peer(0)
            if layers == 2:
                diagonals(6, 0)
                for k in range(KD):
                    act.wait_ge(pl_ps, n.take(pl_ps))
                    s_.copy(h_t[:, k, 0:SEQ], psum[:, 4 + k % 4, :]).then_inc(pl_ev, n.post(pl_ev))
                residual_norms()
                meet(act, n, [pl_ev, rms_ready])
                peer(1)

        @block.tensor
        def _(pe):
            n = Counts()
            mm = nc.tensor.matmul

            pe.sem_inc(w_free, n.post(w_free, 2))
            pe.sem_inc(v_done, n.post(v_done, RING))
            pe.sem_inc(row_ps, n.post(row_ps, 2))
            pe.sem_inc(pe_group, n.post(pe_group))
            pe.wait_ge(masks_ready, 1)
            pe.wait_ge(rep_ready, 1)

            def product(dst, lhs, rhs, k):
                for j in range(k):
                    ins = mm(dst, lhs(j), rhs(j), start=(j == 0), stop=(j == k - 1))
                return ins

            def mod_blocks(pairs, both):
                per, shared = (4, 2) if both else (2, 1)
                with n.loop(pe, pairs, {mod_ps: per, w_free: 2},
                            {mod_ev: per, mod_acc_ready: shared, w_full[0]: 16, w_full[1]: 16}) as i:
                    for e in range(2):
                        w = wbuf[:, e, :].rearrange("p (k m) -> p k m", k=KD)
                        pe.wait_ge(w_full[e], n.take(w_full[e], 16))
                        if both or e == 0:
                            pe.wait_ge(mod_ev, n.take(mod_ev))
                            product(psum[:, 2 * e, :], lambda k: cond_rep[:, k, :], lambda k: w[:, k, :],
                                    KD).then_inc(mod_ps, n.post(mod_ps))
                        if both or e == 1:
                            pe.wait_ge(mod_ev, n.take(mod_ev))
                            pe.wait_ge(mod_acc_ready, n.take(mod_acc_ready))
                            mm(psum[:, 2 * e + 1, :], ones[:, :], mod_acc[:, e, 0:512], start=True,
                               stop=True).then_inc(mod_ps, n.post(mod_ps))
                        pe.wait_ge(mod_ps, n.own(mod_ps))
                        pe.sem_inc(w_free, n.post(w_free))

            def transposes(lo, hi):
                for t in range(lo, hi):
                    pe.wait_ge(h_ready, n.take(h_ready))
                    for b in range(2):
                        if t > lo:
                            pe.wait_ge(ht_ready, n.take(ht_ready))
                        for k in range(4):
                            ins = nc.tensor.transpose(psum[:, b, k * P:(k + 1) * P],
                                                      h_tok[:, t, (b * 4 + k) * P:(b * 4 + k + 1) * P], ident[:, :])
                        ins.then_inc(tr_ps, n.post(tr_ps))
                pe.wait_ge(ht_ready, n.take(ht_ready, 2))

            mod_blocks(2, True)
            mod_blocks(4, False)
            transposes(0, TT)

            wdt = wbuf[:, 0, 0:KD * 2 * HEADS].rearrange("p (k m) -> p k m", k=KD)
            pe.wait_ge(w_full[0], n.take(w_full[0], 16))
            for t in range(TT):
                ins = product(psum[:, 2, t * 2 * HEADS:(t + 1) * 2 * HEADS],
                              lambda k: h_t[:, k, t * P:(t + 1) * P], lambda k: wdt[:, k, :], KD)
            ins.then_inc(dt_ps, n.post(dt_ps))
            pe.wait_ge(w_full[1], n.take(w_full[1], 16))
            pe.wait_ge(dt_ps, n.own(dt_ps))
            pe.sem_inc(w_free, n.post(w_free, 2))
            pe.wait_ge(a_ready, n.take(a_ready))
            mm(psum[:, 1, 0:n384], ones[:, :], av[:, :, :], start=True, stop=True)
            mm(psum[:, 2, 0:n384 // 2], mask_gt[:, :], av[:, :, 0:HEADS], start=True, stop=True)
            mm(psum[:, 3, 0:n384 // 2], mask_lt[:, :], av[:, :, HEADS:2 * HEADS], start=True,
               stop=True).then_inc(seg_ps, n.post(seg_ps))
            pe.wait_ge(seg_exp, n.take(seg_exp))

            with n.loop(pe, GROUPS,
                        {pj_ps: NU, w_free: 2, tok_ps: TT, st_ps: 1, dee_ps: 2 * LAT, cb_ps: LAT, y_ps: LAT,
                         pe_group: 1},
                        {w_full[0]: 16, w_full[1]: 16, pj_ev: NU, xs_ready: CONVS, tok_ready: TT, xd_ready: 10,
                         st_done: 1, avb_ready: 2 * LAT, r_ready: 2 * LAT, e_ready: 2 * LAT, m_ready: LAT,
                         y_ev: LAT}) as g:
                wx = wbuf[:, 0, :].rearrange("p (k m) -> p k m", k=KD)
                wz = wbuf[:, 1, 0:2048].rearrange("p (k m) -> p k m", k=KD)

                def project(unit):
                    kind, col = UNITS[unit]
                    lo, hi = (0, CTX_LEN) if kind == "ctx" else (CTX_LEN, TT * P)
                    if kind == "z":
                        lo, hi, col = CTX_LEN + col % 2 * 2 * P, CTX_LEN + (col % 2 + 1) * 2 * P, col // 2
                    if unit == 0:
                        pe.wait_ge(w_full[0], n.take(w_full[0], 16))
                    if unit == 7:
                        pe.wait_ge(pj_ps, n.own(pj_ps))
                        pe.sem_inc(w_free, n.post(w_free))
                        pe.wait_ge(w_full[1], n.take(w_full[1], 16))
                    pe.wait_ge(pj_ev, n.take(pj_ev, 1, 0 if unit else 2))
                    w = wz if kind == "z" else wx
                    ins = product(psum[:, UNIT_BANKS[unit], 0:hi - lo], lambda j: w[:, j, col * P:(col + 1) * P],
                                  lambda j: h_t[:, j, lo:hi], KD)
                    ins.then_inc(pj_ps, n.post(pj_ps))

                for unit in range(CONVS):
                    project(unit)
                for t in range(TT):
                    if t == 0:
                        pe.wait_ge(xs_ready, n.take(xs_ready, CONVS - 1))
                    if t >= 2:
                        pe.wait_ge(tok_ready, n.take(tok_ready))
                    for j in range(3):
                        src = cv_c[:, j, t * P:(t + 1) * P] if t < CTX else cv_l[:, j, (t - CTX) * P:(t - CTX + 1) * P]
                        ins = nc.tensor.transpose(psum[:, 6 + t % 2, j * P:(j + 1) * P], src, ident[:, :])
                    ins.then_inc(tok_ps, n.post(tok_ps))
                project(7)
                project(8)
                pe.wait_ge(tok_ready, n.take(tok_ready, 2))
                pe.wait_ge(pj_ev, n.take(pj_ev, 0, 3))
                for s in range(5):
                    for w, tile in ((0, F_TILES[s]), (1, B_TILES[s])):
                        pe.wait_ge(xd_ready, n.take(xd_ready))
                        ins = mm(psum[:, ST_BANKS[s], w * 256:(w + 1) * 256], tok[:, tile, 2 * P:3 * P], xd[:, s, w, :],
                                 start=True, stop=True)
                ins.then_inc(st_ps, n.post(st_ps))

                def decays(c):
                    pe.wait_ge(r_ready, n.take(r_ready, 2))
                    if c == 1:
                        pe.wait_ge(pj_ev, n.take(pj_ev, 0, 3))
                    if c > 0:
                        pe.wait_ge(e_ready, n.take(e_ready, 2))
                    mm(psum[:, 3, :], mask_gt[:, :], r1[:, 0, :, :], start=True, stop=False)
                    mm(psum[:, 3, :], mask_lt[:, :], r1[:, 1, :, :], start=False, stop=True).then_inc(
                        dee_ps, n.post(dee_ps))
                    if c == 0:
                        project(9)
                    pe.wait_ge(avb_ready, n.take(avb_ready, 2))
                    for w, mask in ((0, mask_le), (1, mask_ge)):
                        for pair in range(2):
                            o = (w * 2 + pair) * P
                            ins = mm(psum[:, 4, o:o + P], avb[:, w, pair * P:(pair + 1) * P], mask[:, :],
                                     start=True, stop=True)
                    ins.then_inc(dee_ps, n.post(dee_ps))
                    if c == 0:
                        pe.wait_ge(st_done, n.take(st_done))
                        pe.wait_ge(xs_ready, n.take(xs_ready))
                    mm(psum[:, (7, 2)[c % 2], 0:P], cv_l[:, 2, c * P:(c + 1) * P], cv_l[:, 3, c * P:(c + 1) * P],
                       start=True, stop=True).then_inc(cb_ps, n.post(cb_ps))

                def outputs(c):
                    if c == 2:
                        pe.wait_ge(y_ev, n.take(y_ev))
                    if c == LAT - 1:
                        pe.wait_ge(pj_ev, n.take(pj_ev, 0, 3))
                    for w in range(2):
                        for pair in range(2):
                            o = (w * 2 + pair) * P
                            mm(psum[:, (5, 0)[c % 2], o:o + P], s_in[:, w, c, pair * P:(pair + 1) * P],
                               cv_l[:, 3, c * P:(c + 1) * P], start=True, stop=True)
                    pe.wait_ge(m_ready, n.take(m_ready))
                    for r in range(HPG):
                        half, pair = r % 2, r // 2
                        ins = mm(psum[half * HD:(half + 1) * HD, (6, 1)[c % 2], pair * P:(pair + 1) * P],
                                 tok[:, CTX + c, r * HD:(r + 1) * HD], m_mat[:, c % 2, r, :], start=True, stop=True)
                    ins.then_inc(y_ps, n.post(y_ps))

                decays(0)
                for c in range(1, LAT):
                    decays(c)
                    outputs(c - 1)
                pe.wait_ge(y_ev, n.take(y_ev))
                project(10)
                pe.wait_ge(pj_ps, n.own(pj_ps))
                pe.sem_inc(w_free, n.post(w_free))
                outputs(LAT - 1)
                pe.wait_ge(e_ready, n.take(e_ready, 2))
                pe.wait_ge(y_ev, n.take(y_ev, 2))
                pe.wait_ge(y_ps, n.own(y_ps))
                pe.sem_inc(pe_group, n.post(pe_group))

            pe.wait_ge(dve_group, GROUPS + 1)
            pe.wait_ge(yn_ready, GROUPS)
            for t in range(LAT):
                ins = mm(psum[:, 0, t:t + 1], sqacc[:, t * P:(t + 1) * P], ones[:, 0:1], start=True, stop=True)
            ins.then_inc(ysq_ps, n.post(ysq_ps))
            pe.wait_ge(ysq_rt, 1)
            for m in range(4):
                w = wbuf[:, m % 2, :].rearrange("p (k d) -> p k d", k=4)
                pe.wait_ge(w_full[m % 2], n.take(w_full[m % 2], 16))
                order = [(k, t) for k in range(4) for t in range(LAT)]
                if m == 3:
                    order.sort(key=lambda kt: kt[1])
                for k, t in order:
                    for h in range(2):
                        ins = mm(psum[:, 2 * t + h, :], y_t[:, 4 * m + k, t * P:(t + 1) * P],
                                 w[:, k, h * 512:(h + 1) * 512], start=(m + k == 0), stop=(m == 3 and k == 3))
                    if m == 3 and k == 3:
                        ins.then_inc(op_ps, n.post(op_ps))
                if m < 3:
                    ins.then_inc(w_free, n.post(w_free))
                else:
                    pe.wait_ge(op_ps, n.own(op_ps))
                    pe.sem_inc(w_free, n.post(w_free))
            meet(pe, n, [op_ps])

            def peer(layer):
                transposes(0, 1)
                pe.wait_ge(in_keys, n.take(in_keys, 16))

                def queries(e, s):
                    w = wbuf[:, e, :].rearrange("p (k m) -> p k m", k=KD)
                    ins = product(psum[:, 2 + s % 2, 0:3 * P], lambda k: w[:, k, (s % 4) * P:(s % 4 + 1) * P],
                                  lambda k: h_t[:, k, P:SEQ], KD)
                    ins.then_inc(q_ps, n.post(q_ps))
                    if s % 4 == 3:
                        pe.wait_ge(q_ps, n.own(q_ps))
                        pe.sem_inc(w_free, n.post(w_free))

                def key_scores(i, s):
                    pe.wait_ge(qt_ready, n.take(qt_ready))
                    if s >= 2:
                        pe.wait_ge(s_ev, n.take(s_ev))
                    for t in range(LAT - 1):
                        ins = mm(psum[:, 4 + s % 2, t * P:(t + 1) * P], q_t[:, s % 2, t * P:(t + 1) * P],
                                 keys[:, (HALVES[i] * 8 + s) * NKEY:(HALVES[i] * 8 + s + 1) * NKEY],
                                 start=True, stop=True)
                    ins.then_inc(s_ps, n.post(s_ps))

                def first_queries(m):
                    w = wbuf[:, m % 2, :].rearrange("p (k m) -> p k m", k=KD)
                    pe.wait_ge(w_full[m % 2], n.take(w_full[m % 2], 16))
                    for s in range(4):
                        ins = product(psum[:, 2 + m % 2, s * P:(s + 1) * P], lambda k: w[:, k, s * P:(s + 1) * P],
                                      lambda k: h_t[:, k, 0:P], KD)
                    ins.then_inc(q_ps, n.post(q_ps))
                    if m < 2:
                        pe.wait_ge(q_ps, n.own(q_ps))
                        pe.sem_inc(w_free, n.post(w_free))

                def first_scores(m):
                    pe.wait_ge(qt_ready, n.take(qt_ready))
                    if m >= 2:
                        pe.wait_ge(s_ev, n.take(s_ev))
                    for s in range(4):
                        ins = mm(psum[:, 4 + m % 2, s * P:(s + 1) * P], q_0[:, m % 2, s * P:(s + 1) * P],
                                 keys[:, (4 * m + s) * NKEY:(4 * m + s + 1) * NKEY], start=True, stop=True)
                    ins.then_inc(s_ps, n.post(s_ps))

                for m in range(4):
                    first_queries(m)
                    first_scores(m)
                transposes(1, LAT)
                pe.wait_ge(s_ev, n.take(s_ev, 2))
                for i in range(2):
                    for s in range(8):
                        if i == 1 and s % 4 == 0:
                            pe.wait_ge(w_full[s // 4], n.take(w_full[s // 4], 16))
                        queries(s // 4, s)
                        if s >= 1:
                            key_scores(i, s - 1)
                    key_scores(i, 7)
                    pe.wait_ge(s_ev, n.take(s_ev, 2))
                pe.sem_inc(scored, n.post(scored))
                for tile in range(LAT):
                    pe.wait_ge(y_free, n.take(y_free))
                    for h in range(2):
                        mm(psum[:, h, :], zeros[:, :], h_tok[:, 0, 0:512], start=True, stop=True, skip_group_check=True)
                    with n.loop(pe, 2 * BATCHES, {v_done: RING},
                                {dg_ready: RING, **{s: 16 for s in v_full}}) as b:
                        for j in range(RING):
                            pe.wait_ge(v_full[j], n.take(v_full[j], 16))
                            pe.wait_ge(dg_ready, n.take(dg_ready))
                            for h in range(2):
                                ins = mm(psum[:, h, :], diag[:, j, :], v_buf[j][:, h * 512:(h + 1) * 512],
                                         start=False, stop=True, skip_group_check=True)
                            ins.then_inc(v_done, n.post(v_done))
                meet(pe, n, [v_done])

            peer(0)
            if layers == 2:
                for b in range(MOD_BLOCKS):
                    pe.wait_ge(row_dg, n.take(row_dg, 4))
                    if b >= 8:
                        pe.wait_ge(row_ev, n.take(row_ev))
                    mm(psum[:, b % 8, :], ones[:, :], diag[:, b % 2 * 4:b % 2 * 4 + 4, :], start=True,
                       stop=True).then_inc(row_ps, n.post(row_ps))
                pe.wait_ge(h_ready, n.take(h_ready, LAT))
                for k in range(KD):
                    gidx, m = k // 2, k // 4
                    if k % 4 == 0:
                        pe.wait_ge(w_full[m], n.take(w_full[m], 16))
                    if k < 4:
                        pe.wait_ge(row_ev, n.take(row_ev))
                    else:
                        pe.wait_ge(pl_ev, n.take(pl_ev))
                    w = wbuf[:, m, :].rearrange("p (g t n) -> p g t n", g=2, t=LAT)
                    ins = product(psum[:, 4 + k % 4, :], lambda t: h_tok[:, t, k * P:(k + 1) * P],
                                  lambda t: w[:, gidx % 2, t, :], LAT)
                    ins.then_inc(pl_ps, n.post(pl_ps))
                    if k % 4 == 3:
                        pe.wait_ge(pl_ps, n.own(pl_ps))
                        pe.sem_inc(w_free, n.post(w_free))
                pe.wait_ge(pl_ev, n.take(pl_ev, 4))
                pe.wait_ge(row_ev, n.take(row_ev, 4))
                w = pool_w.rearrange("p (g c n) -> p g c n", g=PGROUPS, c=2)
                pe.wait_ge(in_poolw, 16)
                for t in range(LAT):
                    for gi in range(PGROUPS):
                        for c in range(2):
                            ins = mm(psum[:, 2 * t + gi // 2, (gi % 2) * 256:(gi % 2 + 1) * 256],
                                     h_t[:, 2 * gi + c, t * P:(t + 1) * P], w[:, gi, c, :],
                                     start=(c == 0), stop=(c == 1))
                    ins.then_inc(py_ps, n.post(py_ps))
                meet(pe, n, [py_ps])
                peer(1)

        @block.vector
        def _(dve):
            n = Counts()
            v_ = nc.vector

            def step(ins):
                ins.then_inc(dve_step, n.post(dve_step))

            def link(ins):
                step(ins)
                dve.wait_ge(dve_step, n.own(dve_step))

            def tt(o, i0, i1, op):
                return v_.tensor_tensor(out=o, in0=i0, in1=i1, op=op)

            def stt(o, i0, s, i1, op0, op1):
                return v_.scalar_tensor_tensor(out=o, in0=i0, scalar=s, in1=i1, op0=op0, op1=op1)

            dve.sem_inc(mod_ev, n.post(mod_ev, 2))
            dve.sem_inc(dve_group, n.post(dve_group))
            dve.sem_inc(u_free, n.post(u_free, RING))
            dve.sem_inc(y_free, n.post(y_free))
            dve.sem_inc(mw_free, n.post(mw_free, 2))

            def replicate():
                v_.tensor_copy(cond_rep, bc(cond[:, 0, :], P)).then_inc(rep_ready, n.post(rep_ready))
                dve.wait_ge(rep_ready, n.own(rep_ready))

            def mod_rows(pairs, first, both):
                per, shared = (4, 2) if both else (2, 1)

                def accumulate(e, s):
                    w = wbuf[:, e, :].rearrange("p (k m) -> p k m", k=KD)
                    acc = mod_acc[:, e, 0:512]
                    dve.wait_ge(w_full[e], n.take(w_full[e], 16))
                    link(v_.tensor_scalar(acc, w[:, 0, :], cond[:, s, 0:1], None, ALU.mult))
                    for k in range(1, KD):
                        ins = stt(acc, w[:, k, :], cond[:, s, k:k + 1], acc, ALU.mult, ALU.add)
                        if k < KD - 1:
                            link(ins)
                        else:
                            ins.then_inc(mod_acc_ready, n.post(mod_acc_ready))

                def add_block(i, e, s, bank):
                    dve.wait_ge(mod_ps, n.take(mod_ps))
                    to = (mod_ctx if s else mod_row)[:, bass.ds(i * 1024 + (first + e) * 512, 512)]
                    tt(to, to, psum[:, bank, :], ALU.add).then_inc(mod_ev, n.post(mod_ev))

                posts = {mod_ev: per, mod_acc_ready: shared, dve_step: shared * (KD - 1)}
                takes = {mod_ps: per, w_full[1]: 16}
                if both:
                    takes[w_full[0]] = 16
                with n.loop(dve, pairs, posts, takes) as i:
                    if both:
                        for e in range(2):
                            accumulate(e, 1)
                            add_block(i, e, 0, 2 * e)
                            add_block(i, e, 1, 2 * e + 1)
                    else:
                        accumulate(1, 0)
                        add_block(i, 0, 0, 0)
                        add_block(i, 1, 0, 3)
                dve.wait_ge(mod_ev, n.own(mod_ev))

            def row(r):
                return mod_row[:, r * D:(r + 1) * D]

            def scale_row(sub):
                r = row(1 + 3 * sub)
                link(stt(r, r, 1.0, nw_row[:, sub * D:(sub + 1) * D], ALU.add, ALU.mult))

            def modulated(tiles, signals=1):
                dve.wait_ge(rms_ready, n.take(rms_ready, signals))
                link(v_.reciprocal(rinv[:, 0:len(tiles)], rms[:, 0:len(tiles)]))
                for c, (src, arow, brow, dst) in enumerate(tiles):
                    link(stt(dst, src, rinv[:, c:c + 1], arow, ALU.mult, ALU.mult))
                    tt(dst, dst, brow, ALU.add).then_inc(h_ready, n.post(h_ready))

            dve.wait_ge(cond_ready, n.take(cond_ready))
            dve.wait_ge(masks_ready, 1)
            replicate()
            dve.wait_ge(in_modb, 8 * 16)
            mod_rows(2, 0, True)
            mod_rows(4, 4, False)
            dve.wait_ge(in_nw, 2 * 16)
            link(stt(mod_ctx[:, D:2 * D], mod_ctx[:, D:2 * D], 1.0, nw_row[:, 0:D], ALU.add, ALU.mult))
            scale_row(0)
            scale_row(1)
            modulated([(x_ctx[:, t, :], mod_ctx[:, D:2 * D], mod_ctx[:, 0:D], h_tok[:, t, :]) for t in range(CTX)] +
                      [(x_res[:, t, :], row(1), row(0), h_tok[:, CTX + t, :]) for t in range(LAT)])

            dve.wait_ge(in_small, 7 * 16)
            dve.wait_ge(dt_ps, n.take(dt_ps))
            dve.wait_ge(h_ready, n.own(h_ready))
            link(tt(dt_x, psum[:, 2, 0:n384].rearrange("p (t h) -> p t h", t=TT), rep(dtb[:, :], TT), ALU.add))
            stt(dt_u, dt_x, -1.0, dt_x, ALU.mult, ALU.max).then_inc(dt_abs, n.post(dt_abs))
            dve.wait_ge(dt_exp, n.take(dt_exp))
            link(v_.tensor_scalar(dt_z, dt_u, 2.0, None, ALU.add))
            link(v_.reciprocal(dt_q, dt_z))
            link(tt(dt_z, dt_u, dt_q, ALU.mult))
            link(tt(dt_u, dt_z, dt_z, ALU.mult))
            link(v_.tensor_scalar(dt_q, dt_u, 1.0 / (2 * SERIES + 1), None, ALU.mult))
            for k in range(SERIES - 1, 0, -1):
                link(stt(dt_q, dt_q, 1.0 / (2 * k + 1), dt_u, ALU.add, ALU.mult))
            link(stt(dt_q, dt_q, 1.0, dt_z, ALU.add, ALU.mult))
            link(v_.tensor_scalar(dt_x, dt_x, 0.0, None, ALU.max))
            link(stt(dtv[:, :, :], dt_q, 2.0, dt_x, ALU.mult, ALU.add))
            stt(av[:, :, :], dtv[:, :, :], -1.0, rep(alr[:, :], TT), ALU.mult, ALU.mult).then_inc(
                a_ready, n.post(a_ready))
            dve.wait_ge(seg_exp, n.take(seg_exp))
            link(v_.memset(sqacc[:, :], 0.0))
            tt(wd[:, :, :], wd[:, :, :], dtv[:, :, :], ALU.mult).then_inc(dec_ready, n.post(dec_ready))
            dve.wait_ge(dec_ready, n.own(dec_ready))

            dve.wait_ge(crow_ready, n.take(crow_ready))
            steps = CONVS * (TAPS - 1) + 17 + LAT * 9 + 2
            with n.loop(dve, GROUPS, {dve_step: steps, mw_free: MOD_PER, conv_done: CONVS, st_done: 1, m_ready: LAT,
                                      y_ev: LAT, yz_ready: 1, dve_group: 1},
                        {pj_ev: NU, pe_group: 1, st_ps: 1, t1_ready: LAT, e_ready: 2 * LAT, cb_ps: LAT,
                         y_ps: LAT, xs_ready: CONVS, sq_ready: 1, **{s: 8 * MOD_PER for s in mw_full}}) as g:

                def mod_column(k):
                    buf = mw_buf[k % 2]
                    dve.wait_ge(mw_full[k % 2], n.take(mw_full[k % 2], 16))
                    v_.tensor_tensor_reduce(out=buf, in0=buf, in1=c_row[:, :], scale=1.0, scalar=0.0, op0=ALU.mult,
                                            op1=ALU.add, accum_out=mod_six[:, k:k + 1]).then_inc(
                        mw_free, n.post(mw_free))

                dve.wait_ge(pe_group, n.take(pe_group))
                for k in range(MOD_PER // 2):
                    mod_column(k)
                for k in range(CONVS):
                    dve.wait_ge(pj_ev, n.take(pj_ev, 1, 3))
                    kind, j = UNITS[k]
                    width = CTX_LEN if kind == "ctx" else SEQ
                    src, dst = (pre_c, cv_c[:, j, :]) if kind == "ctx" else (pre_l, cv_l[:, j, :])

                    def weight(tap):
                        return cw[:, bass.ds(g * (4 * TAPS) + (j * TAPS + tap), 1)]

                    link(v_.tensor_scalar(dst, src[:, j, 0:width], weight(0), cbias[:, bass.ds(g * 4 + j, 1)],
                                           ALU.mult, ALU.add))
                    for tap in range(1, TAPS):
                        ins = stt(dst, src[:, j, tap:tap + width], weight(tap), dst, ALU.mult, ALU.add)
                        if tap < TAPS - 1:
                            link(ins)
                        else:
                            ins.then_inc(conv_done, n.post(conv_done))
                    if k < MOD_PER // 2:
                        mod_column(MOD_PER // 2 + k)
                dve.wait_ge(mw_free, n.own(mw_free))
                link(v_.tensor_copy(mod_col[:, bass.ds(g * MOD_PER, MOD_PER)], mod_six[:, :]))

                def triangles(c):
                    dve.wait_ge(t1_ready, n.take(t1_ready))
                    for r in range(HPG):
                        step(stt(tw[:, r, :], mask_ge[:, :], dtv[:, CTX + c, bass.ds(g * HPG + (HEADS + r), 1)],
                                 t1[:, r, :], ALU.mult, ALU.add))
                    dve.wait_ge(dve_step, n.own(dve_step))

                triangles(0)
                dve.wait_ge(st_ps, n.take(st_ps))
                where = {}
                for s in range(5):
                    for w, tile in ((0, F_TILES[s]), (1, B_TILES[s])):
                        new = psum[:, ST_BANKS[s], w * 256:(w + 1) * 256]
                        if s == 0:
                            dst = st_tmp[:, w, 0, :]
                            link(v_.tensor_copy(dst, new))
                        else:
                            dst = s_in[:, w, s - 1 if w == 0 else LAT - s, :]
                            old, mid = where[w], st_tmp[:, w, 1, :]
                            link(tt(mid.rearrange("p (h d) -> p h d", h=HPG),
                                     old.rearrange("p (h d) -> p h d", h=HPG),
                                     bc(ea[:, tile, bass.ds(g * HPG + w * HEADS, HPG)], HD), ALU.mult))
                            ins = tt(dst, mid, new, ALU.add)
                            if s == 4 and w == 1:
                                ins.then_inc(st_done, n.post(st_done))
                            else:
                                link(ins)
                        where[w] = dst
                dve.wait_ge(st_done, n.own(st_done))
                dve.wait_ge(xs_ready, n.take(xs_ready, CONVS))

                def prepare(c):
                    b = c % 2
                    if c > 0:
                        triangles(c)
                    dve.wait_ge(e_ready, n.take(e_ready, 2 if c else 1))
                    link(tt(m_mat[:, b, :, :], tw[:, :, :], e_mat, ALU.mult))
                    dve.wait_ge(cb_ps, n.take(cb_ps))
                    tt(m_mat[:, b, :, :], m_mat[:, b, :, :], rep(psum[:, (7, 2)[b], 0:P], HPG),
                       ALU.mult).then_inc(m_ready, n.post(m_ready))

                def finish(c):
                    if c == LAT - 1:
                        dve.wait_ge(e_ready, n.take(e_ready))
                    dve.wait_ge(y_ps, n.take(y_ps))
                    if c > 0:
                        dve.wait_ge(y_ev, n.own(y_ev))
                    step(tt(y_st, psum[:, (5, 0)[c % 2], :], ef[:, c % 2, :], ALU.mult))
                    for pair in range(2):
                        step(stt(y_t[:, bass.ds(g * 2 + pair, 1), c * P:(c + 1) * P].rearrange("p o t -> p (o t)"),
                                 cv_l[:, pair, c * P:(c + 1) * P],
                                 dcol[:, bass.ds(g * 2 + pair, 1)], psum[:, (6, 1)[c % 2], pair * P:(pair + 1) * P],
                                 ALU.mult, ALU.add))
                    dve.wait_ge(dve_step, n.own(dve_step))
                    y_c = y_t[:, bass.ds(g * 2, 2), c * P:(c + 1) * P]
                    for w in range(2):
                        share = y_st[:, w * 2 * P:(w + 1) * 2 * P].rearrange("p (o t) -> p o t", o=2)
                        ins = tt(y_c, y_c, share, ALU.add)
                        if w == 0:
                            link(ins)
                        else:
                            ins.then_inc(y_ev, n.post(y_ev))

                prepare(0)
                for c in range(1, LAT):
                    prepare(c)
                    finish(c - 1)
                finish(LAT - 1)
                dve.wait_ge(y_ev, n.own(y_ev))
                dve.wait_ge(pj_ev, n.take(pj_ev, NU - CONVS, 3))
                both = y_t[:, bass.ds(g * 2, 2), :]
                tt(both, both, z_t[:, :, :], ALU.mult).then_inc(yz_ready, n.post(yz_ready))
                dve.wait_ge(sq_ready, n.take(sq_ready))
                link(tt(sqacc[:, :], sqacc[:, :], z_t[:, 0, :], ALU.add))
                tt(sqacc[:, :], sqacc[:, :], z_t[:, 1, :], ALU.add).then_inc(dve_group, n.post(dve_group))
                dve.wait_ge(dve_group, n.own(dve_group))

            dve.wait_ge(ysq_rt, 1)
            link(v_.reciprocal(rinv[:, 0:LAT], rms[:, 0:LAT]))
            for t in range(LAT):
                dve.wait_ge(op_ps, n.take(op_ps))
                for h in range(2):
                    o = slice(h * 512, (h + 1) * 512)
                    step(stt(scr[:, o], psum[:, 2 * t + h, :], rinv[:, t:t + 1],
                             mod_row[:, 2 * D + h * 512:2 * D + (h + 1) * 512], ALU.mult, ALU.mult))
                dve.wait_ge(dve_step, n.own(dve_step))
                tt(x_res[:, t, :], x_res[:, t, :], scr[:, 0:D], ALU.add).then_inc(res_ready, n.post(res_ready))
                dve.wait_ge(res_ready, n.own(res_ready))
            meet(dve, n, [dve_step])

            def peer(layer):
                modulated([(x_res[:, t, :], row(4), row(3), h_tok[:, t, :]) for t in range(LAT)])
                dve.wait_ge(h_ready, n.own(h_ready))

                def load_scores(tile, lo, hi):
                    if tile == 1 and lo == 0:
                        dve.wait_ge(s_ev, n.take(s_ev, HH))
                    o = slice(lo * NKEY, hi * NKEY)
                    link(v_.tensor_copy(work[:, o], scores[:, tile - 1, o]))

                def top16(val, idx, src):
                    link(v_.max(val[:, 0:8], src))
                    link(v_.max_index(idx[:, 0:8], val[:, 0:8], src))
                    link(v_.match_replace(src, val[:, 0:8], src, LOWEST))
                    link(v_.max(val[:, 8:16], src))
                    link(v_.max_index(idx[:, 8:16], val[:, 8:16], src))

                def key_rows(lo, hi):
                    for r in range(lo, hi):
                        top16(top_v[:, r % CROWS, :], top_i[:, r % CROWS, :], work[:, r * NKEY:(r + 1) * NKEY])

                def pairs(chunk, h):
                    o = (chunk % 2 * CHEADS + h) * 2 * NKEY
                    return work[:, o:o + TOPK * TOPK]

                def candidates(chunk):
                    link(v_.tensor_copy(top_f[:, :, :], top_i[:, :, :]))
                    for h in range(CHEADS):
                        step(tt(pairs(chunk, h).rearrange("p (i j) -> p i j", i=TOPK),
                                bc(top_v[:, 2 * h, :], TOPK), rep(top_v[:, 2 * h + 1, :], TOPK), ALU.add))
                    dve.wait_ge(dve_step, n.own(dve_step))

                def best_rows(chunk, lo, hi):
                    for h in range(lo, hi):
                        top16(best[:, h, :], pos[:, h, :], pairs(chunk, h))

                def indices(chunk, which):
                    flat = pos[:, :, :].rearrange("p h k -> p (h k)")
                    if which == 0:
                        link(v_.tensor_scalar(part[:, 0, :], flat, 4, None, ALU.logical_shift_right))
                        link(v_.tensor_scalar(part[:, 1, :], flat, 15, None, ALU.bitwise_and))
                        link(v_.tensor_copy(part_f[:, :, :], part[:, :, :]))
                    link(tt(pick, bc(part_f[:, which, :], TOPK), rep(iota_i[:, :], CSEL), ALU.is_equal))
                    for h in range(CHEADS):
                        sl = pick[:, h * TOPK:(h + 1) * TOPK, :]
                        step(tt(sl, sl, rep(top_f[:, 2 * h + which, :], TOPK), ALU.mult))
                    dve.wait_ge(dve_step, n.own(dve_step))
                    link(v_.tensor_reduce(ids_f[:, which, :], pick, AX.X, ALU.add))
                    if which == 1:
                        link(stt(ids_f[:, 0, :], ids_f[:, 0, :], float(NKEY), ids_f[:, 1, :], ALU.mult, ALU.add))
                        v_.tensor_scalar(ids[:, chunk * CSEL:(chunk + 1) * CSEL], ids_f[:, 0, :],
                                         float(layer * NEXP), None, ALU.add).then_inc(idx_ready, n.post(idx_ready))
                        dve.wait_ge(idx_ready, n.own(idx_ready))

                def soft_in():
                    tt(soft[:, :, :], best[:, :, :], best[:, :, 0:1].to_broadcast([P, CHEADS, TOPK]),
                       ALU.subtract).then_inc(ex_in, n.post(ex_in))

                def soft_out():
                    dve.wait_ge(ex_ready, n.take(ex_ready))
                    link(v_.tensor_reduce(soft_s[:, 0, :], soft_e[:, :, :], AX.X, ALU.add))
                    link(v_.reciprocal(soft_s[:, 1, :], soft_s[:, 0, :]))
                    link(tt(gate[:, :].rearrange("p (h k) -> p h k", h=CHEADS), soft_e[:, :, :],
                            bc(soft_s[:, 1, :], TOPK), ALU.mult))

                def piece(chunk, b):
                    tile, row = chunk // 2, chunk % 2 * CROWS + 2 * b
                    if tile == 0 and b in (0, 2):
                        dve.wait_ge(s_ev, n.take(s_ev))
                    if b < 4:
                        if tile > 0:
                            load_scores(tile, row, row + 2)
                        key_rows(row, row + 2)
                    if b == 4:
                        candidates(chunk)
                        best_rows(chunk, 0, 1)
                    if b == 5:
                        best_rows(chunk, 1, 3)
                    if b == 6:
                        best_rows(chunk, 3, 4)
                        indices(chunk, 0)
                    if b == 7:
                        indices(chunk, 1)
                        soft_in()

                def add_experts(tile):
                    dve.wait_ge(v_done, n.take(v_done, SEL, RING))
                    for h in range(2):
                        o = slice(h * 512, (h + 1) * 512)
                        ins = tt(y_tmp[:, o], psum[:, h, :], mod_row[:, 5 * D + h * 512:5 * D + (h + 1) * 512],
                                 ALU.mult)
                        if h == 0:
                            link(ins)
                        else:
                            ins.then_inc(y_free, n.post(y_free))
                    dve.wait_ge(y_free, n.own(y_free))
                    tt(x_res[:, tile, :], x_res[:, tile, :], y_tmp, ALU.add).then_inc(res_ready, n.post(res_ready))
                    dve.wait_ge(res_ready, n.own(res_ready))

                def final(lo, hi):
                    dve.wait_ge(in_fin, 16)
                    dve.wait_ge(rms_ready, n.take(rms_ready))
                    link(v_.reciprocal(rinv[:, lo:hi], rms[:, lo:hi]))
                    for t in range(lo, hi):
                        stt(h_tok[:, t, :], x_res[:, t, :], rinv[:, t:t + 1], nw_row[:, 0:D], ALU.mult,
                            ALU.mult).then_inc(x_ready, n.post(x_ready))

                if layer == 0:
                    for k in range(TOPK):
                        link(v_.memset(iota_i[:, k:k + 1], float(k)))
                for b in range(BATCHES):
                    piece(0, b)
                for chunk in range(CHUNKS):
                    for b in range(BATCHES):
                        if b == BATCHES - 1:
                            soft_out()
                        if chunk < CHUNKS - 1:
                            piece(chunk + 1, b)
                        for j in range(RING):
                            col = b * RING + j
                            dve.wait_ge(u_full[j], n.take(u_full[j], 16))
                            v_.tensor_tensor_reduce(out=u_buf[j], in0=u_buf[j], in1=h_tok[:, chunk // 2, :], scale=1.0,
                                                    scalar=0.0, op0=ALU.mult, op1=ALU.add,
                                                    accum_out=dots[:, col:col + 1]).then_inc(u_free, n.post(u_free))
                    dve.wait_ge(u_free, n.own(u_free))
                    dve.sem_inc(a_dots, n.post(a_dots))
                    if chunk == CHUNKS - 1:
                        dve.sem_inc(u_used, n.post(u_used))
                    dve.wait_ge(gelu_ready, n.take(gelu_ready))
                    tt(wts[:, chunk * CSEL:(chunk + 1) * CSEL], gelu[:, :], gate[:, :], ALU.mult).then_inc(
                        w_ready, n.post(w_ready))
                    dve.wait_ge(w_ready, n.own(w_ready))
                    if chunk % 2 == 0 and chunk > 0:
                        add_experts(chunk // 2 - 1)
                if layer == 1:
                    final(0, LAT - 1)
                add_experts(LAT - 1)
                if layer == 1:
                    final(LAT - 1, LAT)
                meet(dve, n, [dve_step])

            peer(0)
            if layers == 2:
                def add_rows(lo, hi):
                    for b in range(lo, hi):
                        dve.wait_ge(row_ps, n.take(row_ps, 1, 2))
                        to = mod_row[:, b * 512:(b + 1) * 512]
                        tt(to, to, psum[:, b % 8, :], ALU.add).then_inc(row_ev, n.post(row_ev))
                    dve.wait_ge(row_ev, n.own(row_ev))

                dve.wait_ge(in_modb, 14 * 16)
                dve.wait_ge(in_nw, 4 * 16)
                add_rows(0, 4)
                scale_row(0)
                modulated([(x_res[:, t, :], row(1), row(0), h_tok[:, t, :]) for t in range(LAT)], 2)
                add_rows(4, MOD_BLOCKS)
                scale_row(1)
                dve.wait_ge(in_row, 16)
                link(tt(row(2), row(2), y_tmp, ALU.mult))
                for t in range(LAT):
                    dve.wait_ge(py_ps, n.take(py_ps))
                    for h in range(2):
                        o = slice(h * 512, (h + 1) * 512)
                        step(tt(scr[:, o], psum[:, 2 * t + h, :], mod_row[:, 2 * D + h * 512:2 * D + (h + 1) * 512],
                                ALU.mult))
                    dve.wait_ge(dve_step, n.own(dve_step))
                    tt(x_res[:, t, :], x_res[:, t, :], scr[:, 0:D], ALU.add).then_inc(res_ready, n.post(res_ready))
                    dve.wait_ge(res_ready, n.own(res_ready))
                meet(dve, n, [dve_step])
                peer(1)


_ORDER = ("x", "c", "ctx", "c_ctx", "c_row", "mod_w", "mod_wt", "mod_b", "norm_w", "xbc_w", "z_w", "dt_w",
          "conv_w", "conv_b", "dt_bias", "a_log", "ssd_d", "ssd_norm_w", "out_w", "pool_w", "pool_m",
          "pool_scale", "q_w", "keys",
          "u", "v", "final_norm_w")


def pool_matrices(rows=8, width=64, windows=(2, 4, 8, 16)):
    import numpy as np

    def line(count, k):
        lo = k // 2
        hi = k - 1 - lo
        m = np.zeros((count, count))
        for t in range(count):
            a, b = max(t - lo, 0), min(t + hi + 1, count)
            m[a:b, t] = 1.0 / (b - a)
        return m

    mats = [np.kron(line(rows, k), line(width, k)) - np.eye(rows * width) for k in windows]
    m = np.stack(mats).astype(np.float32)
    m = m.reshape(2, 2, LAT, P, SEQ).transpose(0, 3, 1, 2, 4)
    return np.ascontiguousarray(m.reshape(2, P, 2 * LAT * SEQ))


def kernel(x, c, ctx, c_ctx, mod_w, mod_b, norm_w, ssd_in_w, ssd_conv_w, ssd_conv_b, ssd_dt_bias,
           ssd_a_log, ssd_d, ssd_norm_w, ssd_out_w, pool_w, pool_scale, peer_q_w, peer_keys,
           peer_u, peer_v, final_norm_w):
    import numpy as _np
    import concourse.bacc as _bacc
    from concourse import mybir as _mybir
    from concourse.bass_utils import run_bass_kernel_spmd as _run

    def cols(w, blocks, width):
        k = w.shape[0] // P
        return w.reshape(k, P, blocks, width).transpose(2, 1, 0, 3).reshape(blocks, P, k * width)

    in_w = _np.asarray(ssd_in_w)[0]
    z_w, x_w, b_w, c_w, dt_w = _np.split(in_w, [INNER, 2 * INNER, 2 * INNER + D, 2 * INNER + 2 * D], axis=1)
    kd = D // P
    xbc = _np.concatenate([x_w.reshape(kd, P, GROUPS, 2 * P), b_w.reshape(kd, P, GROUPS, P),
                           c_w.reshape(kd, P, GROUPS, P)], axis=3)
    xbc = xbc.transpose(2, 1, 0, 3).reshape(GROUPS, P, kd * 4 * P)

    def channels(v):
        v = _np.asarray(v)
        xx = v[:, :INNER].reshape(-1, GROUPS, 2, P)
        bb = v[:, INNER:INNER + D].reshape(-1, GROUPS, 1, P)
        cc = v[:, INNER + D:].reshape(-1, GROUPS, 1, P)
        return _np.concatenate([xx, bb, cc], axis=2).transpose(3, 1, 2, 0).reshape(P, -1)

    mod_w = _np.asarray(mod_w)
    q_w = _np.asarray(peer_q_w)
    arrays = {
        "x": _np.asarray(x)[0], "ctx": _np.asarray(ctx)[0],
        "c": _np.asarray(c).reshape(KD, P).T, "c_ctx": _np.asarray(c_ctx).reshape(KD, P).T,
        "c_row": _np.asarray(c).reshape(-1), "mod_w": cols(mod_w[0], MOD_BLOCKS, 512),
        "mod_wt": mod_w[1].T.reshape(MOD_COLS, P, D),
        "mod_b": mod_b, "norm_w": norm_w,
        "xbc_w": xbc, "z_w": cols(z_w, GROUPS, 2 * P), "dt_w": cols(dt_w, 1, 2 * HEADS)[0],
        "conv_w": channels(_np.asarray(ssd_conv_w)[0]), "conv_b": channels(ssd_conv_b),
        "dt_bias": _np.asarray(ssd_dt_bias).reshape(-1), "a_log": _np.asarray(ssd_a_log).reshape(-1),
        "ssd_d": _np.asarray(ssd_d).reshape(CI, 2).T, "ssd_norm_w": _np.asarray(ssd_norm_w).reshape(CI, P).T,
        "out_w": _np.asarray(ssd_out_w)[0].reshape(4, 4, P, D).transpose(0, 2, 1, 3).reshape(4, P, 4 * D),
        "pool_w": _np.asarray(pool_w)[0].reshape(PGROUPS, 2, P, 2 * P).transpose(2, 0, 1, 3).reshape(P, -1),
        "pool_m": pool_matrices(), "pool_scale": _np.asarray(pool_scale)[0],
        "q_w": _np.stack([cols(q_w[i], 4, 512) for i in range(2)]),
        "keys": _np.asarray(peer_keys).reshape(2, HH, NKEY, P).transpose(0, 3, 1, 2).reshape(2, P, HH * NKEY),
        "u": _np.asarray(peer_u).reshape(2 * NEXP, D), "v": _np.asarray(peer_v).reshape(2 * NEXP, D),
        "final_norm_w": final_norm_w,
    }
    nc = _bacc.Bacc("TRN2", target_bir_lowering=False, num_devices=1)
    given, aps = {}, {}
    for name in _ORDER:
        array = _np.ascontiguousarray(arrays[name])
        given[f"in_{name}"] = array
        aps[name] = nc.dram_tensor(f"in_{name}", array.shape, _mybir.dt.from_np(array.dtype),
                                   kind="ExternalInput").ap()
    out = nc.dram_tensor("out_0", (SEQ, D), _mybir.dt.from_np(_np.dtype("float32")), kind="ExternalOutput").ap()
    hybrid(nc, aps, out)
    r = _run(nc, [given], core_ids=[0])
    return r.results[0]["out_0"].reshape(1, SEQ, D)
```
